# Optimizing a Trainium2 kernel written in Bass

```python
import math
import jax, jax.numpy as jnp
from jax import lax
import numpy as np

D_MODEL = 2048
BATCH = 1
SEQ = 512
DEPTH = 1
DEC_BATCH = 1
DEC_SEQ = 64
PAST_LEN = 128

CHUNK = 64
N_MIXERS = 4
D_MIX = D_MODEL
GROUP_W = D_MIX // N_MIXERS
SSM_HEAD_DIM = 64
SSM_HEADS = GROUP_W // SSM_HEAD_DIM
SSM_GROUPS = 2
SSM_STATE = 128
SSM_CONV = 4
SSM_CONV_DIM = GROUP_W + 2 * SSM_GROUPS * SSM_STATE
HGRN_HEAD_DIM = 128
HGRN_HEADS = GROUP_W // HGRN_HEAD_DIM
HGRN_F_FLOOR = 1e-30
FOX_HEAD_DIM = 64
FOX_HEADS = GROUP_W // FOX_HEAD_DIM
FOX_Q_BLOCK = 128
FOX_F_BIAS_INIT = 2.0
LRU_BLOCKS = 4
LRU_BLOCK_W = GROUP_W // LRU_BLOCKS
LRU_CONV = 4
LRU_C = 8.0
D_FF = -(-8 * D_MODEL // (3 * 256)) * 256
EPS = 1e-6
IN_WIDTHS = (GROUP_W, SSM_CONV_DIM, SSM_HEADS,
             GROUP_W, GROUP_W, GROUP_W, GROUP_W,
             GROUP_W, GROUP_W, GROUP_W, FOX_HEADS, GROUP_W,
             GROUP_W, GROUP_W)
D_IN = sum(IN_WIDTHS)

kernel_name = 'hybrid_ssd_hgrn2_fox_rglru_stream_step'

def _normalize(x):
    xf = x.astype(jnp.float32)
    return (xf * lax.rsqrt(jnp.mean(xf * xf, axis=-1, keepdims=True) + EPS)).astype(x.dtype)

def _rms(x, g):
    return _normalize(x) * g.astype(x.dtype)

def _split_in(h):
    parts = []
    off = 0
    for w in IN_WIDTHS:
        parts.append(h[..., off:off + w])
        off += w
    return parts

def _causal_conv(x, buf, w, bias):
    K = w.shape[0]
    T = x.shape[1]
    xp = jnp.concatenate([buf.astype(x.dtype), x], axis=1)
    y = bias.astype(x.dtype)
    for j in range(K):
        y = y + xp[:, j:j + T] * w[j]
    return y, xp[:, T:]

def _chunk_recurrence(q, k, v, log_g, s0):
    b, T, H, dk = q.shape
    dv = v.shape[-1]
    L = CHUNK if T % CHUNK == 0 else math.gcd(T, CHUNK)
    nc = T // L

    def blocks(a):
        return jnp.moveaxis(a.astype(jnp.float32).reshape(b, nc, L, *a.shape[2:]), 1, 0)

    tri = jnp.arange(L)[:, None] >= jnp.arange(L)[None, :]
    scalar = log_g.shape[-1] == 1

    def step(S, blk):
        qc, kc, vc, gc = blk
        cum = jnp.cumsum(gc, axis=1)
        diff = jnp.where(tri[None, :, :, None, None], cum[:, :, None] - cum[:, None, :], -jnp.inf)
        dec = jnp.exp(diff)
        if scalar:
            att = jnp.einsum('bthd,bshd->btsh', qc, kc) * dec[..., 0]
        else:
            att = jnp.einsum('bthd,bshd,btshd->btsh', qc, kc, dec)
        o = (jnp.einsum('btsh,bshv->bthv', att, vc)
             + jnp.einsum('bthd,bhdv->bthv', qc * jnp.exp(cum), S))
        tot = cum[:, -1]
        k_dec = kc * jnp.exp(tot[:, None] - cum)
        S = jnp.exp(tot)[..., None] * S + jnp.einsum('bshd,bshv->bhdv', k_dec, vc)
        return S, o

    S, o = lax.scan(step, s0.astype(jnp.float32), (blocks(q), blocks(k), blocks(v), blocks(log_g)))
    o = jnp.moveaxis(o, 0, 1).reshape(b, T, H, dv)
    return o.astype(v.dtype), S.astype(s0.dtype)

def _fox_attention(q, k, v, cq, ck):
    b, Tq, H, dh = q.shape
    Tk = k.shape[1]
    q_off = Tk - Tq
    QB = FOX_Q_BLOCK if Tq % FOX_Q_BLOCK == 0 else Tq
    nb = Tq // QB
    kpos = jnp.arange(Tk)
    ckh = jnp.swapaxes(ck, 1, 2)

    def one(blk):
        qb, cqb, qpos = blk
        s = jnp.einsum('bqhd,bkhd->bhqk', qb, k).astype(jnp.float32)
        s = s + jnp.swapaxes(cqb, 1, 2)[..., None] - ckh[:, :, None, :]
        s = jnp.where(kpos[None, :] <= qpos[:, None], s, -jnp.inf)
        p = jax.nn.softmax(s, axis=-1)
        return jnp.einsum('bhqk,bkhd->bqhd', p.astype(v.dtype), v)

    qs = jnp.moveaxis(q.reshape(b, nb, QB, H, dh), 1, 0)
    cqs = jnp.moveaxis(cq.reshape(b, nb, QB, H), 1, 0)
    qpos = (q_off + jnp.arange(Tq)).reshape(nb, QB)
    o = lax.map(one, (qs, cqs, qpos))
    return jnp.moveaxis(o, 0, 1).reshape(b, Tq, H, dh)

def _lin_combine(c1, c2):
    a1, b1 = c1
    a2, b2 = c2
    return a1 * a2, a2 * b1 + b2

def _rglru(xc, lam, w_r, b_r, w_i, b_i, h0, pos0):
    b, T, W = xc.shape
    xb = xc.reshape(b, T, LRU_BLOCKS, LRU_BLOCK_W)
    r = jax.nn.sigmoid(jnp.einsum('btnc,ncd->btnd', xb, w_r).reshape(b, T, W) + b_r).astype(jnp.float32)
    i = jax.nn.sigmoid(jnp.einsum('btnc,ncd->btnd', xb, w_i).reshape(b, T, W) + b_i).astype(jnp.float32)
    log_a = LRU_C * r * jax.nn.log_sigmoid(lam.astype(jnp.float32))
    reset = ((pos0 + jnp.arange(T)) == 0)[None, :, None]
    a = jnp.where(reset, 0.0, jnp.exp(log_a))
    mult = jnp.where(reset, 1.0, jnp.sqrt(-jnp.expm1(2.0 * log_a)))
    u = mult * i * xc.astype(jnp.float32)
    u = u.at[:, 0].add(a[:, 0] * h0.astype(jnp.float32))
    _, h = lax.associative_scan(_lin_combine, (a, u), axis=1)
    return h.astype(xc.dtype), h[:, -1].astype(h0.dtype)

def _layer(x, state, pr):
    (ssm_conv, ssm_s, hgrn_s, fox_k, fox_v, fox_lf, lru_conv, lru_h) = state
    f32 = jnp.float32
    b, T, _ = x.shape
    past = fox_k.shape[1]
    h = _rms(x, pr['ln1'])
    (a_z, a_xbc, a_dt, b_q, b_f, b_i, b_g,
     c_q, c_k, c_v, c_f, c_g, d_x, d_g) = _split_in(h @ pr['w_in'])

    xbc, ssm_conv_new = _causal_conv(a_xbc, ssm_conv, pr['ssm_conv_w'], pr['ssm_conv_b'])
    xbc = jax.nn.silu(xbc)
    gn = SSM_GROUPS * SSM_STATE
    a_x = xbc[..., :GROUP_W].reshape(b, T, SSM_HEADS, SSM_HEAD_DIM)
    a_B = jnp.repeat(xbc[..., GROUP_W:GROUP_W + gn].reshape(b, T, SSM_GROUPS, SSM_STATE),
                     SSM_HEADS // SSM_GROUPS, axis=2)
    a_C = jnp.repeat(xbc[..., GROUP_W + gn:].reshape(b, T, SSM_GROUPS, SSM_STATE),
                     SSM_HEADS // SSM_GROUPS, axis=2)
    dt = jax.nn.softplus(a_dt.astype(f32) + pr['ssm_dt_bias'].astype(f32))
    A = -jnp.exp(pr['ssm_a_log'].astype(f32))
    o, ssm_s_new = _chunk_recurrence(a_C, a_B, a_x * dt[..., None].astype(a_x.dtype),
                                     (dt * A)[..., None], ssm_s)
    ya = (o + pr['ssm_d'][:, None] * a_x).reshape(b, T, GROUP_W) * jax.nn.silu(a_z)
    ya = _normalize(ya.reshape(b, T, SSM_GROUPS, GROUP_W // SSM_GROUPS)).reshape(b, T, GROUP_W) * pr['ssm_norm']

    lb = pr['lb'].astype(f32)
    fr = b_f.astype(f32)
    f_gate = lb + (1.0 - lb) * jax.nn.sigmoid(fr)
    logf = jnp.log(jnp.maximum(f_gate, HGRN_F_FLOOR))
    hk = (1.0 - lb) * jax.nn.sigmoid(-fr)
    hq = jax.nn.silu(b_q)
    hs = lambda t: t.reshape(b, T, HGRN_HEADS, HGRN_HEAD_DIM)
    o, hgrn_s_new = _chunk_recurrence(hs(hq), hs(hk), hs(b_i), hs(logf), hgrn_s)
    yb = _rms(o, pr['hgrn_norm'].reshape(HGRN_HEADS, HGRN_HEAD_DIM)).reshape(b, T, GROUP_W) * jax.nn.silu(b_g)

    fs = lambda t: t.reshape(b, T, FOX_HEADS, FOX_HEAD_DIM)
    fq = _rms(fs(c_q), pr['fox_q_norm']) * (FOX_HEAD_DIM ** -0.5)
    fk = _rms(fs(c_k), pr['fox_k_norm'])
    fv = fs(c_v)
    flf = jax.nn.log_sigmoid(c_f.astype(f32) + pr['fox_f_bias'].astype(f32))
    K = jnp.concatenate([fox_k.astype(fk.dtype), fk], axis=1)
    V = jnp.concatenate([fox_v.astype(fv.dtype), fv], axis=1)
    cum = jnp.cumsum(jnp.concatenate([fox_lf.astype(f32), flf], axis=1), axis=1)
    o = _fox_attention(fq, K, V, cum[:, past:], cum)
    yc = o.reshape(b, T, GROUP_W) * jax.nn.sigmoid(c_g)

    xc, lru_conv_new = _causal_conv(d_x, lru_conv, pr['lru_conv_w'], pr['lru_conv_b'])
    hseq, lru_h_new = _rglru(xc, pr['lru_lambda'], pr['lru_w_r'], pr['lru_b_r'],
                             pr['lru_w_i'], pr['lru_b_i'], lru_h, past)
    yd = hseq * jax.nn.gelu(d_g)

    x = x + jnp.concatenate([ya, yb, yc, yd], axis=-1) @ pr['w_out']
    h2 = _rms(x, pr['ln2'])
    x = x + (jax.nn.silu(h2 @ pr['w_gate']) * (h2 @ pr['w_up'])) @ pr['w_down']
    return x, (ssm_conv_new, ssm_s_new, hgrn_s_new, fk, fv, flf, lru_conv_new, lru_h_new)

def _stack_states(states):
    return [jnp.stack(parts, axis=0) for parts in zip(*states)]

def setup_inputs(seed: int = 0) -> dict:
    key = jax.random.key(seed)
    ks = jax.random.split(key, 40)
    f32 = jnp.float32

    def nrm(k, shape, scale):
        return jax.random.normal(k, shape, f32) * scale

    def uni(k, shape, lo, hi):
        return jax.random.uniform(k, shape, f32, lo, hi)

    dt0 = jnp.exp(uni(ks[20], (DEPTH, SSM_HEADS), math.log(1e-3), math.log(1e-1)))
    a0 = uni(ks[33], (DEPTH, GROUP_W), 0.9, 0.999) ** (1.0 / LRU_C)
    return {
        'x_prompt': nrm(ks[0], (BATCH, SEQ, D_MODEL), 1.0),
        'x_sample': nrm(ks[1], (DEC_BATCH, DEC_SEQ, D_MODEL), 1.0),
        'cache_fox_k': nrm(ks[2], (DEPTH, DEC_BATCH, PAST_LEN, FOX_HEADS, FOX_HEAD_DIM), 1.0),
        'cache_fox_v': nrm(ks[3], (DEPTH, DEC_BATCH, PAST_LEN, FOX_HEADS, FOX_HEAD_DIM), 1.0),
        'cache_fox_logf': jax.nn.log_sigmoid(FOX_F_BIAS_INIT + nrm(ks[4], (DEPTH, DEC_BATCH, PAST_LEN, FOX_HEADS), 1.0)),
        'state_ssm_conv': nrm(ks[5], (DEPTH, DEC_BATCH, SSM_CONV - 1, SSM_CONV_DIM), 1.0),
        'state_ssm': nrm(ks[6], (DEPTH, DEC_BATCH, SSM_HEADS, SSM_STATE, SSM_HEAD_DIM), 0.1),
        'state_hgrn': nrm(ks[7], (DEPTH, DEC_BATCH, HGRN_HEADS, HGRN_HEAD_DIM, HGRN_HEAD_DIM), 0.1),
        'state_lru_conv': nrm(ks[8], (DEPTH, DEC_BATCH, LRU_CONV - 1, GROUP_W), 1.0),
        'state_lru': nrm(ks[9], (DEPTH, DEC_BATCH, GROUP_W), 0.3),
        'ln1': 1.0 + nrm(ks[10], (DEPTH, D_MODEL), 0.02),
        'ln2': 1.0 + nrm(ks[11], (DEPTH, D_MODEL), 0.02),
        'w_in': nrm(ks[12], (DEPTH, D_MODEL, D_IN), D_MODEL ** -0.5),
        'w_out': nrm(ks[13], (DEPTH, D_MIX, D_MODEL), D_MIX ** -0.5),
        'ssm_conv_w': nrm(ks[14], (DEPTH, SSM_CONV, SSM_CONV_DIM), SSM_CONV ** -0.5),
        'ssm_conv_b': nrm(ks[15], (DEPTH, SSM_CONV_DIM), 0.02),
        'ssm_dt_bias': dt0 + jnp.log(-jnp.expm1(-dt0)),
        'ssm_a_log': jnp.log(uni(ks[21], (DEPTH, SSM_HEADS), 1.0, 16.0)),
        'ssm_d': 1.0 + nrm(ks[22], (DEPTH, SSM_HEADS), 0.1),
        'ssm_norm': 1.0 + nrm(ks[23], (DEPTH, GROUP_W), 0.02),
        'hgrn_lb_logits': nrm(ks[24], (DEPTH, GROUP_W), 0.5),
        'hgrn_norm': 1.0 + nrm(ks[25], (DEPTH, GROUP_W), 0.02),
        'fox_q_norm': 1.0 + nrm(ks[26], (DEPTH, FOX_HEAD_DIM), 0.02),
        'fox_k_norm': 1.0 + nrm(ks[27], (DEPTH, FOX_HEAD_DIM), 0.02),
        'fox_f_bias': FOX_F_BIAS_INIT + nrm(ks[28], (DEPTH, FOX_HEADS), 0.1),
        'lru_conv_w': nrm(ks[29], (DEPTH, LRU_CONV, GROUP_W), LRU_CONV ** -0.5),
        'lru_conv_b': nrm(ks[30], (DEPTH, GROUP_W), 0.02),
        'lru_w_r': nrm(ks[31], (DEPTH, LRU_BLOCKS, LRU_BLOCK_W, LRU_BLOCK_W), LRU_BLOCK_W ** -0.5),
        'lru_b_r': nrm(ks[32], (DEPTH, GROUP_W), 0.02),
        'lru_w_i': nrm(ks[34], (DEPTH, LRU_BLOCKS, LRU_BLOCK_W, LRU_BLOCK_W), LRU_BLOCK_W ** -0.5),
        'lru_b_i': nrm(ks[35], (DEPTH, GROUP_W), 0.02),
        'lru_lambda': jnp.log(a0) - jnp.log1p(-a0),
        'w_gate': nrm(ks[36], (DEPTH, D_MODEL, D_FF), D_MODEL ** -0.5),
        'w_up': nrm(ks[37], (DEPTH, D_MODEL, D_FF), D_MODEL ** -0.5),
        'w_down': nrm(ks[38], (DEPTH, D_FF, D_MODEL), D_FF ** -0.5),
    }

def reference(x_prompt, x_sample, cache_fox_k, cache_fox_v, cache_fox_logf, state_ssm_conv, state_ssm,
              state_hgrn, state_lru_conv, state_lru, ln1, ln2, w_in, w_out, ssm_conv_w, ssm_conv_b,
              ssm_dt_bias, ssm_a_log, ssm_d, ssm_norm, hgrn_lb_logits, hgrn_norm, fox_q_norm, fox_k_norm,
              fox_f_bias, lru_conv_w, lru_conv_b, lru_w_r, lru_b_r, lru_w_i, lru_b_i, lru_lambda,
              w_gate, w_up, w_down):
    f32 = jnp.float32
    lb_p = jax.nn.softmax(hgrn_lb_logits.astype(f32), axis=0)
    lower_bounds = jnp.cumsum(lb_p, axis=0) - lb_p[0]
    layers = [dict(ln1=ln1[l], ln2=ln2[l], w_in=w_in[l], w_out=w_out[l], ssm_conv_w=ssm_conv_w[l],
                   ssm_conv_b=ssm_conv_b[l], ssm_dt_bias=ssm_dt_bias[l], ssm_a_log=ssm_a_log[l],
                   ssm_d=ssm_d[l], ssm_norm=ssm_norm[l], lb=lower_bounds[l], hgrn_norm=hgrn_norm[l],
                   fox_q_norm=fox_q_norm[l], fox_k_norm=fox_k_norm[l], fox_f_bias=fox_f_bias[l],
                   lru_conv_w=lru_conv_w[l], lru_conv_b=lru_conv_b[l], lru_w_r=lru_w_r[l], lru_b_r=lru_b_r[l],
                   lru_w_i=lru_w_i[l], lru_b_i=lru_b_i[l], lru_lambda=lru_lambda[l],
                   w_gate=w_gate[l], w_up=w_up[l], w_down=w_down[l]) for l in range(DEPTH)]
    bp = x_prompt.shape[0]
    dtp = x_prompt.dtype
    fresh = (jnp.zeros((bp, SSM_CONV - 1, SSM_CONV_DIM), dtp),
             jnp.zeros((bp, SSM_HEADS, SSM_STATE, SSM_HEAD_DIM), dtp),
             jnp.zeros((bp, HGRN_HEADS, HGRN_HEAD_DIM, HGRN_HEAD_DIM), dtp),
             jnp.zeros((bp, 0, FOX_HEADS, FOX_HEAD_DIM), dtp),
             jnp.zeros((bp, 0, FOX_HEADS, FOX_HEAD_DIM), dtp),
             jnp.zeros((bp, 0, FOX_HEADS), f32),
             jnp.zeros((bp, LRU_CONV - 1, GROUP_W), dtp),
             jnp.zeros((bp, GROUP_W), dtp))
    y_prompt = x_prompt
    y_sample = x_sample
    prompt_states = []
    sample_states = []
    for l in range(DEPTH):
        y_prompt, st_p = _layer(y_prompt, fresh, layers[l])
        prompt_states.append(st_p)
        past = (state_ssm_conv[l], state_ssm[l], state_hgrn[l], cache_fox_k[l], cache_fox_v[l],
                cache_fox_logf[l], state_lru_conv[l], state_lru[l])
        y_sample, st_s = _layer(y_sample, past, layers[l])
        sample_states.append(st_s)
    (p_ssm_conv, p_ssm, p_hgrn, p_fox_k, p_fox_v, p_fox_logf, p_lru_conv, p_lru) = _stack_states(prompt_states)
    (s_ssm_conv, s_ssm, s_hgrn, s_fox_k, s_fox_v, s_fox_logf, s_lru_conv, s_lru) = _stack_states(sample_states)
    return (y_prompt, y_sample, p_ssm_conv, p_ssm, p_hgrn, p_fox_k, p_fox_v, p_fox_logf, p_lru_conv, p_lru,
            s_ssm_conv, s_ssm, s_hgrn, s_fox_k, s_fox_v, s_fox_logf, s_lru_conv, s_lru)


_drawn_inputs = setup_inputs


def setup_inputs(seed=0):
    import zlib

    import numpy as np

    out = dict(_drawn_inputs(seed))
    spreads = {}
    factors = {'cache_fox_k': 3.028,
     'cache_fox_logf': 6.821,
     'state_hgrn': 8.0,
     'ln2': 4.448,
     'ssm_norm': 5.783,
     'hgrn_norm': 8.0,
     'fox_q_norm': 8.0,
     'fox_k_norm': 2.709,
     'lru_b_r': 8.0,
     'lru_b_i': 6.75}
    for name, (base, spread) in spreads.items():
        noise = np.random.default_rng([zlib.crc32(name.encode()), seed]).standard_normal(out[name].shape)
        drawn = base * np.exp(spread * noise) if base else spread * noise
        out[name] = __import__('jax').numpy.asarray(drawn.astype(out[name].dtype))
    for name, factor in factors.items():
        out[name] = (out[name] * factor).astype(out[name].dtype)
    return out
```

```python
from contextlib import ExitStack

import concourse.bass as bass
from concourse import mybir

ACT = mybir.ActivationFunctionType
ALU = mybir.AluOpType
AX = mybir.AxisListType
F32 = mybir.dt.float32
F32R = mybir.dt.float32r
I8 = mybir.dt.int8

P = 128
D = 2048
KT = D // P
NP_TOK, NS_TOK = 512, 64
TOK = NP_TOK + NS_TOK
HT = TOK // 2
PAST = 128
GW = 512
FF = 5632
GROUPS = FF // (4 * P)
EPS = 1e-6
CHUNKS = [(c * P, P) for c in range(4)] + [(NP_TOK, NS_TOK)]
PAD = TOK + 7
SAMPLE_AT = 3 + NP_TOK
CONV = TOK + 4
LEVELS = 7
NEG = -1e30
F_FLOOR = 1e-30
TWO60 = float(2 ** 60)
RING = 4

(W_Z, W_X, W_B, W_C, W_DT) = (0, 512, 1024, 1280, 1536)
(W_BQ, W_BF, W_BI, W_BG) = (1544, 2056, 2568, 3080)
(W_CQ, W_CK, W_CV, W_CF, W_CG) = (3592, 4104, 4616, 5128, 5136)
(W_DX, W_DG) = (5648, 6160)

R_LN1, R_LN2, R_SCW, R_SCB, R_SCS, R_SNORM, R_HNORM, R_LB, R_LCW, R_LCB = (
    0, 16, 32, 64, 72, 96, 100, 104, 108, 124)
R_LCS, R_BR, R_BI, R_LAM, R_H0, R_QN, R_KN = (128, 140, 144, 148, 152, 156, 157)
O_PSC, O_SSC, O_PLC, O_SLC, O_PLH, O_SLH, O_ALL = (0, 24, 48, 60, 72, 76, 80)

UNITS = ([("ssd", g) for g in range(2)] + [("hgrn", n) for n in range(4)]
         + [("fox", n) for n in range(4)] + [("lru", n) for n in range(4)])
PARTS = {"ssd": ["B", "C", "x0", "x1", "z0", "z1"], "hgrn": ["q", "f", "i", "g"],
         "fox": ["cq", "ck", "cv", "cg"], "lru": ["dx", "dg"]}
STAGES = {"small": 2, "ssd": 11, "hgrn": 8, "fox": 8, "lru": 3}


def column_of(kind, n, part):
    return {"B": W_B + n * P, "C": W_C + n * P, "x0": W_X + 2 * n * P, "x1": W_X + (2 * n + 1) * P,
            "z0": W_Z + 2 * n * P, "z1": W_Z + (2 * n + 1) * P,
            "q": W_BQ + n * P, "f": W_BF + n * P, "i": W_BI + n * P, "g": W_BG + n * P,
            "cq": W_CQ + n * P, "ck": W_CK + n * P, "cv": W_CV + n * P, "cg": W_CG + n * P,
            "dx": W_DX + n * P, "dg": W_DG + n * P}[part]


def plan_phase1():
    blocks = [("small", 0, None, 0)]
    for u, (kind, n) in enumerate(UNITS):
        blocks += [(kind, n, part, u) for part in PARTS[kind]]
    order = [("half", 0, 0), ("half", 0, 1)]
    pending = [("small", 0, s, 0) for s in range(STAGES["small"])]
    b = 1
    for u, (kind, n) in enumerate(UNITS):
        slots = 2 * len(PARTS[kind])
        total, done = len(pending), 0
        for i in range(slots):
            order.append(("half", b + i // 2, i % 2))
            upto = (i + 1) * total // slots
            order += [("stage",) + s for s in pending[done:upto]]
            done = upto
        pending = [(kind, n, s, u) for s in range(STAGES[kind])]
        b += len(PARTS[kind])
    return blocks, order, pending


BLOCKS, ORDER, TAIL = plan_phase1()
N1 = len(BLOCKS)
N2 = KT
N3 = 12 * GROUPS
NB = N1 + N2 + N3
HALVES = 2 * NB



Y_TILES, Y_AFTER = [], []
for _kind, _n in UNITS:
    Y_TILES += {"ssd": [2 * _n, 2 * _n + 1], "hgrn": [4 + _n], "fox": [8 + _n], "lru": [12 + _n]}[_kind]
    Y_AFTER.append(len(Y_TILES))


FOX_ITEMS = [(_hh, 4) for _hh in range(2)] + [(_hh, _tb) for _tb in range(4) for _hh in range(2)]


def hybrid_layer(nc, a, o):
    (o_yp, o_ys, o_psc, o_pss, o_phg, o_pfk, o_pfv, o_pfl, o_plc, o_plh,
     o_ssc, o_sss, o_shg, o_sfk, o_sfv, o_sfl, o_slc, o_slh) = o
    ctx = ExitStack()
    with ctx:
        def fixed(name, shape, dt=F32):
            return ctx.enter_context(nc.sbuf_tensor(name, shape, dt))

        h_hi = fixed("h_hi", [P, KT, TOK], F32R)
        h_lo = fixed("h_lo", [P, KT, TOK], F32R)
        raw = [fixed(f"raw{i}", [P, 16 * P]) for i in range(2)]
        w_hi = [fixed(f"w_hi{i}", [P, 8 * P], F32R) for i in range(RING)]
        w_lo = [fixed(f"w_lo{i}", [P, 8 * P], F32R) for i in range(RING)]
        ident = fixed("ident", [P, P])
        ones = fixed("ones", [P, P])
        pcol = fixed("pcol", [P, 192])
        const = fixed("const", [P, 4])
        eps_col, zeros3 = const[:, 0:1], const[:, 1:4]

        with ExitStack() as r0:
            xT0 = r0.enter_context(nc.sbuf_tensor("xT0", [P, KT, TOK], F32))
            xtok = r0.enter_context(nc.sbuf_tensor("xtok", [P, 5, D], F32))
            sq0 = r0.enter_context(nc.sbuf_tensor("sq0", [P, TOK], F32))
            ss0 = r0.enter_context(nc.sbuf_tensor("ss0", [P, TOK], F32))
            prow0 = r0.enter_context(nc.sbuf_tensor("prow0", [P, P], F32))
            prow1 = r0.enter_context(nc.sbuf_tensor("prow1", [64, P], F32))
        rstd0, t0 = xtok[:, 0, 0:TOK], [xtok[:, 1, 0:TOK], xtok[:, 2, 0:TOK]]

        part = {}
        with ExitStack() as r1:
            def arena(name, shape, dt=F32):
                return r1.enter_context(nc.sbuf_tensor(name, shape, dt))

            for par in range(2):
                for k in range(2, 6):
                    part[par, k] = arena(f"part{par}{k}", [P, PAD + 1])
            y_out = [arena(f"y_out{i}", [P, TOK]) for i in range(2)]
            maskneg = arena("maskneg", [P, P])
            tri = arena("tri", [P, P])
            block_ones = arena("block_ones", [P, P])
            level_mask = arena("level_mask", [P, LEVELS, 256], I8)
            small_cum = arena("small_cum", [P, TOK])
            small_col = arena("small_col", [P, 5, P])
            cum_t = arena("cum_t", [P, 704])
            cum_s = arena("cum_s", [P, 704])
            cache_k = arena("cache_k", [P, GW])
            cache_v = arena("cache_v", [P, GW])
            for par in range(2):
                for k in range(2):
                    part[par, k] = arena(f"part{par}{k}", [P, PAD + 1])
            scratch = arena("scratch", [P, 8200])
            out_col = arena("out_col", [P, O_ALL])
            past_logf = arena("past_logf", [P, 8])
            ssm_d8 = arena("ssm_d8", [P, 8])
            sel_fox = arena("sel_fox", [P, 8])
            tot8 = arena("tot8", [P, 8, 5])
            ssm_etot = arena("ssm_etot", [P, 8, 5])
            hgrn_etot = arena("hgrn_etot", [P, 5])
            cols = arena("cols", [P, 40])
            lru_w = arena("lru_w", [P, 2, P])
            oc_rows = arena("oc_rows", [O_ALL, P])
        C_BIAS, C_SGN, C_A, C_LS8, C_NLS8, C_LB, C_1MLB, C_NM, C_RS, C_RI, C_T, C_QN, C_SD = (
            0, 1, 2, 3, 7, 11, 15, 19, 21, 23, 25, 29, 30)

        def cut(at, *shape):
            n = 1
            for s in shape:
                n *= s
            ap = scratch[:, at:at + n]
            return ap if len(shape) == 1 else ap.rearrange("p (x y) -> p x y", x=shape[0])

        sm_z, sm_e, sm_s, sm_s2, sm_t, sm_rows, sm_la, sm_arg = [cut(i * CONV, CONV) for i in range(8)]
        sd_cw = [cut(i * CONV, CONV) for i in range(4)]
        sd_b = cut(0, 5, P)
        sd_v, sd_vd = cut(640, 5, 2 * P), cut(1920, 5, 2 * P)
        sd_s = cut(3200, 6, 2 * P)
        sd_tmp = cut(4736, 2 * P)
        sd_cb, sd_bc, sd_cd, sd_att = [cut(4992 + i * TOK, TOK) for i in range(4)]
        sd_y = [cut(7296, TOK), sd_cb]
        sd_sq = [sd_cd, sd_att]
        hg_lf, hg_lf2, hg_k, hg_cum, hg_qc, hg_kd, hg_att = [cut(i * TOK, TOK) for i in range(7)]
        hg_z = [cut((7 + i) * TOK, TOK) for i in range(2)]
        hg_v, hg_kt = cut(9 * TOK, 5, P), cut(9 * TOK + 640, 5, P)
        hg_s = cut(9 * TOK + 1280, 6, P)
        fx_sqq, fx_sqk, fx_q, fx_k = [cut(i * TOK, TOK) for i in range(4)]
        fx_kt, fx_v = cut(4 * TOK, 5, P), cut(4 * TOK + 640, 5, P)
        fx_kc = cut(4 * TOK + 1280, P)
        fx_ex = [cut(4 * TOK + 1408 + i * 512, 512) for i in range(2)]
        fx_pt = [cut(4 * TOK + 2432 + i * 512, 512) for i in range(2)]
        fx_ch = [cut(4 * TOK + 3456 + i * 704, 704) for i in range(2)]
        fx_os = cut(4 * TOK + 4864, NS_TOK)
        lr_x, lr_r, lr_i, lr_th, lr_a, lr_m = [cut(i * CONV, CONV) for i in range(6)]

        with ExitStack() as r2:
            def late(name, shape, dt=F32):
                return r2.enter_context(nc.sbuf_tensor(name, shape, dt))

            y32 = late("y32", [P, KT, TOK])
            xT = late("xT", [P, KT, TOK])
            ss2 = late("ss2", [P, TOK])
            sq2 = [late(f"sq2_{i}", [P, TOK]) for i in range(2)]
            rstd2 = late("rstd2", [P, TOK])
            t2 = sq2
            y_tok = [late(f"y_tok{i}", [P, 512]) for i in range(2)]
        with ExitStack() as r3:
            act_hi = r3.enter_context(nc.sbuf_tensor("act_hi", [P, 4, TOK], F32R))
            act_lo = r3.enter_context(nc.sbuf_tensor("act_lo", [P, 4, TOK], F32R))
            silu = [r3.enter_context(nc.sbuf_tensor(f"silu{i}", [P, TOK], F32)) for i in range(2)]
            glu = [r3.enter_context(nc.sbuf_tensor(f"glu{i}", [P, TOK], F32)) for i in range(2)]

        pair = [ctx.enter_context(nc.psum_tensor(f"pair{i}", [P, 1024], F32)) for i in range(4)]

        def banks(t, n=HT):
            return t[:, :].rearrange("p (b n) -> p b n", b=2)[:, :, 0:n]

        def two(ap):
            return ap.rearrange("p (b n) -> p b n", b=2)

        def raw_half(at):
            block, h = raw[(at // 2) % 2], at % 2
            if at >= 2 * (N1 + N2 + 8):
                src = block[:, :].rearrange("p (k c) -> p k c", k=4)[:, :, h * 2 * P:(h + 1) * 2 * P]
            else:
                src = block[:, h * 8 * P:(h + 1) * 8 * P].rearrange("p (k c) -> p k c", k=8)
            k = src.shape[1]
            return src, *[w[at % RING][:, :].rearrange("p (k c) -> p k c", k=k) for w in (w_hi, w_lo)]

        xT_dram = nc.dram_tensor("xT_spill", [KT, P, TOK], F32, kind="Internal").ap()
        mixed_dram = nc.dram_tensor("mixed_spill", [KT, P, TOK], F32, kind="Internal").ap()

        S = {}
        for name in """
        pe_step dve_step act_step pool_step
        ident_made consts_made raw0_loaded raw1_loaded hi_done lo_done half_used evac_done
        x_loaded0 x_loaded1 x_loaded2 x_loaded3 x_loaded4 prow_loaded prow_zeroed pcol_psum pcol_ready
        xt_psum xt_copied xt_spilled x_squared ss_ready ss_psum rstd_ready norm_t norm_hi norm_lo
        cols_set bias_loaded cache_loaded lru_w_loaded ssm_in_loaded hgrn_in_loaded
        sm_abs sm_exp sm_a sm_arg_ready sm_cum sm_rows_ready sm_past_psum sm_tr sm_col sm_tot sm_tot_psum sm_etot sm_fox sm_fox2 logf_out
        y_done y_stored
        sd_conv sd_silu sd_tr sd_btok sd_vx sd_cb_psum sd_cbm sd_kv sd_state sd_bc_psum sd_bc_copied sd_argd sd_expd sd_attd
        sd_o sd_yv sd_sqd sd_stat sd_rstd sd_out
        hg_f hg_ln hg_cumd hg_ec hg_karg hg_kexp hg_kdd hg_tr hg_tok hg_diag hg_att0 hg_zarg hg_zexp hg_zd hg_lvl hg_lvld hg_kv
        hg_state hg_o hg_sqd hg_stat hg_rstd hg_out
        fx_sqd fx_stat fx_rstd fx_qkd fx_tr fx_tok fx_bias fx_score fx_neg fx_expd fx_pd fx_t fx_ptd fx_pv fx_osd fx_kout fx_vout
        lr_conv lr_gates lr_act lr_m2 lr_sqrt oc_ready oc_psum oc_copied oc_stored
        """.split():
            S[name] = ctx.enter_context(nc.semaphore(name))
        for name in """
        y_loaded xT_loaded x2_done x2_squared x2_summed
        silu_done glu_done act_hi_done act_lo_done down_out x_added
        out_psum out_copied0 out_copied1 out_stored0 out_stored1
        """.split():
            S[name] = ctx.enter_context(nc.semaphore(name))

        block = ctx.enter_context(nc.Block())

        class Own:

            def __init__(self, eng, step_name):
                self.eng, self.step_name, self.count = eng, step_name, {}

            def tell(self, ins, name):
                self.count[name] = self.count.get(name, 0) + 1
                ins.then_inc(S[name], 1)

            def mark(self, ins, name):
                self.tell(ins, name)
                self.eng.wait_ge(S[name], self.count[name])

            def step(self, ins):
                self.mark(ins, self.step_name)

        @block.sync
        def _(sp):
            for c, (t_0, n) in enumerate(CHUNKS):
                src = a["x_prompt"][0, t_0:t_0 + n, :] if c < 4 else a["x_sample"][0]
                sp.dma_start(xtok[0:n, c, :], src).then_inc(S[f"x_loaded{c}"], 16)

            def prow(r, n):
                return prow0[r:r + n, :] if r < P else prow1[r - P:r - P + n, :]

            sp.wait_ge(S["prow_zeroed"], 1)
            for name, r, n in (("ln1", R_LN1, 16), ("ln2", R_LN2, 16), ("ssm_conv_b", R_SCB, 8),
                               ("ssm_norm", R_SNORM, 4), ("hgrn_norm", R_HNORM, 4), ("hgrn_lb_logits", R_LB, 4),
                               ("lru_conv_b", R_LCB, 4), ("lru_b_r", R_BR, 4), ("lru_b_i", R_BI, 4),
                               ("lru_lambda", R_LAM, 4)):
                sp.dma_start(prow(r, n), a[name][0].rearrange("(n p) -> n p", p=P)).then_inc(S["prow_loaded"], 16)
            sp.dma_start(prow(R_H0, 4), a["state_lru"][0, 0].rearrange("(n p) -> n p", p=P)
                         ).then_inc(S["prow_loaded"], 16)
            for name, r, j, n in (("ssm_conv_w", R_SCW, 4, 8), ("lru_conv_w", R_LCW, 4, 4)):
                sp.dma_start(prow(r, j * n), a[name][0].rearrange("j (n p) -> (j n) p", p=P)
                             ).then_inc(S["prow_loaded"], 16)
            for name, r, j, n in (("state_ssm_conv", R_SCS, 3, 8), ("state_lru_conv", R_LCS, 3, 4)):
                sp.dma_start(prow(r, j * n), a[name][0, 0].rearrange("j (n p) -> (j n) p", p=P)
                             ).then_inc(S["prow_loaded"], 16)
            for name, r in (("fox_q_norm", R_QN), ("fox_k_norm", R_KN)):
                for k in range(2):
                    sp.dma_start(prow(r, 1)[:, 64 * k:64 * k + 64], a[name]).then_inc(S["prow_loaded"], 16)

            w_in = a["w_in"][0].rearrange("(k p) c -> p k c", p=P)
            for n, (kind, unit, pt, u) in enumerate(BLOCKS):
                if n >= 2:
                    sp.wait_ge(S["lo_done"], 2 * n - 2)
                dst = raw[n % 2][:, :].rearrange("p (k c) -> p k c", c=P)
                if kind == "small":
                    sp.dma_start(dst[:, :, 0:64], w_in[:, :, W_CF:W_CF + 64]).then_inc(S["raw0_loaded"], 16)
                    sp.dma_start(dst[:, :, 64:P], w_in[:, :, W_DT:W_DT + 64]).then_inc(S["raw0_loaded"], 16)
                else:
                    c0 = column_of(kind, unit, pt)
                    sp.dma_start(dst, w_in[:, :, c0:c0 + P]).then_inc(S[f"raw{n % 2}_loaded"], 16)
                if n == 2:
                    sp.wait_ge(S["norm_lo"], KT)
                    sp.wait_ge(S["xt_spilled"], 16 * KT)
                    sp.wait_ge(S["cols_set"], 1)
                    for dst2, src in ((cols[0:8, C_BIAS:C_BIAS + 1], a["fox_f_bias"]),
                                      (cols[64:72, C_BIAS:C_BIAS + 1], a["ssm_dt_bias"]),
                                      (cols[64:72, C_A:C_A + 1], a["ssm_a_log"])):
                        sp.dma_start(dst2, src.rearrange("a h -> h a")).then_inc(S["bias_loaded"], 16)
                    sp.dma_start(ssm_d8[:, :], a["ssm_d"].to_broadcast([P, 8])).then_inc(S["bias_loaded"], 16)
                    for dst2, src in ((cache_k[:, :], a["cache_fox_k"][0, 0].rearrange("t h d -> t (h d)")),
                                      (cache_v[:, :], a["cache_fox_v"][0, 0].rearrange("t h d -> t (h d)")),
                                      (past_logf[:, :], a["cache_fox_logf"][0, 0])):
                        sp.dma_start(dst2, src).then_inc(S["cache_loaded"], 16)

            w_out = a["w_out"][0].rearrange("(k p) c -> p k c", p=P)
            for n in range(N1, N1 + 2):
                sp.wait_ge(S["lo_done"], 2 * n - 2)
                c0 = (n - N1) * P
                sp.dma_start(raw[n % 2][:, :].rearrange("p (k c) -> p k c", c=P), w_out[:, :, c0:c0 + P]
                             ).then_inc(S[f"raw{n % 2}_loaded"], 16)
            sp.wait_ge(S["y_done"], 12)
            sp.wait_ge(S["y_stored"], 16 * 12)
            for q in range(4):
                sp.dma_start(y32[:, 3 * q:3 * q + 3, :], mixed_dram[3 * q:3 * q + 3].rearrange("k p t -> p k t")
                             ).then_inc(S["y_loaded"], 16)
            sp.wait_ge(S["y_done"], 16)
            sp.wait_ge(S["oc_stored"], 96)
            for q in range(4):
                sp.dma_start(xT[:, 4 * q:4 * q + 4, :], xT_dram[4 * q:4 * q + 4].rearrange("k p t -> p k t")
                             ).then_inc(S["xT_loaded"], 16)
            with sp.Fori(0, (N2 - 2) // 2) as i:
                for j in range(2):
                    n = N1 + 2 + j
                    sp.wait_ge(S["lo_done"], i * 4 + (2 * n - 2))
                    sp.dma_start(raw[n % 2][:, :].rearrange("p (k c) -> p k c", c=P),
                                 w_out[:, :, bass.ds(i * (2 * P) + (2 + j) * P, P)]
                                 ).then_inc(S[f"raw{n % 2}_loaded"], 16)
            w_gate = a["w_gate"][0].rearrange("(k p) c -> p k c", p=P)
            w_up = a["w_up"][0].rearrange("(k p) c -> p k c", p=P)
            with sp.Fori(0, GROUPS) as g:
                for j in range(12):
                    n = N1 + N2 + j
                    sp.wait_ge(S["lo_done"], g * 24 + (2 * n - 2))
                    if j < 8:
                        w = w_gate if j % 2 == 0 else w_up
                        sp.dma_start(raw[n % 2][:, :].rearrange("p (k c) -> p k c", c=P),
                                     w[:, :, bass.ds(g * (4 * P) + (j // 2) * P, P)]
                                     ).then_inc(S[f"raw{n % 2}_loaded"], 16)
                    else:
                        c0 = (j - 8) * 4 * P
                        src = a["w_down"][0][bass.ds(g * (4 * P), 4 * P), :].rearrange("(k p) c -> p k c", p=P)
                        sp.dma_start(raw[n % 2][:, :].rearrange("p (k c) -> p k c", k=4), src[:, :, c0:c0 + 4 * P]
                                     ).then_inc(S[f"raw{n % 2}_loaded"], 16)

        @block.gpsimd
        def _(pool):
            own = Own(pool, "pool_step")
            own.step(pool.memset(ones[:, :], 1.0))
            own.step(pool.memset(const[:, :], 0.0))
            own.step(pool.memset(const[:, 0:1], EPS))
            own.mark(pool.affine_select(out=ident[:, :], in_=ones[:, :], compare_op=ALU.is_equal, fill=0.0, base=0,
                                        pattern=[[-1, P]], channel_multiplier=1), "ident_made")

            def lo_half(u):
                value, at = u if isinstance(u, tuple) else (u, u)
                pool.wait_ge(S["hi_done"], value + 1)
                src, hi, lo = raw_half(at)
                pool.tensor_tensor(lo, src, hi.bitcast(F32), ALU.subtract).then_inc(S["lo_done"], 1)

            for u in range(4):
                lo_half(u)
            pool.wait_ge(S["norm_lo"], KT)
            pool.wait_ge(S["xt_spilled"], 16 * KT)
            own.step(pool.affine_select(out=tri[:, :], in_=ones[:, :], compare_op=ALU.is_ge, fill=0.0, base=0,
                                        pattern=[[1, P]], channel_multiplier=-1))
            own.step(pool.memset(maskneg[:, :], 0.0))
            own.step(pool.affine_select(out=maskneg[:, :], in_=maskneg[:, :], compare_op=ALU.is_ge, fill=NEG, base=0,
                                        pattern=[[-1, P]], channel_multiplier=1))
            own.step(pool.memset(block_ones[:, :], 0.0))
            own.step(pool.memset(block_ones[0:64, 0:64], 1.0))
            own.step(pool.memset(block_ones[64:P, 64:P], 1.0))
            own.step(pool.memset(level_mask[:, :, :], 1))
            for lv in range(LEVELS):
                h = 1 << lv
                m = level_mask[:, lv, :].rearrange("p (c b j) -> p c b j", c=4, j=h)
                own.step(pool.affine_select(out=m, in_=m, compare_op=ALU.is_ge, fill=0.0, base=0,
                                            pattern=[[0, 4], [-2 * h, 64 // h], [0, h]], channel_multiplier=1))
                last = pool.affine_select(out=m, in_=m, compare_op=ALU.is_ge, fill=0.0, base=h - 1,
                                          pattern=[[0, 4], [2 * h, 64 // h], [0, h]], channel_multiplier=-1)
                if lv < LEVELS - 1:
                    own.step(last)
            own.mark(last, "consts_made")
            before = 2 * (N1 + N2)
            whole = (before - 4) // 4
            with pool.Fori(0, whole) as i:
                for j in range(4):
                    lo_half((i * 4 + (4 + j), 4 + j))
            for u in range(4 + whole * 4, before):
                lo_half(u)
            with pool.Fori(0, GROUPS) as g:
                for j in range(24):
                    lo_half((g * 24 + (before + j), before + j))

        @block.tensor
        def _(pe):
            def mm(out, lhsT, rhs, start=True, stop=True):
                return nc.tensor.matmul(out, lhsT, rhs, start=start, stop=stop)

            def gemm_half(value, at, h, dst, inputs_of=None):
                pe.wait_ge(S["lo_done"], value + 1)
                wh, wl = w_hi[at % RING], w_lo[at % RING]
                for k in range(8):
                    kt = 8 * h + k
                    if inputs_of is not None:
                        pe.wait_ge(S["norm_lo"], inputs_of + kt + 1)
                    first, last = (h == 0 and k == 0), (h == 1 and k == 7)
                    for q, (w, x) in enumerate(((wh, h_hi), (wh, h_lo), (wl, h_hi))):
                        for b in range(2):
                            m = mm(dst[:, b * 512:b * 512 + HT], w[:, k * P:(k + 1) * P],
                                   x[:, kt, b * HT:(b + 1) * HT], start=first and q == 0, stop=last and q == 2)
                return m

            def sum_over_partitions(dst, src, mat, start=True, stop=True):
                for b in range(2):
                    m = mm(dst[:, b * 512:b * 512 + HT], mat[:, :], src[:, b * HT:(b + 1) * HT], start, stop)
                return m

            def chunk_transposes(dst, src):
                for c, (t_0, n) in enumerate(CHUNKS):
                    m = pe.transpose(dst[0:n, c * P:(c + 1) * P], src[:, t_0:t_0 + n], ident[:, :])
                return m

            pe.wait_ge(S["ident_made"], 1)
            for k in range(KT):
                if k >= 4:
                    pe.wait_ge(S["xt_copied"], k - 3)
                for c, (t_0, n) in enumerate(CHUNKS):
                    if k == 0:
                        pe.wait_ge(S[f"x_loaded{c}"], 16)
                    m = pe.transpose(pair[k % 4][:, t_0:t_0 + n], xtok[0:n, c, k * P:(k + 1) * P], ident[0:n, 0:n])
                m.then_inc(S["xt_psum"], 1)
            pe.wait_ge(S["prow_loaded"], 16 * 19)
            pe.wait_ge(S["xt_copied"], 13)
            pe.transpose(pair[0][:, 0:P], prow0[:, :], ident[:, :])
            pe.transpose(pair[0][:, P:P + 64], prow1[:, :], ident[0:64, 0:64]).then_inc(S["pcol_psum"], 1)
            pe.wait_ge(S["ss_ready"], 1)
            pe.wait_ge(S["xt_copied"], 14)
            sum_over_partitions(pair[1], ss0, ones).then_inc(S["ss_psum"], 1)

            def small(n, s, u):
                if s == 0:
                    pe.wait_ge(S["cache_loaded"], 48)
                    pe.transpose(pair[3][0:8, 0:P], past_logf[:, :], ident[:, :]).then_inc(S["sm_past_psum"], 1)
                else:
                    pe.wait_ge(S["sm_rows_ready"], 1)
                    chunk_transposes(pair[2], sm_rows[:, 0:TOK]).then_inc(S["sm_tr"], 1)
                    pe.wait_ge(S["sm_tot"], 1)
                    mm(pair[3][:, 512:552], ones[64:72, :], tot8[64:72, :, :].rearrange("p h c -> p (h c)")
                       ).then_inc(S["sm_tot_psum"], 1)

            def ssd(g, s, u):
                if s == 1:
                    pe.wait_ge(S["sd_silu"], 4 * g + 4)
                    if u > 0:
                        pe.wait_ge(S["y_done"], Y_AFTER[u - 1])
                    else:
                        pe.wait_ge(S["sm_col"], 1)
                        pe.wait_ge(S["sm_etot"], 1)
                    chunk_transposes(pair[2], part[u % 2, 0]).then_inc(S["sd_tr"], 1)
                    chunk_transposes(pair[3], part[u % 2, 2]).then_inc(S["sd_tr"], 1)
                elif s == 2:
                    pe.wait_ge(S["sd_btok"], g + 1)
                    chunk_transposes(pair[2], part[u % 2, 3]).then_inc(S["sd_tr"], 1)
                    pe.wait_ge(S["sd_vx"], 2 * g + 1)
                    for c, (t_0, n) in enumerate(CHUNKS):
                        m = mm(pair[3][0:n, t_0:t_0 + n], part[u % 2, 0][:, t_0:t_0 + n], part[u % 2, 1][:, t_0:t_0 + n])
                    m.then_inc(S["sd_cb_psum"], 1)
                elif s == 3:
                    pe.wait_ge(S["sd_cbm"], g + 1)
                    for c, (t_0, n) in enumerate(CHUNKS):
                        dst = pair[3][:, c * 2 * P:(c + 1) * 2 * P] if c < 4 else pair[2][:, 0:2 * P]
                        m = mm(dst, sd_b[0:n, c, :], sd_vd[0:n, c, :])
                    m.then_inc(S["sd_kv"], 1)
                if 4 <= s <= 8:
                    hh = s - 5
                    if hh >= 0:
                        pe.wait_ge(S["sd_attd"], 4 * g + hh + 1)
                        if hh == 2:
                            pe.wait_ge(S["sd_yv"], 2 * g + 1)
                        pb, vc = 64 * (hh % 2), slice(64 * hh, 64 * hh + 64)
                        for c, (t_0, n) in enumerate(CHUNKS):
                            out = pair[3][pb:pb + 64, t_0:t_0 + n]
                            m = mm(out, sd_v[0:n, c, vc], sd_att[0:n, t_0:t_0 + n], True, c == 0)
                            if c > 0:
                                m = mm(out, sd_s[:, c - 1 if c < 4 else 4, vc], sd_cd[:, t_0:t_0 + n], False, True)
                        m.then_inc(S["sd_o"], 1)
                    if hh < 3:
                        if s == 4:
                            pe.wait_ge(S["sd_state"], g + 1)
                        else:
                            pe.wait_ge(S["sd_bc_copied"], 4 * g + hh + 1)
                        h = 4 * g + hh + 1
                        row = ident[64:72, 64 + h:65 + h].to_broadcast([8, P])
                        mm(pair[2][:, 0:512], row, small_cum[64:72, 0:512])
                        mm(pair[2][:, 512:TOK], row, small_cum[64:72, 512:TOK]).then_inc(S["sd_bc_psum"], 1)
                elif s == 9:
                    pe.wait_ge(S["sd_sqd"], 2 * g + 2)
                    sum_over_partitions(pair[2], sd_sq[0], ones, True, False)
                    sum_over_partitions(pair[2], sd_sq[1], ones, False, True).then_inc(S["sd_stat"], 1)

            def hgrn(n, s, u):
                if s == 1:
                    pe.wait_ge(S["y_done"], Y_AFTER[u - 1])
                    pe.wait_ge(S["evac_done"], 1 + 12 + 4 * n + 3)
                    chunk_transposes(pair[2], part[u % 2, 2]).then_inc(S["hg_tr"], 1)
                    pe.wait_ge(S["hg_kdd"], n + 1)
                    chunk_transposes(pair[3], hg_kd).then_inc(S["hg_tr"], 1)
                elif s == 2:
                    pe.wait_ge(S["hg_tok"], 2 * n + 1)
                    for c, (t_0, m_) in enumerate(CHUNKS):
                        m = mm(pair[2][0:m_, t_0:t_0 + m_], hg_k[:, t_0:t_0 + m_], part[u % 2, 0][:, t_0:t_0 + m_])
                    m.then_inc(S["hg_diag"], 1)
                    pe.wait_ge(S["hg_tok"], 2 * n + 2)
                    level(n, 0, u)
                    level(n, 1, u)
                elif s in (3, 4):
                    level(n, 2 * s - 4, u)
                    level(n, 2 * s - 3, u)
                    if s == 4:
                        pe.wait_ge(S["hg_att0"], n + 1)
                        for c, (t_0, m_) in enumerate(CHUNKS):
                            m = mm(pair[2][:, c * P:(c + 1) * P], hg_kt[0:m_, c, :], hg_v[0:m_, c, :])
                        m.then_inc(S["hg_kv"], 1)
                elif s == 5:
                    level(n, 6, u)
                elif s == 6:
                    pe.wait_ge(S["hg_state"], n + 1)
                    pe.wait_ge(S["hg_lvld"], LEVELS * (n + 1))
                    for c, (t_0, m_) in enumerate(CHUNKS):
                        out = pair[3][:, t_0:t_0 + m_]
                        m = mm(out, hg_v[0:m_, c, :], hg_att[0:m_, t_0:t_0 + m_], True, c == 0)
                        if c > 0:
                            m = mm(out, hg_s[:, c - 1 if c < 4 else 4, :], hg_qc[:, t_0:t_0 + m_], False, True)
                    m.then_inc(S["hg_o"], 1)
                elif s == 7:
                    pe.wait_ge(S["hg_sqd"], n + 1)
                    sum_over_partitions(pair[2], hg_lf, ones).then_inc(S["hg_stat"], 1)

            def level(n, lv, u):
                h = 1 << lv
                pe.wait_ge(S["hg_zd"], LEVELS * n + lv + 1)
                if lv >= 2:
                    pe.wait_ge(S["hg_lvld"], LEVELS * n + lv - 1)
                bank = pair[3][:, 512 * (lv % 2):512 * (lv % 2) + 512]
                z = hg_z[lv % 2]
                for c, (t_0, n_) in enumerate(CHUNKS if lv < 6 else CHUNKS[:4]):
                    right = z[:, t_0:t_0 + n_].rearrange("p (b s j) -> p b s j", s=2, j=h)[:, :, 1, :]
                    w = n_ // 2
                    m = mm(bank[0:n_, c * 64:c * 64 + w].rearrange("p (b j) -> p b j", j=h), z[:, t_0:t_0 + n_], right)
                m.then_inc(S["hg_lvl"], 1)

            def fox_step(n, k):
                base = 10 * n
                if k + 2 < 10:
                    i = k + 2
                    hh, tb = FOX_ITEMS[i]
                    pb = 64 * hh
                    if i >= 2:
                        pe.wait_ge(S["fx_expd"], base + i - 1)
                    bank = pair[2][:, 512 * (i % 2):512 * (i % 2) + 512]
                    if tb < 4:
                        t_0, m_, keys, k0, q0 = tb * P, P, (tb + 1) * P, 0, tb * P
                    else:
                        t_0, m_, keys, k0, q0 = NP_TOK, NS_TOK, PAST + NS_TOK, NP_TOK, NP_TOK + PAST
                    q = fx_q[pb:pb + 64, t_0:t_0 + m_]
                    mm(bank[0:m_, 0:keys], cum_t[pb:pb + 40, q0:q0 + m_], fx_ch[hh][pb:pb + 40, k0:k0 + keys], True, False)
                    if tb < 4:
                        mm(bank[0:m_, 0:keys], q, fx_k[pb:pb + 64, 0:keys], False, False)
                    else:
                        mm(bank[0:m_, 0:PAST], q, fx_kc[pb:pb + 64, :], False, False)
                        mm(bank[0:m_, PAST:keys], q, fx_k[pb:pb + 64, t_0:t_0 + m_], False, False)
                    r = slice(0, P) if m_ == P else slice(pb, pb + NS_TOK)
                    mm(bank[0:m_, keys - m_:keys], ident[r, r], maskneg[r, r], False, True
                       ).then_inc(S["fx_score"], 1)
                if 0 <= k + 1 < 10:
                    i = k + 1
                    hh, tb = FOX_ITEMS[i]
                    pe.wait_ge(S["fx_pd"], base + i + 1)
                    if i >= 1:
                        pe.wait_ge(S["fx_ptd"], base + i)
                    p = fx_ex[i % 2]
                    blocks = [(b * P, P) for b in range(tb + 1)] if tb < 4 else [(0, P), (P, NS_TOK)]
                    m_ = P if tb < 4 else NS_TOK
                    for b, (s_0, w) in enumerate(blocks):
                        m = pe.transpose(pair[3][0:w, 512 + b * m_:512 + (b + 1) * m_], p[0:m_, s_0:s_0 + w],
                                         ident[0:m_, 0:m_])
                    m.then_inc(S["fx_t"], 1)
                if 0 <= k:
                    hh, tb = FOX_ITEMS[k]
                    pb = 64 * hh
                    pe.wait_ge(S["fx_ptd"], base + k + 1)
                    pt = fx_pt[k % 2]
                    if tb < 4:
                        if k == 2:
                            pe.wait_ge(S["fx_osd"], n + 1)
                        out = pair[3][pb:pb + 64, tb * P:(tb + 1) * P]
                        for b in range(tb + 1):
                            m = mm(out, fx_v[:, b, pb:pb + 64], pt[:, b * P:(b + 1) * P], b == 0, b == tb)
                    else:
                        out = pair[3][pb:pb + 64, 0:NS_TOK]
                        mm(out, cache_v[:, P * n + pb:P * n + pb + 64], pt[:, 0:NS_TOK], True, False)
                        m = mm(out, fx_v[0:NS_TOK, 4, pb:pb + 64], pt[0:NS_TOK, NS_TOK:2 * NS_TOK], False, True)
                    m.then_inc(S["fx_pv"], 1)

            def fox(n, s, u):
                if s == 1:
                    pe.wait_ge(S["y_done"], Y_AFTER[u - 1])
                    pe.wait_ge(S["fx_sqd"], 2 * n + 2)
                    sum_over_partitions(pair[2], fx_sqq, block_ones).then_inc(S["fx_stat"], 1)
                    sum_over_partitions(pair[3], fx_sqk, block_ones).then_inc(S["fx_stat"], 1)
                elif s == 2:
                    pe.wait_ge(S["fx_qkd"], 2 * n + 2)
                    chunk_transposes(pair[2], fx_k)
                    pe.transpose(pair[2][:, 5 * P:6 * P], cache_k[:, n * P:(n + 1) * P], ident[:, :]
                                 ).then_inc(S["fx_tr"], 1)
                    chunk_transposes(pair[3], part[u % 2, 2]).then_inc(S["fx_tr"], 1)
                elif s == 3:
                    pe.wait_ge(S["fx_tok"], 3 * n + 3)
                    pe.wait_ge(S["fx_bias"], 2 * n + 2)
                    for k in (-2, -1, 0):
                        fox_step(n, k)
                elif 4 <= s <= 6:
                    for k in range(3 * s - 11, 3 * s - 8):
                        fox_step(n, k)

            def lru(n, s, u):
                if s == 1:
                    pe.wait_ge(S["lr_conv"], n + 1)
                    pe.wait_ge(S["lru_w_loaded"], 32 * (n + 1))
                    pe.wait_ge(S["y_done"], Y_AFTER[u - 1])
                    for w in range(2):
                        for b in range(2):
                            m = mm(pair[2 + w][:, 512 * b:512 * b + 290], lru_w[:, w, :], lr_x[:, 290 * b:290 * b + 290])
                        m.then_inc(S["lr_gates"], 1)

            mixers = {"small": small, "ssd": ssd, "hgrn": hgrn, "fox": fox, "lru": lru}

            for task in ORDER:
                if task[0] == "half":
                    _, n, h = task
                    if h == 0 and n >= 2:
                        pe.wait_ge(S["evac_done"], n - 1)
                    m = gemm_half(2 * n + h, 2 * n + h, h, pair[n % 2], inputs_of=0 if n == 0 else None)
                    m.then_inc(S["half_used"], 1)
                else:
                    _, kind, n, s, u = task
                    mixers[kind](n, s, u)
            for kind, n, s, u in TAIL:
                mixers[kind](n, s, u)
            pe.wait_ge(S["oc_ready"], 1)
            pe.wait_ge(S["y_done"], 16)
            pe.transpose(pair[2][0:O_ALL, 0:P], out_col[:, :], ident[:, :]).then_inc(S["oc_psum"], 1)

            def wout_block(value_block, j, wait_inputs):
                n = N1 + j
                dst = pair[j % 4]
                if j < 2 and isinstance(value_block, int):
                    pe.wait_ge(S["evac_done"], N1)
                for h in range(2):
                    m = gemm_half(value_block * 2 + (2 * N1 + h), 2 * n + h, h, dst,
                                  inputs_of=KT if wait_inputs else None)
                    m.then_inc(S["half_used"], 1)

            pe.wait_ge(S["oc_copied"], 1)
            for j in range(4):
                wout_block(j, j, j == 0)
            with pe.Fori(1, N2 // 4) as i:
                for j in range(4):
                    pe.wait_ge(S["x2_done"], i * 4 + (j - 3))
                    wout_block(i * 4 + j, j, False)
            pe.wait_ge(S["x2_summed"], N2)
            sum_over_partitions(pair[0], ss2, ones).then_inc(S["ss_psum"], 1)

            def swiglu(g, first):
                for j in range(8):
                    if not first or j >= 4:
                        if j < 4:
                            pe.wait_ge(S["x_added"], g * 16 + (j - 3))
                        elif j % 2 == 0:
                            pe.wait_ge(S["glu_done"], g * 4 + (j // 2 - 1))
                    for h in range(2):
                        at = 2 * (N1 + N2 + j) + h
                        if first and j == 0 and h == 0:
                            pe.wait_ge(S["rstd_ready"], 2)
                        m = gemm_half(g * 24 + at, at, h, pair[j % 4], inputs_of=2 * KT if first and j == 0 else None)
                        m.then_inc(S["half_used"], 1)
                for q in range(8):
                    at = 2 * (N1 + N2 + 8) + q
                    pe.wait_ge(S["lo_done"], g * 24 + (at + 1))
                    wh, wl = w_hi[at % RING], w_lo[at % RING]
                    for jj in range(2):
                        n = 2 * q + jj
                        if n == 0:
                            pe.wait_ge(S["glu_done"], g * 4 + 3)
                        elif n == 2:
                            pe.wait_ge(S["glu_done"], g * 4 + 4)
                        elif n >= 4:
                            pe.wait_ge(S["x_added"], g * 16 + (n - 3))
                        dst = pair[n % 4]
                        for k in range(4):
                            if n == 0:
                                pe.wait_ge(S["act_lo_done"], g * 4 + (k + 1))
                            for r, (w, x) in enumerate(((wh, act_hi), (wh, act_lo), (wl, act_hi))):
                                for b in range(2):
                                    c0 = k * 2 * P + jj * P
                                    m = mm(dst[:, b * 512:b * 512 + HT], w[:, c0:c0 + P],
                                           x[:, k, b * HT:(b + 1) * HT], k == 0 and r == 0, k == 3 and r == 2)
                        m.then_inc(S["half_used" if jj else "down_out"], 1)

            swiglu(0, True)
            with pe.Fori(1, GROUPS) as g:
                swiglu(g, False)

            i = 0
            for q in range(4):
                pe.wait_ge(S["x_added"], 16 * GROUPS)
                for c, (t_0, n) in enumerate(CHUNKS):
                    if i >= 8:
                        pe.wait_ge(S[f"out_copied{i % 2}"], (i - 8) // 2 + 1)
                    dst = pair[(i % 8) // 2][0:n, 512 * (i % 2):512 * (i % 2) + 512]
                    for f in range(4):
                        m = pe.transpose(dst[:, f * P:(f + 1) * P], xT[:, 4 * q + f, t_0:t_0 + n], ident[:, :])
                    m.then_inc(S["out_psum"], 1)
                    i += 1

        @block.scalar
        def _(act):
            own = Own(act, "act_step")

            def fn(out, in_, f, **kw):
                return nc.scalar.activation(out, in_, f, **kw)

            def hi_half(value, at):
                n = at // 2
                if at % 2 == 0:
                    extra = 16 if n % 2 == 0 else 0
                    act.wait_ge(S[f"raw{n % 2}_loaded"], (value - at) * 4 + (16 * (n // 2 + 1) + extra))
                if at >= RING:
                    act.wait_ge(S["half_used"], value - 3)
                src, hi, _ = raw_half(at)
                fn(hi, src, ACT.Copy).then_inc(S["hi_done"], 1)

            def squares(out, src, name):
                own.tell(fn(out, src, ACT.Square), name)

            def rstd_of(out, psum, width, name, src_name, count):
                act.wait_ge(S[src_name], count)
                own.step(fn(out, psum, ACT.Ln, scale=1.0 / width, bias=eps_col))
                own.mark(fn(out, out, ACT.Exp, scale=-0.5), name)

            for u in range(3):
                hi_half(u, u)
            for k in range(KT):
                act.wait_ge(S["xt_copied"], k + 1)
                act.dma_start(xT_dram[k], xT0[:, k, :]).then_inc(S["xt_spilled"], 16)
            act.wait_ge(S["pcol_psum"], 1)
            own.mark(fn(pcol[:, :], pair[0][:, 0:192], ACT.Copy), "pcol_ready")
            rstd_of(two(rstd0), banks(pair[1]), D, "rstd_ready", "ss_psum", 1)
            for k in range(KT):
                act.wait_ge(S["norm_t"], k + 1)
                own.tell(fn(h_hi[:, k, :], t0[k % 2], ACT.Copy), "norm_hi")

            def evacuate(n):
                kind, unit, pt, u = BLOCKS[n]
                if kind == "small":
                    return
                act.wait_ge(S["half_used"], 2 * n + 2)
                if u >= 2:
                    act.wait_ge(S["y_done"], Y_AFTER[u - 2])
                if n == 1:
                    act.wait_ge(S["evac_done"], 1)
                    act.wait_ge(S["norm_lo"], KT)
                    act.wait_ge(S["xt_spilled"], 16 * KT)
                src = pair[n % 2]
                slot = {"B": 0, "C": 1, "x0": 2, "x1": 3, "z0": 4, "z1": 5, "q": 0, "f": 1, "i": 2, "g": 3,
                        "cq": 0, "ck": 1, "cv": 2, "cg": 3, "dx": 0, "dg": 1}[pt]
                dst = part[u % 2, slot]
                if pt in ("B", "C", "x0", "x1", "dx"):
                    if pt == "dx":
                        state = pcol[:, R_LCS:R_LCS + 12].rearrange("p (j t) -> p j t", j=3)[:, :, unit]
                    else:
                        tile = {"x0": 2 * unit, "x1": 2 * unit + 1, "B": 4 + unit, "C": 6 + unit}[pt]
                        state = pcol[:, R_SCS:R_SCS + 24].rearrange("p (j t) -> p j t", j=3)[:, :, tile]
                    fn(dst[:, 0:3], zeros3, ACT.Copy)
                    fn(dst[:, PAD - 1:PAD], zeros3[:, 0:1], ACT.Copy)
                    fn(dst[:, SAMPLE_AT:SAMPLE_AT + 3], state, ACT.Copy)
                    fn(dst[:, 3:3 + HT], src[:, 0:HT], ACT.Copy)
                    fn(dst[:, 3 + HT:SAMPLE_AT], src[:, 512:512 + NP_TOK - HT], ACT.Copy)
                    ins = fn(dst[:, SAMPLE_AT + 3:SAMPLE_AT + 3 + NS_TOK], src[:, 512 + NP_TOK - HT:512 + HT], ACT.Copy)
                elif pt == "f":
                    fn(two(part[u % 2, 4][:, 0:TOK]), banks(src), ACT.Sigmoid, scale=-1.0)
                    ins = fn(two(dst[:, 0:TOK]), banks(src), ACT.Sigmoid)
                else:
                    f = {"z0": ACT.Silu, "z1": ACT.Silu, "q": ACT.Silu, "g": ACT.Silu, "cg": ACT.Sigmoid,
                         "dg": ACT.Gelu_apprx_tanh}.get(pt, ACT.Copy)
                    ins = fn(two(dst[:, 0:TOK]), banks(src), f)
                ins.then_inc(S["evac_done"], 1)

            def unit_starts(u):
                if u > 0:
                    act.wait_ge(S["y_done"], Y_AFTER[u - 1])

            def store_y(u):
                for j in range(Y_AFTER[u - 1] if u else 0, Y_AFTER[u]):
                    act.wait_ge(S["y_done"], j + 1)
                    act.dma_start(mixed_dram[Y_TILES[j]], y_out[j % 2][:, :]).then_inc(S["y_stored"], 16)

            def small(n, s, u):
                if s == 0:
                    act.wait_ge(S["sm_abs"], 1)
                    own.mark(fn(sm_e[:, 0:CONV], sm_e[:, 0:CONV], ACT.Exp, scale=-1.0), "sm_exp")
                    act.wait_ge(S["bias_loaded"], 64)
                    fn(cols[64:96, C_A:C_A + 1], cols[64:96, C_A:C_A + 1], ACT.Exp)
                    own.mark(fn(cols[:, C_LB:C_LB + 4], cols[:, C_LB:C_LB + 4], ACT.Exp), "sm_a")
                else:
                    act.wait_ge(S["sm_arg_ready"], 1)
                    fn(sm_rows[32:64, 0:TOK], small_cum[64:96, :], ACT.Copy)
                    own.mark(fn(sm_rows[96:P, 0:TOK], sm_arg[64:96, 0:TOK], ACT.Exp), "sm_rows_ready")
                    act.wait_ge(S["sm_tr"], 1)
                    fn(small_col[:, 0:4, :], pair[2][:, 0:512].rearrange("p (c n) -> p c n", c=4), ACT.Copy)
                    own.mark(fn(small_col[0:64, 4, :], pair[2][0:64, 512:640], ACT.Copy), "sm_col")
                    act.wait_ge(S["sm_tot_psum"], 1)
                    own.mark(fn(ssm_etot[:, :, :].rearrange("p h c -> p (h c)"), pair[3][:, 512:552], ACT.Exp), "sm_etot")
                    act.wait_ge(S["sm_fox"], 1)
                    fn(cum_s[32:64, :], cum_t[0:32, :], ACT.Copy)
                    fn(cum_s[96:P, :], cum_t[0:32, :], ACT.Copy)
                    own.mark(fn(cum_t[64:96, :], cum_t[0:32, :], ACT.Copy), "sm_fox2")
                    act.dma_start(o_pfl[0, 0].rearrange("(c t) h -> t c h", t=P), small_col[:, 0:4, 0:8]
                                  ).then_inc(S["logf_out"], 16)
                    act.dma_start(o_sfl[0, 0], small_col[0:64, 4, 0:8]).then_inc(S["logf_out"], 16)

            def ssd(g, s, u):
                if s == 0:
                    unit_starts(u)
                    act.dma_start(sd_s[:, 4, :].rearrange("n (h v) -> n h v", h=4),
                                  a["state_ssm"][0, 0, 4 * g:4 * g + 4].rearrange("h n v -> n h v")
                                  ).then_inc(S["ssm_in_loaded"], 16)
                elif s == 1:
                    for j in range(4):
                        act.wait_ge(S["sd_conv"], 4 * g + j + 1)
                        dst = part[u % 2, j]
                        fn(dst[:, 0:NP_TOK], sd_cw[j][:, 0:NP_TOK], ACT.Silu)
                        own.tell(fn(dst[:, NP_TOK:TOK], sd_cw[j][:, SAMPLE_AT:SAMPLE_AT + NS_TOK], ACT.Silu), "sd_silu")
                    act.wait_ge(S["sd_tr"], 3 * g + 1)
                    act.wait_ge(S["sd_silu"], 4 * g + 4)
                    fn(sd_b[:, 0:4, :], pair[2][:, 0:512].rearrange("p (c n) -> p c n", c=4), ACT.Copy)
                    own.tell(fn(sd_b[0:64, 4, :], pair[2][0:64, 512:640], ACT.Copy), "sd_btok")
                elif 4 <= s <= 7:
                    i = 4 * g + s - 4
                    act.wait_ge(S["sd_bc_psum"], i + 1)
                    if i > 4 * g:
                        act.wait_ge(S["sd_attd"], i)
                    own.mark(fn(sd_bc, pair[2][:, 0:TOK], ACT.Copy), "sd_bc_copied")
                    fn(sd_cd, sd_bc, ACT.Exp)
                    act.wait_ge(S["sd_argd"], i + 1)
                    own.mark(fn(sd_att, sd_att, ACT.Exp), "sd_expd")
                    if s == 4:
                        act.wait_ge(S["sd_state"], g + 1)
                        for slot, dst in ((3, o_pss), (5, o_sss)):
                            act.dma_start(dst[0, 0, 4 * g:4 * g + 4].rearrange("h n v -> n h v"),
                                          sd_s[:, slot, :].rearrange("n (h v) -> n h v", h=4)).then_inc(S["sd_out"], 16)
                elif s == 9:
                    for t in range(2):
                        act.wait_ge(S["sd_yv"], 2 * g + 2)
                        squares(sd_sq[t], sd_y[t], "sd_sqd")
                elif s == 10:
                    act.wait_ge(S["sd_sqd"], 2 * g + 2)
                    rstd_of(two(sd_bc), banks(pair[2]), 2 * P, "sd_rstd", "sd_stat", g + 1)

            def tokens_out(dst, psum):
                fn(dst[:, 0:4, :], psum[:, 0:512].rearrange("p (c n) -> p c n", c=4), ACT.Copy)
                return fn(dst[0:64, 4, :], psum[0:64, 512:640], ACT.Copy)

            def zexp(n, lv):
                act.wait_ge(S["hg_zarg"], LEVELS * n + lv + 1)
                w = TOK if lv < 6 else NP_TOK
                own.tell(fn(hg_z[lv % 2][:, 0:w], hg_z[lv % 2][:, 0:w], ACT.Exp), "hg_zexp")

            def hgrn(n, s, u):
                if s == 0:
                    unit_starts(u)
                    store_y(u - 1)
                    act.dma_start(hg_s[:, 4, :], a["state_hgrn"][0, 0, n]).then_inc(S["hgrn_in_loaded"], 16)
                    act.wait_ge(S["hg_f"], n + 1)
                    fn(hg_lf, hg_lf, ACT.Ln)
                    own.tell(fn(hg_lf2, hg_lf2, ACT.Ln), "hg_ln")
                    act.wait_ge(S["hg_cumd"], n + 1)
                    own.tell(fn(hg_qc, hg_cum, ACT.Exp), "hg_ec")
                    fn(hgrn_etot[:, 0:4], hg_cum[:, 0:NP_TOK].rearrange("p (c t) -> p c t", c=4)[:, :, P - 1], ACT.Exp)
                    fn(hgrn_etot[:, 4:5], hg_cum[:, TOK - 1:TOK], ACT.Exp)
                    act.wait_ge(S["hg_karg"], n + 1)
                    own.tell(fn(hg_kd, hg_kd, ACT.Exp), "hg_kexp")
                elif s == 1:
                    act.wait_ge(S["hg_tr"], 2 * n + 1)
                    own.tell(tokens_out(hg_v, pair[2]), "hg_tok")
                    zexp(n, 0)
                    zexp(n, 1)
                    act.wait_ge(S["hg_tr"], 2 * n + 2)
                    own.tell(tokens_out(hg_kt, pair[3]), "hg_tok")
                elif s == 2:
                    zexp(n, 2)
                    zexp(n, 3)
                elif s == 3:
                    zexp(n, 4)
                    zexp(n, 5)
                elif s == 4:
                    zexp(n, 6)
                elif s == 5:
                    act.wait_ge(S["hg_state"], n + 1)
                    for slot, dst in ((3, o_phg), (5, o_shg)):
                        act.dma_start(dst[0, 0, n], hg_s[:, slot, :]).then_inc(S["hg_out"], 16)
                elif s == 6:
                    act.wait_ge(S["hg_o"], n + 1)
                    squares(hg_lf, pair[3][:, 0:TOK], "hg_sqd")
                elif s == 7:
                    act.wait_ge(S["hg_sqd"], n + 1)
                    rstd_of(two(hg_lf2), banks(pair[2]), P, "hg_rstd", "hg_stat", n + 1)

            def fox_act(n, i):
                hh, tb = FOX_ITEMS[i]
                m_, keys = (P, (tb + 1) * P) if tb < 4 else (NS_TOK, PAST + NS_TOK)
                act.wait_ge(S["fx_neg"], 10 * n + i + 1)
                bank = pair[2][:, 512 * (i % 2):512 * (i % 2) + 512]
                own.tell(fn(fx_ex[i % 2][0:m_, 0:keys], bank[0:m_, 0:keys], ACT.Exp,
                            bias=cols[0:m_, C_NM + i % 2:C_NM + i % 2 + 1],
                            accum_out=cols[0:m_, C_RS + i % 2:C_RS + i % 2 + 1]), "fx_expd")

            def fox_act_pt(n, i):
                hh, tb = FOX_ITEMS[i]
                act.wait_ge(S["fx_t"], 10 * n + i + 1)
                if tb < 4:
                    ins = fn(fx_pt[i % 2][:, 0:(tb + 1) * P], pair[3][:, 512:512 + (tb + 1) * P], ACT.Copy)
                else:
                    fn(fx_pt[i % 2][:, 0:NS_TOK], pair[3][:, 512:512 + NS_TOK], ACT.Copy)
                    ins = fn(fx_pt[i % 2][0:NS_TOK, NS_TOK:2 * NS_TOK],
                             pair[3][0:NS_TOK, 512 + NS_TOK:512 + 2 * NS_TOK], ACT.Copy)
                own.tell(ins, "fx_ptd")

            def fox(n, s, u):
                if s == 0:
                    unit_starts(u)
                    store_y(u - 1)
                    if n > 0:
                        act.wait_ge(S["fx_kout"], 32 * n)
                        act.wait_ge(S["fx_vout"], 32 * n)
                    act.wait_ge(S["evac_done"], 1 + 12 + 16 + 4 * n + 4)
                    squares(fx_sqq, part[u % 2, 0][:, 0:TOK], "fx_sqd")
                    squares(fx_sqk, part[u % 2, 1][:, 0:TOK], "fx_sqd")
                elif s == 1:
                    rstd_of(two(fx_sqq), banks(pair[2]), 64, "fx_rstd", "fx_stat", 2 * n + 1)
                    rstd_of(two(fx_sqk), banks(pair[3]), 64, "fx_rstd", "fx_stat", 2 * n + 2)
                elif s == 2:
                    act.wait_ge(S["fx_tr"], 2 * n + 1)
                    own.mark(tokens_out(fx_kt, pair[2]), "fx_tok")
                    own.tell(fn(fx_kc, pair[2][:, 640:768], ACT.Copy), "fx_tok")
                    act.wait_ge(S["fx_tr"], 2 * n + 2)
                    own.mark(tokens_out(fx_v, pair[3]), "fx_tok")
                    for src, dp, ds, name in ((fx_kt, o_pfk, o_sfk, "fx_kout"), (fx_v, o_pfv, o_sfv, "fx_vout")):
                        act.dma_start(dp[0, 0].rearrange("(c t) h d -> t c (h d)", t=P)[:, :, n * P:(n + 1) * P],
                                      src[:, 0:4, :]).then_inc(S[name], 16)
                        act.dma_start(ds[0, 0].rearrange("t h d -> t (h d)")[:, n * P:(n + 1) * P],
                                      src[0:64, 4, :]).then_inc(S[name], 16)
                elif 3 <= s <= 6:
                    for k in ((-2, -1, 0), (1, 2, 3), (4, 5, 6), (7, 8, 9))[s - 3]:
                        if k + 2 < 10:
                            fox_act(n, k + 2)
                        if 0 <= k + 1 < 10:
                            fox_act_pt(n, k + 1)

            def lru(n, s, u):
                if s == 0:
                    unit_starts(u)
                    if n == 0:
                        store_y(u - 1)
                    for w, name in enumerate(("lru_w_r", "lru_w_i")):
                        act.dma_start(lru_w[:, w, :], a[name][0, n]).then_inc(S["lru_w_loaded"], 16)
                elif s == 1:
                    act.wait_ge(S["lr_gates"], 2 * n + 2)
                    lb = ((lr_r, pair[2], R_BR), (lr_i, pair[3], R_BI))
                    for dst, src, r in lb:
                        ins = fn(dst.rearrange("p (b n) -> p b n", b=2), banks(src, 290), ACT.Sigmoid,
                                 bias=pcol[:, r + n:r + n + 1])
                    own.step(ins)
                    fn(lr_th, lr_r, ACT.Tanh, scale=cols[:, C_NLS8 + n:C_NLS8 + n + 1])
                    own.tell(fn(lr_a, lr_r, ACT.Exp, scale=cols[:, C_LS8 + n:C_LS8 + n + 1]), "lr_act")
                elif s == 2:
                    act.wait_ge(S["lr_m2"], n + 1)
                    own.tell(fn(lr_m, lr_m, ACT.Sqrt), "lr_sqrt")

            mixers = {"small": small, "ssd": ssd, "hgrn": hgrn, "fox": fox, "lru": lru}
            for task in ORDER:
                if task[0] == "half":
                    _, n, h = task
                    hi_half(2 * n + h + 3, 2 * n + h + 3)
                    if h == 1:
                        evacuate(n)
                else:
                    _, kind, n, s, u = task
                    if (kind, s) == ("ssd", 0) and u > 0:
                        store_y(u - 1)
                    mixers[kind](n, s, u)

            def split_y(ks):
                for k in ks:
                    if k < 12:
                        act.wait_ge(S["y_loaded"], 64)
                    else:
                        act.wait_ge(S["y_done"], k + 1)
                    if k == 0:
                        act.wait_ge(S["half_used"], 2 * N1)
                    own.tell(fn(h_hi[:, k, :], y32[:, k, :], ACT.Copy), "norm_hi")

            assert [t[2] for t in TAIL] == [0, 1, 2]
            for kind, n, s, u in TAIL:
                if s == 2:
                    split_y(range(12))
                mixers[kind](n, s, u)
            split_y(range(12, KT))
            act.wait_ge(S["oc_psum"], 1)
            own.mark(fn(oc_rows[:, :], pair[2][0:O_ALL, 0:P], ACT.Copy), "oc_copied")
            for r, dst, j, t in ((O_PSC, o_psc, 3, 8), (O_SSC, o_ssc, 3, 8), (O_PLC, o_plc, 3, 4), (O_SLC, o_slc, 3, 4)):
                act.dma_start(dst[0, 0].rearrange("j (t p) -> (j t) p", p=P), oc_rows[r:r + j * t, :]
                              ).then_inc(S["oc_stored"], 16)
            for r, dst in ((O_PLH, o_plh), (O_SLH, o_slh)):
                act.dma_start(dst[0, 0].rearrange("(t p) -> t p", p=P), oc_rows[r:r + 4, :]).then_inc(S["oc_stored"], 16)

            def wout_squares(value, j):
                act.wait_ge(S["x2_done"], value + 1)
                if j >= 2 or not isinstance(value, int):
                    act.wait_ge(S["x2_summed"], value - 1)
                src = xT[:, bass.ds(value, 1), :].rearrange("p a t -> p (a t)")
                own.tell(fn(sq2[j % 2][:, :], src, ACT.Square), "x2_squared")

            for j in range(4):
                for h in range(2):
                    at = 2 * (N1 + j) + h + 3
                    hi_half(at, at)
                wout_squares(j, j)
            with act.Fori(1, N2 // 4) as i:
                for j in range(4):
                    for h in range(2):
                        at = 2 * (N1 + j) + h + 3
                        hi_half(i * 8 + at, at)
                    wout_squares(i * 4 + j, j)
            rstd_of(two(rstd2[:, :]), banks(pair[0]), D, "rstd_ready", "ss_psum", 2)
            for k in range(KT):
                act.wait_ge(S["norm_t"], KT + k + 1)
                own.tell(fn(h_hi[:, k, :], t2[k % 2][:, :], ACT.Copy), "norm_hi")

            def swiglu(g, first, last):
                for j in range(12):
                    for h in range(2):
                        at = 2 * (N1 + N2 + j) + h + 3
                        if at < 2 * (N1 + N2 + 12):
                            hi_half(g * 24 + at, at)
                        elif not last:
                            hi_half(g * 24 + at, at - 24)
                    if j < 8:
                        t = j // 2
                        if j % 2 == 0:
                            act.wait_ge(S["half_used"], g * 24 + 2 * (N1 + N2 + j + 1))
                            if not first or t >= 2:
                                act.wait_ge(S["glu_done"], g * 4 + (t - 1))
                            own.tell(fn(two(silu[t % 2][:, :]), banks(pair[j % 4]), ACT.Silu), "silu_done")
                        else:
                            act.wait_ge(S["glu_done"], g * 4 + (t + 1))
                            own.tell(fn(act_hi[:, t, :], glu[t % 2][:, :], ACT.Copy), "act_hi_done")

            swiglu(0, True, False)
            with act.Fori(1, GROUPS - 1) as g:
                swiglu(g, False, False)
            swiglu(GROUPS - 1, False, True)

            i = 0
            for q in range(4):
                for c, (t_0, n) in enumerate(CHUNKS):
                    if i % 2 == 1:
                        act.wait_ge(S["out_psum"], i + 1)
                        if i >= 3:
                            act.wait_ge(S["out_stored1"], 16 * ((i - 1) // 2))
                        bank = pair[(i % 8) // 2][0:n, 512:1024]
                        own.mark(fn(y_tok[1][0:n, :], bank, ACT.Copy), "out_copied1")
                    else:
                        act.wait_ge(S["out_copied0"], i // 2 + 1)
                    dst = o_yp[0, t_0:t_0 + n, :] if c < 4 else o_ys[0]
                    act.dma_start(dst[:, 512 * q:512 * q + 512], y_tok[i % 2][0:n, :]).then_inc(S[f"out_stored{i % 2}"], 16)
                    i += 1
            act.wait_ge(S["out_stored0"], 160)
            act.wait_ge(S["out_stored1"], 160)
            act.wait_ge(S["logf_out"], 32)
            act.wait_ge(S["oc_stored"], 96)
            act.wait_ge(S["sd_out"], 64)
            act.wait_ge(S["hg_out"], 128)
            act.wait_ge(S["fx_kout"], 128)
            act.wait_ge(S["fx_vout"], 128)

        @block.vector
        def _(dve):
            own = Own(dve, "dve_step")
            V = nc.vector

            def tt(out, x, y, op):
                return V.tensor_tensor(out, x, y, op)

            def ts(out, x, s1, s2=None, op0=ALU.mult, op1=None):
                if s2 is None:
                    return V.tensor_scalar(out, x, s1, None, op0)
                return V.tensor_scalar(out, x, s1, s2, op0, op1)

            def stt(out, x, s, y, op0, op1):
                return V.scalar_tensor_tensor(out=out, in0=x, scalar=s, in1=y, op0=op0, op1=op1)

            own.mark(V.memset(prow1[:, :], 0.0), "prow_zeroed")
            own.step(V.memset(ss0[:, :], 0.0))
            for k in range(KT):
                dve.wait_ge(S["xt_psum"], k + 1)
                own.mark(V.tensor_copy(xT0[:, k, :], pair[k % 4][:, 0:TOK]), "xt_copied")
                own.step(tt(sq0[:, :], xT0[:, k, :], xT0[:, k, :], ALU.mult))
                if k < KT - 1:
                    own.step(tt(ss0[:, :], ss0[:, :], sq0[:, :], ALU.add))
                else:
                    own.mark(tt(ss0[:, :], ss0[:, :], sq0[:, :], ALU.add), "ss_ready")

            def normalise(base, x, gain, rstd, t):
                def lo(k):
                    dve.wait_ge(S["norm_hi"], base + k + 1)
                    own.tell(tt(h_lo[:, k, :], t[k % 2], h_hi[:, k, :].bitcast(F32), ALU.subtract), "norm_lo")
                for k in range(KT):
                    if k >= 2:
                        dve.wait_ge(S["norm_lo"], base + k - 1)
                    own.tell(stt(t[k % 2], x[:, k, :], pcol[:, gain + k:gain + k + 1], rstd, ALU.mult, ALU.mult), "norm_t")
                    if k >= 1:
                        lo(k - 1)
                lo(KT - 1)

            dve.wait_ge(S["pcol_ready"], 1)
            dve.wait_ge(S["rstd_ready"], 1)
            normalise(0, xT0, R_LN1, rstd0, t0)

            dve.wait_ge(S["norm_lo"], KT)
            dve.wait_ge(S["xt_spilled"], 16 * KT)
            own.step(V.memset(cols[:, :], 0.0))
            own.step(V.memset(cols[0:64, C_SGN:C_SGN + 1], -1.0))
            own.step(V.memset(cols[64:P, C_SGN:C_SGN + 1], 1.0))
            own.step(ts(cols[:, C_QN:C_QN + 1], pcol[:, R_QN:R_QN + 1], 64 ** -0.5))
            own.step(V.memset(cum_t[0:32, :], 0.0))
            own.step(V.memset(cum_t[32:64, :], -1.0))
            own.step(V.memset(cum_t[96:P, :], -1.0))
            own.step(V.memset(cum_s[:, :], 1.0))
            for r in (0, 64):
                own.step(tt(sel_fox[r:r + 64, :], ident[r:r + 64, r:r + 8], ident[r:r + 64, r + 32:r + 40], ALU.add))
            lg = pcol[:, R_LB:R_LB + 4]
            own.mark(tt(cols[:, C_LB:C_LB + 4], lg, lg, ALU.subtract), "cols_set")

            def conv(dst, x, w_base, stride, b_col):
                own.step(ts(dst, x[:, 3:3 + CONV], pcol[:, w_base + 3 * stride:w_base + 3 * stride + 1], b_col,
                            ALU.mult, ALU.add))
                for j in (2, 1, 0):
                    ins = stt(dst, x[:, j:j + CONV], pcol[:, w_base + j * stride:w_base + j * stride + 1], dst,
                              ALU.mult, ALU.add)
                    if j:
                        own.step(ins)
                return ins

            def keep_rows(x, prompt_at, sample_at, n_tiles, tile):
                for at, src in ((prompt_at, x[:, NP_TOK:NP_TOK + 3]), (sample_at, x[:, PAD - 4:PAD - 1])):
                    dst = out_col[:, at:at + 3 * n_tiles].rearrange("p (j t) -> p j t", j=3)[:, :, tile]
                    V.tensor_copy(dst, src)

            def small(n, s, u):
                if s == 0:
                    dve.wait_ge(S["half_used"], 2)
                    dve.wait_ge(S["bias_loaded"], 64)
                    own.tell(ts(two(sm_z[:, 0:TOK]), banks(pair[0]), cols[:, C_BIAS:C_BIAS + 1],
                                cols[:, C_SGN:C_SGN + 1], ALU.add, ALU.mult), "evac_done")
                    own.step(ts(sm_z[:, TOK:CONV], pcol[:, R_LAM:R_LAM + 4], -1.0))
                    for k in range(2):
                        own.step(V.tensor_copy(cols[64 * k:64 * k + 64, C_SD:C_SD + 4],
                                               ssm_d8[64 * k:64 * k + 64, :].rearrange("p (r k) -> p k r", k=2)[:, k, :]))
                    own.mark(stt(sm_e, sm_z, -1.0, sm_z, ALU.mult, ALU.max), "sm_abs")
                    dve.wait_ge(S["sm_past_psum"], 1)
                    own.step(V.tensor_copy(sm_la[0:8, 0:P], pair[3][0:8, 0:P]))
                    dve.wait_ge(S["sm_exp"], 1)
                    own.step(ts(sm_t, sm_e, 2.0, None, ALU.add))
                    own.step(V.reciprocal(sm_t, sm_t))
                    own.step(tt(sm_s, sm_e, sm_t, ALU.mult))
                    own.step(tt(sm_s2, sm_s, sm_s, ALU.mult))
                    own.step(ts(sm_t, sm_s2, 1.0 / 17))
                    for c in (15, 13, 11, 9, 7, 5, 3):
                        own.step(stt(sm_t, sm_t, 1.0 / c, sm_s2, ALU.add, ALU.mult))
                    own.step(stt(sm_t, sm_t, 1.0, sm_s, ALU.add, ALU.mult))
                    own.step(ts(sm_z, sm_z, 0.0, None, ALU.max))
                    own.step(stt(sm_z, sm_t, 2.0, sm_z, ALU.mult, ALU.add))
                    own.step(ts(cols[:, C_LS8:C_LS8 + 4], sm_z[:, TOK:CONV], -8.0))
                    own.step(ts(cols[:, C_NLS8:C_NLS8 + 4], sm_z[:, TOK:CONV], 8.0))
                    own.step(ts(sm_rows[0:32, 0:TOK], sm_z[0:32, 0:TOK], -1.0))
                    own.step(V.tensor_copy(sm_rows[64:96, 0:TOK], sm_z[64:96, 0:TOK]))
                    dve.wait_ge(S["sm_a"], 1)
                    own.step(V.reciprocal(cols[:, C_T:C_T + 4], cols[:, C_LB:C_LB + 4]))
                    own.step(tt(cols[:, C_T:C_T + 4], cols[:, C_T:C_T + 4], cols[:, C_LB:C_LB + 4], ALU.mult))
                    own.step(tt(cols[:, C_LB:C_LB + 4], cols[:, C_T:C_T + 4], cols[:, C_T:C_T + 4], ALU.subtract))
                    own.step(ts(cols[:, C_1MLB:C_1MLB + 4], cols[:, C_LB:C_LB + 4], -1.0, 1.0, ALU.mult, ALU.add))
                    own.step(ts(sm_arg[64:96, 0:TOK], sm_z[64:96, 0:TOK], cols[64:96, C_A:C_A + 1], -1.0,
                                ALU.mult, ALU.mult))
                    for t_0, m in CHUNKS:
                        own.step(V.tensor_tensor_scan(small_cum[64:96, t_0:t_0 + m], ones[64:96, 0:m],
                                                      sm_arg[64:96, t_0:t_0 + m], 0.0, ALU.mult, ALU.add))
                    for (t_0, m), c in zip(CHUNKS, range(5)):
                        own.step(tt(sm_arg[64:96, t_0:t_0 + m],
                                    small_cum[64:96, t_0 + m - 1:t_0 + m].to_broadcast([32, m]),
                                    small_cum[64:96, t_0:t_0 + m], ALU.subtract))
                        last = tt(tot8[64:72, :, c], ident[64:72, 64:72],
                                  small_cum[64:72, t_0 + m - 1:t_0 + m].to_broadcast([8, 8]), ALU.mult)
                        if c < 4:
                            own.step(last)
                    own.mark(last, "sm_tot")
                    own.mark(V.memset(cols[:, C_T:C_T + 1], 0.0), "sm_arg_ready")
                    own.step(V.tensor_tensor_scan(cum_t[0:8, 0:NP_TOK], cum_s[0:8, 0:NP_TOK], sm_rows[0:8, 0:NP_TOK],
                                                  0.0, ALU.mult, ALU.add))
                    own.step(V.tensor_tensor_scan(cum_t[0:8, 512:640], cum_s[0:8, 512:640], sm_la[0:8, 0:P],
                                                  0.0, ALU.mult, ALU.add))
                    own.mark(V.tensor_tensor_scan(cum_t[0:8, 640:704], cum_s[0:8, 640:704], sm_rows[0:8, NP_TOK:TOK],
                                                  cum_t[0:8, 639:640], ALU.mult, ALU.add), "sm_fox")

            def ssd(g, s, u):
                if s == 0:
                    if u == 0:
                        dve.wait_ge(S["sm_fox2"], 1)
                        dve.wait_ge(S["sm_col"], 1)
                    else:
                        dve.wait_ge(S["sd_out"], 32 * g)
                    dve.wait_ge(S["evac_done"], 1 + 6 * g + 4)
                    for j, tile in enumerate((4 + g, 6 + g, 2 * g, 2 * g + 1)):
                        x = part[u % 2, j]
                        keep_rows(x, O_PSC, O_SSC, 8, tile)
                        own.tell(conv(sd_cw[j], x, R_SCW + tile, 8, pcol[:, R_SCB + tile:R_SCB + tile + 1]), "sd_conv")
                elif s in (1, 2):
                    t = s - 1
                    dve.wait_ge(S["sd_tr"], 3 * g + 2 + t)
                    src = pair[3 - t]
                    c0 = 64 + 4 * g + 2 * t
                    V.tensor_tensor(sd_v[:, 0:4, t * P:(t + 1) * P].rearrange("p c (h d) -> p c h d", h=2),
                                    src[:, 0:512].rearrange("p (c h d) -> p c h d", c=4, h=2),
                                    small_col[:, 0:4, c0:c0 + 2].unsqueeze(3).to_broadcast([P, 4, 2, 64]), ALU.mult)
                    own.mark(tt(sd_v[0:64, 4, t * P:(t + 1) * P].rearrange("p (h d) -> p h d", h=2),
                                src[0:64, 512:640].rearrange("p (h d) -> p h d", h=2),
                                small_col[0:64, 4, c0:c0 + 2].unsqueeze(2).to_broadcast([64, 2, 64]), ALU.mult), "sd_vx")
                    if s == 2:
                        c1 = 96 + 4 * g
                        tt(sd_vd[:, 0:4, :].rearrange("p c (h d) -> p c h d", h=4),
                           sd_v[:, 0:4, :].rearrange("p c (h d) -> p c h d", h=4),
                           small_col[:, 0:4, c1:c1 + 4].unsqueeze(3).to_broadcast([P, 4, 4, 64]), ALU.mult)
                        tt(sd_vd[0:64, 4, :].rearrange("p (h d) -> p h d", h=4),
                           sd_v[0:64, 4, :].rearrange("p (h d) -> p h d", h=4),
                           small_col[0:64, 4, c1:c1 + 4].unsqueeze(2).to_broadcast([64, 4, 64]), ALU.mult)
                        dve.wait_ge(S["sd_cb_psum"], g + 1)
                        dve.wait_ge(S["consts_made"], 1)
                        tt(sd_cb[:, 0:512].rearrange("p (c t) -> p c t", c=4),
                           pair[3][:, 0:512].rearrange("p (c t) -> p c t", c=4),
                           tri[:, :].unsqueeze(1).to_broadcast([P, 4, P]), ALU.mult)
                        own.mark(tt(sd_cb[0:64, 512:TOK], pair[3][0:64, 512:TOK], tri[0:64, 0:64], ALU.mult), "sd_cbm")
                elif s == 3:
                    dve.wait_ge(S["sd_kv"], g + 1)
                    dve.wait_ge(S["ssm_in_loaded"], 16 * (g + 1))
                    own.step(V.tensor_copy(sd_s[:, 0, :], pair[3][:, 0:2 * P]))
                    for c in range(1, 5):
                        before, after = (c - 1, c) if c < 4 else (4, 5)
                        kv = pair[3][:, c * 2 * P:(c + 1) * 2 * P] if c < 4 else pair[2][:, 0:2 * P]
                        own.step(tt(sd_tmp.rearrange("p (h v) -> p h v", h=4),
                                    sd_s[:, before, :].rearrange("p (h v) -> p h v", h=4),
                                    ssm_etot[:, 4 * g:4 * g + 4, c].unsqueeze(2).to_broadcast([P, 4, 64]), ALU.mult))
                        last = tt(sd_s[:, after, :], sd_tmp, kv, ALU.add)
                        if c < 4:
                            own.step(last)
                    own.mark(last, "sd_state")
                if 4 <= s <= 7:
                    i = 4 * g + s - 4
                    h = i
                    dve.wait_ge(S["sd_bc_copied"], i + 1)
                    for c, (t_0, m) in enumerate(CHUNKS):
                        last = ts(sd_att[0:m, t_0:t_0 + m], sd_bc[0:m, t_0:t_0 + m],
                                  small_col[0:m, c, 32 + h:33 + h], 0.0, ALU.subtract, ALU.min)
                        if c == 3:
                            V.memset(sd_att[64:P, 512:TOK], 0.0)
                    own.mark(last, "sd_argd")
                    dve.wait_ge(S["sd_expd"], i + 1)
                    tt(sd_att[:, 0:512], sd_att[:, 0:512], sd_cb[:, 0:512], ALU.mult)
                    tt(sd_att[0:64, 512:TOK], sd_att[0:64, 512:TOK], sd_cb[0:64, 512:TOK], ALU.mult)
                    own.mark(tt(sd_cd, sd_cd, part[u % 2, 1][:, 0:TOK], ALU.mult), "sd_attd")
                if s in (6, 8):
                    t = (s - 6) // 2
                    dve.wait_ge(S["sd_o"], 4 * g + 2 * t + 2)
                    own.step(stt(sd_y[t], part[u % 2, 2 + t][:, 0:TOK], cols[:, C_SD + 2 * g + t:C_SD + 2 * g + t + 1],
                                 pair[3][:, 0:TOK], ALU.mult, ALU.add))
                    own.mark(tt(sd_y[t], sd_y[t], part[u % 2, 4 + t][:, 0:TOK], ALU.mult), "sd_yv")
                elif s == 10:
                    dve.wait_ge(S["sd_rstd"], g + 1)
                    for t in range(2):
                        j = 2 * g + t
                        if j >= 2:
                            dve.wait_ge(S["y_stored"], 16 * (j - 1))
                        own.mark(stt(y_out[j % 2][:, :], sd_y[t], pcol[:, R_SNORM + j:R_SNORM + j + 1], sd_bc,
                                     ALU.mult, ALU.mult), "y_done")

            def z_make(n, lv, u):
                h = 1 << lv
                w = TOK if lv < 6 else NP_TOK
                view = lambda x: x[:, 0:w].rearrange("p (b s j) -> p b s j", s=2, j=h)
                cum, z = view(hg_cum), view(hg_z[lv % 2])
                ref = cum[:, :, 0, h - 1:h].to_broadcast([P, w // (2 * h), h])
                tt(z[:, :, 0, :], ref, cum[:, :, 0, :], ALU.subtract)
                own.tell(tt(z[:, :, 1, :], cum[:, :, 1, :], ref, ALU.subtract), "hg_zarg")

            def z_scale(n, lv, u):
                h = 1 << lv
                w = TOK if lv < 6 else NP_TOK
                view = lambda x: x[:, 0:w].rearrange("p (b s j) -> p b s j", s=2, j=h)
                z = view(hg_z[lv % 2])
                dve.wait_ge(S["hg_zexp"], LEVELS * n + lv + 1)
                tt(z[:, :, 0, :], z[:, :, 0, :], view(hg_k)[:, :, 0, :], ALU.mult)
                own.tell(tt(z[:, :, 1, :], z[:, :, 1, :], view(part[u % 2, 0])[:, :, 1, :], ALU.mult), "hg_zd")

            def z_take(n, lv):
                h = 1 << lv
                dve.wait_ge(S["hg_lvl"], LEVELS * n + lv + 1)
                bank = pair[3][:, 512 * (lv % 2):512 * (lv % 2) + 512]
                for rows, t_0, t_1, c0, c1 in ((P, 0, 512, 0, 256), (64, 512, TOK, 256, 288)):
                    if rows == 64 and lv == 6:
                        continue
                    dst = hg_att[0:rows, t_0:t_1].rearrange("p (b s j) -> p b s j", s=2, j=h)[:, :, 1, :]
                    mask = level_mask[0:rows, lv, 0:c1 - c0].rearrange("p (b j) -> p b j", j=h)
                    last = V.copy_predicated(dst, mask, bank[0:rows, c0:c1].rearrange("p (b j) -> p b j", j=h))
                own.mark(last, "hg_lvld")

            def hgrn(n, s, u):
                if s == 0:
                    dve.wait_ge(S["evac_done"], 1 + 12 + 4 * n + 4)
                    if n > 0:
                        dve.wait_ge(S["hg_out"], 32 * n)
                    else:
                        dve.wait_ge(S["sd_out"], 64)
                    sig, neg = part[u % 2, 1][:, 0:TOK], part[u % 2, 4][:, 0:TOK]
                    lb, om = cols[:, C_LB + n:C_LB + n + 1], cols[:, C_1MLB + n:C_1MLB + n + 1]
                    own.step(ts(hg_lf, sig, om, lb, ALU.mult, ALU.add))
                    own.step(ts(hg_lf2, hg_lf, F_FLOOR, TWO60, ALU.max, ALU.mult))
                    own.step(ts(hg_lf2, hg_lf2, 1.0, None, ALU.min))
                    own.step(ts(hg_k, neg, om))
                    own.mark(ts(hg_lf, hg_lf, 1.0 / TWO60, None, ALU.max), "hg_f")
                    dve.wait_ge(S["hg_ln"], n + 1)
                    own.step(tt(hg_lf, hg_lf, hg_lf2, ALU.add))
                    for t_0, m in CHUNKS:
                        last = V.tensor_tensor_scan(hg_cum[:, t_0:t_0 + m], ones[:, 0:m], hg_lf[:, t_0:t_0 + m],
                                                    0.0, ALU.mult, ALU.add)
                    own.mark(last, "hg_cumd")
                    tt(hg_kd[:, 0:512].rearrange("p (c t) -> p c t", c=4),
                       hg_cum[:, 0:512].rearrange("p (c t) -> p c t", c=4)[:, :, P - 1:P].to_broadcast([P, 4, P]),
                       hg_cum[:, 0:512].rearrange("p (c t) -> p c t", c=4), ALU.subtract)
                    own.mark(tt(hg_kd[:, 512:TOK], hg_cum[:, TOK - 1:TOK].to_broadcast([P, NS_TOK]),
                                hg_cum[:, 512:TOK], ALU.subtract), "hg_karg")
                    dve.wait_ge(S["hg_ec"], n + 1)
                    tt(hg_qc, hg_qc, part[u % 2, 0][:, 0:TOK], ALU.mult)
                    dve.wait_ge(S["hg_kexp"], n + 1)
                    own.mark(tt(hg_kd, hg_kd, hg_k, ALU.mult), "hg_kdd")
                elif s == 1:
                    z_make(n, 0, u)
                    z_make(n, 1, u)
                    z_scale(n, 0, u)
                    z_scale(n, 1, u)
                elif s == 2:
                    dve.wait_ge(S["hg_diag"], n + 1)
                    tt(hg_att[:, 0:512].rearrange("p (c t) -> p c t", c=4),
                       pair[2][:, 0:512].rearrange("p (c t) -> p c t", c=4),
                       ident[:, :].unsqueeze(1).to_broadcast([P, 4, P]), ALU.mult)
                    own.mark(tt(hg_att[0:64, 512:TOK], pair[2][0:64, 512:TOK], ident[0:64, 0:64], ALU.mult), "hg_att0")
                if s in (2, 3, 4):
                    lv = 2 * s - 4
                    z_take(n, lv)
                    z_take(n, lv + 1)
                    z_make(n, lv + 2, u)
                    if s < 4:
                        z_make(n, lv + 3, u)
                    z_scale(n, lv + 2, u)
                    if s < 4:
                        z_scale(n, lv + 3, u)
                if s == 4:
                    dve.wait_ge(S["hg_kv"], n + 1)
                    dve.wait_ge(S["hgrn_in_loaded"], 16 * (n + 1))
                    own.step(V.tensor_copy(hg_s[:, 0, :], pair[2][:, 0:P]))
                    for c in range(1, 5):
                        before, after = (c - 1, c) if c < 4 else (4, 5)
                        last = stt(hg_s[:, after, :], hg_s[:, before, :], hgrn_etot[:, c:c + 1],
                                   pair[2][:, c * P:(c + 1) * P], ALU.mult, ALU.add)
                        if c < 4:
                            own.step(last)
                    own.mark(last, "hg_state")
                elif s == 5:
                    z_take(n, 6)
                elif s == 7:
                    dve.wait_ge(S["hg_rstd"], n + 1)
                    own.step(tt(hg_lf, pair[3][:, 0:TOK], hg_lf2, ALU.mult))
                    j = 4 + n
                    dve.wait_ge(S["y_stored"], 16 * (j - 1))
                    own.mark(stt(y_out[j % 2][:, :], hg_lf, pcol[:, R_HNORM + n:R_HNORM + n + 1],
                                 part[u % 2, 3][:, 0:TOK], ALU.mult, ALU.mult), "y_done")

            def fox_dve(n, i):
                hh, tb = FOX_ITEMS[i]
                m_, keys = (P, (tb + 1) * P) if tb < 4 else (NS_TOK, PAST + NS_TOK)
                dve.wait_ge(S["fx_score"], 10 * n + i + 1)
                bank = pair[2][:, 512 * (i % 2):512 * (i % 2) + 512]
                own.tell(V.tensor_reduce(cols[0:m_, C_NM + i % 2:C_NM + i % 2 + 1], bank[0:m_, 0:keys], AX.X, ALU.max,
                                         negate=True), "fx_neg")

            def fox_norm(n, i):
                hh, tb = FOX_ITEMS[i]
                m_, keys = (P, (tb + 1) * P) if tb < 4 else (NS_TOK, PAST + NS_TOK)
                dve.wait_ge(S["fx_expd"], 10 * n + i + 1)
                own.step(V.reciprocal(cols[0:m_, C_RI + i % 2:C_RI + i % 2 + 1], cols[0:m_, C_RS + i % 2:C_RS + i % 2 + 1]))
                own.tell(ts(fx_ex[i % 2][0:m_, 0:keys], fx_ex[i % 2][0:m_, 0:keys],
                            cols[0:m_, C_RI + i % 2:C_RI + i % 2 + 1]), "fx_pd")

            def fox(n, s, u):
                if s == 1:
                    if n == 0:
                        dve.wait_ge(S["hg_out"], 128)
                    for w, (dst, gain, r) in enumerate(((fx_q, cols[:, C_QN:C_QN + 1], fx_sqq),
                                                        (fx_k, pcol[:, R_KN:R_KN + 1], fx_sqk))):
                        dve.wait_ge(S["fx_rstd"], 2 * n + w + 1)
                        own.tell(stt(dst, part[u % 2, w][:, 0:TOK], gain, r, ALU.mult, ALU.mult), "fx_qkd")
                elif s == 2:
                    for hh in range(2):
                        dve.wait_ge(S["sm_fox2"], 1)
                        h, r = 2 * n + hh, 64 * hh
                        own.tell(ts(fx_ch[hh][r:r + 40, :], cum_s[r:r + 40, :], sel_fox[r:r + 40, h:h + 1]), "fx_bias")
                elif 3 <= s <= 6:
                    for k in ((-2, -1, 0), (1, 2, 3), (4, 5, 6), (7, 8, 9))[s - 3]:
                        if k + 2 < 10:
                            fox_dve(n, k + 2)
                            fox_norm(n, k + 2)
                        if k == 1:
                            dve.wait_ge(S["fx_pv"], 10 * n + 2)
                            own.tell(V.tensor_copy(fx_os, pair[3][:, 0:NS_TOK]), "fx_osd")
                elif s == 7:
                    dve.wait_ge(S["fx_pv"], 10 * n + 10)
                    j = 8 + n
                    dve.wait_ge(S["y_stored"], 16 * (j - 1))
                    dve.wait_ge(S["fx_osd"], n + 1)
                    tt(y_out[j % 2][:, 0:512], pair[3][:, 0:512], part[u % 2, 3][:, 0:512], ALU.mult)
                    own.mark(tt(y_out[j % 2][:, 512:TOK], fx_os, part[u % 2, 3][:, 512:TOK], ALU.mult), "y_done")

            def lru(n, s, u):
                if s == 0:
                    if n == 0:
                        dve.wait_ge(S["fx_kout"], 128)
                        dve.wait_ge(S["fx_vout"], 128)
                    dve.wait_ge(S["evac_done"], 1 + 12 + 32 + 2 * n + 2)
                    x = part[u % 2, 0]
                    keep_rows(x, O_PLC, O_SLC, 4, n)
                    own.mark(conv(lr_x, x, R_LCW + n, 4, pcol[:, R_LCB + n:R_LCB + n + 1]), "lr_conv")
                elif s == 1:
                    dve.wait_ge(S["lr_act"], n + 1)
                    own.step(tt(lr_m, lr_a, lr_a, ALU.mult))
                    own.mark(stt(lr_m, lr_m, 1.0, lr_th, ALU.add, ALU.mult), "lr_m2")
                elif s == 2:
                    own.step(tt(lr_i, lr_i, lr_x, ALU.mult))
                    dve.wait_ge(S["lr_sqrt"], n + 1)
                    own.step(V.memset(lr_m[:, 0:1], 1.0))
                    own.step(tt(lr_m, lr_m, lr_i, ALU.mult))
                    V.tensor_tensor_scan(lr_r[:, 0:NP_TOK], lr_a[:, 0:NP_TOK], lr_m[:, 0:NP_TOK], 0.0, ALU.mult, ALU.add)
                    own.step(V.tensor_tensor_scan(lr_r[:, SAMPLE_AT:SAMPLE_AT + NS_TOK],
                                                  lr_a[:, SAMPLE_AT:SAMPLE_AT + NS_TOK],
                                                  lr_m[:, SAMPLE_AT:SAMPLE_AT + NS_TOK],
                                                  pcol[:, R_H0 + n:R_H0 + n + 1], ALU.mult, ALU.add))
                    V.tensor_copy(out_col[:, O_PLH + n:O_PLH + n + 1], lr_r[:, NP_TOK - 1:NP_TOK])
                    last = V.tensor_copy(out_col[:, O_SLH + n:O_SLH + n + 1],
                                         lr_r[:, SAMPLE_AT + NS_TOK - 1:SAMPLE_AT + NS_TOK])
                    if n == 3:
                        own.mark(last, "oc_ready")
                    if n == 0:
                        dve.wait_ge(S["y_stored"], 16 * 12)
                    g = part[u % 2, 1]
                    tt(y32[:, 12 + n, 0:NP_TOK], lr_r[:, 0:NP_TOK], g[:, 0:NP_TOK], ALU.mult)
                    own.mark(tt(y32[:, 12 + n, NP_TOK:TOK], lr_r[:, SAMPLE_AT:SAMPLE_AT + NS_TOK], g[:, NP_TOK:TOK],
                                ALU.mult), "y_done")

            mixers = {"small": small, "ssd": ssd, "hgrn": hgrn, "fox": fox, "lru": lru}
            for task in ORDER:
                if task[0] == "stage":
                    _, kind, n, s, u = task
                    mixers[kind](n, s, u)

            def split_y(ks):
                for k in ks:
                    dve.wait_ge(S["norm_hi"], KT + k + 1)
                    own.tell(tt(h_lo[:, k, :], y32[:, k, :], h_hi[:, k, :].bitcast(F32), ALU.subtract), "norm_lo")

            for kind, n, s, u in TAIL:
                if s == 2:
                    split_y(range(12))
                mixers[kind](n, s, u)
            split_y(range(12, KT))
            dve.wait_ge(S["xT_loaded"], 64)
            own.step(V.memset(ss2[:, :], 0.0))

            def add_residual(value, j):
                x = xT[:, bass.ds(value, 1), :].rearrange("p a (b n) -> p (a b) n", b=2)
                dve.wait_ge(S["half_used"], value * 2 + (2 * N1 + 2))
                tt(x, x, banks(pair[j % 4]), ALU.add).then_inc(S["x2_done"], 1)
                dve.wait_ge(S["x2_squared"], value + 1)
                if j > 0 or not isinstance(value, int):
                    dve.wait_ge(S["x2_summed"], value + 0)
                tt(ss2[:, :], ss2[:, :], sq2[j % 2][:, :], ALU.add).then_inc(S["x2_summed"], 1)

            for j in range(4):
                add_residual(j, j)
            with dve.Fori(1, N2 // 4) as i:
                for j in range(4):
                    add_residual(i * 4 + j, j)
            dve.wait_ge(S["rstd_ready"], 2)
            dve.wait_ge(S["x2_summed"], N2)
            normalise(2 * KT, xT, R_LN2, rstd2[:, :], [t[:, :] for t in t2])

            def swiglu(g, first):
                for t in range(4):
                    v = g * 4 + t
                    dve.wait_ge(S["silu_done"], v + 1)
                    dve.wait_ge(S["half_used"], g * 24 + 2 * (N1 + N2 + 2 * t + 2))
                    if not first or t >= 2:
                        dve.wait_ge(S["act_lo_done"], v - 1)
                    tt(two(glu[t % 2][:, :]), two(silu[t % 2][:, :]), banks(pair[(2 * t + 1) % 4]), ALU.mult
                       ).then_inc(S["glu_done"], 1)
                    dve.wait_ge(S["act_hi_done"], v + 1)
                    tt(act_lo[:, t, :], glu[t % 2][:, :], act_hi[:, t, :].bitcast(F32), ALU.subtract
                       ).then_inc(S["act_lo_done"], 1)
                for n in range(KT):
                    if n % 2 == 0:
                        dve.wait_ge(S["down_out"], g * 8 + (n // 2 + 1))
                    else:
                        dve.wait_ge(S["half_used"], g * 24 + (2 * (N1 + N2 + 8) + n // 2 + 1))
                    if not first:
                        dve.wait_ge(S["x_added"], g * 16 + (n - 15))
                    tt(two(xT[:, n, :]), two(xT[:, n, :]), banks(pair[n % 4]), ALU.add).then_inc(S["x_added"], 1)

            swiglu(0, True)
            with dve.Fori(1, GROUPS) as g:
                swiglu(g, False)

            i = 0
            for q in range(4):
                for c, (t_0, n) in enumerate(CHUNKS):
                    if i % 2 == 0:
                        dve.wait_ge(S["out_psum"], i + 1)
                        if i >= 2:
                            dve.wait_ge(S["out_stored0"], 16 * (i // 2))
                        own.tell(V.tensor_copy(y_tok[0][0:n, :], pair[(i % 8) // 2][0:n, 0:512]), "out_copied0")
                    i += 1


_PROMPT = [(1, 1, 3, 1024), (1, 1, 8, 128, 64), (1, 1, 4, 128, 128), (1, 1, 512, 8, 64), (1, 1, 512, 8, 64),
           (1, 1, 512, 8), (1, 1, 3, 512), (1, 1, 512)]
_SAMPLE = [(1, 1, 3, 1024), (1, 1, 8, 128, 64), (1, 1, 4, 128, 128), (1, 1, 64, 8, 64), (1, 1, 64, 8, 64),
           (1, 1, 64, 8), (1, 1, 3, 512), (1, 1, 512)]
OUTPUTS = [(1, 512, 2048), (1, 64, 2048)] + _PROMPT + _SAMPLE


def kernel(**inputs):
    import concourse.bacc as bacc
    import numpy as np
    from concourse.bass_utils import run_bass_kernel_spmd

    nc = bacc.Bacc("TRN2", target_bir_lowering=False, num_devices=1)
    arrays, a = {}, {}
    for name, value in inputs.items():
        value = np.ascontiguousarray(value)
        arrays[f"in_{name}_dram"] = value
        a[name] = nc.dram_tensor(f"in_{name}_dram", value.shape, mybir.dt.from_np(value.dtype), kind="ExternalInput").ap()
    o = [nc.dram_tensor(f"out_{i}_dram", shape, F32, kind="ExternalOutput").ap() for i, shape in enumerate(OUTPUTS)]
    hybrid_layer(nc, a, o)
    r = run_bass_kernel_spmd(nc, [arrays], core_ids=[0])
    return tuple(r.results[0][f"out_{i}_dram"] for i in range(len(OUTPUTS)))
```

```python
from contextlib import ExitStack

import concourse.bass as bass
from concourse import mybir

ACT = mybir.ActivationFunctionType
ALU = mybir.AluOpType
AX = mybir.AxisListType
F32 = mybir.dt.float32
F32R = mybir.dt.float32r
I8 = mybir.dt.int8

P = 128
D = 2048
KT = D // P
NP_TOK, NS_TOK = 512, 64
TOK = NP_TOK + NS_TOK
HT = TOK // 2
PAST = 128
GW = 512
FF = 5632
GROUPS = FF // (4 * P)
EPS = 1e-6
CHUNKS = [(c * P, P) for c in range(4)] + [(NP_TOK, NS_TOK)]
PAD = TOK + 7
SAMPLE_AT = 3 + NP_TOK
CONV = TOK + 4
LEVELS = 7
NEG = -1e30
F_FLOOR = 1e-30
TWO60 = float(2 ** 60)
RING = 4

(W_Z, W_X, W_B, W_C, W_DT) = (0, 512, 1024, 1280, 1536)
(W_BQ, W_BF, W_BI, W_BG) = (1544, 2056, 2568, 3080)
(W_CQ, W_CK, W_CV, W_CF, W_CG) = (3592, 4104, 4616, 5128, 5136)
(W_DX, W_DG) = (5648, 6160)

R_LN1, R_LN2, R_SCW, R_SCB, R_SCS, R_SNORM, R_HNORM, R_LB, R_LCW, R_LCB = (
    0, 16, 32, 64, 72, 96, 100, 104, 108, 124)
R_LCS, R_BR, R_BI, R_LAM, R_H0, R_QN, R_KN = (128, 140, 144, 148, 152, 156, 157)
O_PSC, O_SSC, O_PLC, O_SLC, O_PLH, O_SLH, O_ALL = (0, 24, 48, 60, 72, 76, 80)

UNITS = ([("ssd", g) for g in range(2)] + [("hgrn", n) for n in range(4)]
         + [("fox", n) for n in range(4)] + [("lru", n) for n in range(4)])
PARTS = {"ssd": ["B", "C", "x0", "x1", "z0", "z1"], "hgrn": ["q", "f", "i", "g"],
         "fox": ["cq", "ck", "cv", "cg"], "lru": ["dx", "dg"]}
STAGES = {"small": 2, "ssd": 11, "hgrn": 8, "fox": 8, "lru": 4}


def column_of(kind, n, part):
    return {"B": W_B + n * P, "C": W_C + n * P, "x0": W_X + 2 * n * P, "x1": W_X + (2 * n + 1) * P,
            "z0": W_Z + 2 * n * P, "z1": W_Z + (2 * n + 1) * P,
            "q": W_BQ + n * P, "f": W_BF + n * P, "i": W_BI + n * P, "g": W_BG + n * P,
            "cq": W_CQ + n * P, "ck": W_CK + n * P, "cv": W_CV + n * P, "cg": W_CG + n * P,
            "dx": W_DX + n * P, "dg": W_DG + n * P}[part]


def plan_phase1():
    blocks = [("small", 0, None, 0)]
    for u, (kind, n) in enumerate(UNITS):
        if kind != "lru":
            blocks += [(kind, n, part, u) for part in PARTS[kind]]
    order = [("half", 0, 0), ("half", 0, 1)]

    def spread(stages, slots, b):
        done = 0
        for i in range(slots):
            order.append(("half", b + i // 2, i % 2))
            upto = (i + 1) * len(stages) // slots
            order.extend(("stage",) + s for s in stages[done:upto] if s)
            done = upto

    b, pending = 1, []
    for u, (kind, n) in enumerate(UNITS):
        if kind == "lru":
            continue
        stages = [(kind, n, s, u) for s in range(STAGES[kind])]
        if kind == "ssd":
            if n == 0:
                for slot in range(8):
                    order.append(("half", b + slot // 2, slot % 2))
                    order.extend(("stage", "small", 0, s, 0) for s in range(2) if slot == (0, 4)[s])
            else:
                spread(pending, 8, b)
            order.append(("stage",) + stages[0])
            spread([None, None] + stages[1:3], 4, b + 4)
            pending = stages[3:]
        else:
            spread(pending, 8, b)
            pending = stages
        b += len(PARTS[kind])
    spread(pending, 4, b)
    first = UNITS.index(("lru", 0))
    lru = [("dx", 0, None), ("dg", 0, None), ("dx", 1, ([(0, 0)], [(0, 1)])), ("dg", 1, ([(0, 2), (0, 3)], [(1, 0)])),
           ("dx", 2, ([(1, 1)], [(1, 2), (1, 3)])), ("dx", 3, ([(2, 0)], [(2, 1), (3, 0)])),
           ("dg", 2, ([(2, 2)], [(3, 1), (2, 3)])), ("dg", 3, ([(3, 2)], []))]
    for part, n, after in lru:
        blocks.append(("lru", n, part, first + n))
        if after:
            for h in range(2):
                order.append(("half", b, h))
                order.extend(("stage", "lru", m, s, first + m) for m, s in after[h])
        b += 1
    return blocks, order, [("lru", 3, 3, first + 3)]


BLOCKS, ORDER, TAIL = plan_phase1()
N1 = len(BLOCKS)
N2 = KT
N3 = 12 * GROUPS
NB = N1 + N2 + N3
HALVES = 2 * NB
EVACUATED = {blk[:3]: n + 1 for n, blk in enumerate(BLOCKS)}



Y_TILES, Y_AFTER = [], []
for _kind, _n in UNITS:
    Y_TILES += {"ssd": [2 * _n, 2 * _n + 1], "hgrn": [4 + _n], "fox": [8 + _n], "lru": [12 + _n]}[_kind]
    Y_AFTER.append(len(Y_TILES))


OUT_STEPS = [(_i, _q, _c, min(4 * _q + 5 + 4 * _c // 5, KT - 1))
             for _i, (_q, _c) in enumerate((_q, _c) for _q in range(4) for _c in range(5))]
FOX_ITEMS = [(_hh, 4) for _hh in range(2)] + [(_hh, _tb) for _tb in range(4) for _hh in range(2)]

FOX_STEPS = {3: (-2,), 4: (-1, 0, 1), 5: (2, 3, 4), 6: (5, 6, 7), 7: (8, 9)}


def hybrid_layer(nc, a, o):
    (o_yp, o_ys, o_psc, o_pss, o_phg, o_pfk, o_pfv, o_pfl, o_plc, o_plh,
     o_ssc, o_sss, o_shg, o_sfk, o_sfv, o_sfl, o_slc, o_slh) = o
    ctx = ExitStack()
    with ctx:
        def fixed(name, shape, dt=F32):
            return ctx.enter_context(nc.sbuf_tensor(name, shape, dt))

        h_hi = fixed("h_hi", [P, KT, TOK], F32R)
        h_lo = fixed("h_lo", [P, KT, TOK], F32R)
        raw = [fixed(f"raw{i}", [P, 16 * P]) for i in range(2)]
        w_hi = [fixed(f"w_hi{i}", [P, 8 * P], F32R) for i in range(RING)]
        w_lo = [fixed(f"w_lo{i}", [P, 8 * P], F32R) for i in range(RING)]
        ident = fixed("ident", [P, P])
        ones = fixed("ones", [P, P])
        pcol = fixed("pcol", [P, 192])
        const = fixed("const", [P, 4])
        eps_col, zeros3 = const[:, 0:1], const[:, 1:4]

        with ExitStack() as r0:
            xT0 = r0.enter_context(nc.sbuf_tensor("xT0", [P, KT, TOK], F32))
            xtok = r0.enter_context(nc.sbuf_tensor("xtok", [P, 5, D], F32))
            sq0 = r0.enter_context(nc.sbuf_tensor("sq0", [P, D], F32))
            ss_tok = r0.enter_context(nc.sbuf_tensor("ss_tok", [P, 8], F32))
            prow0 = r0.enter_context(nc.sbuf_tensor("prow0", [P, P], F32))
            prow1 = r0.enter_context(nc.sbuf_tensor("prow1", [64, P], F32))
        over_xtok = xtok[:, :, :].rearrange("p c d -> p (c d)")
        t0 = [over_xtok[:, k * TOK:(k + 1) * TOK] for k in range(KT)]
        rstd0 = over_xtok[:, KT * TOK:(KT + 1) * TOK]

        part = {}
        with ExitStack() as r1:
            def arena(name, shape, dt=F32):
                return r1.enter_context(nc.sbuf_tensor(name, shape, dt))

            for par in range(2):
                for k in range(2, 6):
                    part[par, k] = arena(f"part{par}{k}", [P, PAD + 1])
            y_out = [arena(f"y_out{i}", [P, TOK]) for i in range(2)]
            maskneg = arena("maskneg", [P, P], F32R)
            tri = arena("tri", [P, P])
            block_ones = arena("block_ones", [P, P])
            level_mask = arena("level_mask", [P, LEVELS, 256], I8)
            small_cum = arena("small_cum", [P, TOK])
            small_col = arena("small_col", [P, 5, P])
            cum_t = arena("cum_t", [P, 704], F32R)
            cum_s = arena("cum_s", [P, 704], F32R)
            cache_k = arena("cache_k", [P, GW])
            cache_v = arena("cache_v", [P, GW])
            for par in range(2):
                for k in range(2):
                    part[par, k] = arena(f"part{par}{k}", [P, PAD + 1])
            out_col = arena("out_col", [P, O_ALL])
            past_logf = arena("past_logf", [P, 8])
            ssm_d8 = arena("ssm_d8", [P, 8])
            ident_r = arena("ident_r", [P, P], F32R)
            sel_fox = arena("sel_fox", [P, 8])
            tot8 = arena("tot8", [P, 8, 5])
            ssm_etot = arena("ssm_etot", [P, 8, 5])
            hgrn_etot = arena("hgrn_etot", [P, 5])
            cols = arena("cols", [P, 40])
            lru_w = arena("lru_w", [P, 2, P])
            oc_rows = arena("oc_rows", [O_ALL, P])
            with nc.sbuf_tensor("scratch", [P, 7872], F32) as scratch:
                pass
            with nc.sbuf_tensor("fox_scratch", [P, 5824], F32), nc.sbuf_tensor("fx_ch", [P, 2, 704], F32R) as fx_chs:
                fx_ch = [fx_chs[:, i, :] for i in range(2)]
        C_BIAS, C_SGN, C_A, C_LS8, C_NLS8, C_LB, C_1MLB, C_NM, C_RS, C_RI, C_T, C_QN, C_SD = (
            0, 1, 2, 3, 7, 11, 15, 19, 21, 23, 25, 29, 30)

        def cut(at, *shape):
            n = 1
            for s in shape:
                n *= s
            ap = scratch[:, at:at + n]
            return ap if len(shape) == 1 else ap.rearrange("p (x y) -> p x y", x=shape[0])

        sm_z, sm_e, sm_s, sm_s2, sm_t, sm_rows, sm_la, sm_arg = [cut(i * CONV, CONV) for i in range(8)]
        sm_cf = cut(8 * CONV, 704)
        sd_cw = [cut(i * CONV, CONV) for i in range(4)]
        sd_b = cut(0, 5, P)
        sd_v, sd_vd = cut(640, 5, 2 * P), cut(1920, 5, 2 * P)
        sd_s = cut(3200, 6, 2 * P)
        sd_tmp = cut(4736, 2 * P)
        sd_cb, sd_bc, sd_cd, sd_att = [cut(4992 + i * TOK, TOK) for i in range(4)]
        sd_y = [cut(7296, TOK), sd_cb]
        sd_sq = [sd_cd, sd_att]
        hg_lf, hg_lf2, hg_k, hg_cum, hg_qc, hg_kd, hg_att = [cut(i * TOK, TOK) for i in range(7)]
        hg_z = [cut((7 + i) * TOK, TOK) for i in range(2)]
        hg_v, hg_kt = cut(9 * TOK, 5, P), cut(9 * TOK + 640, 5, P)
        hg_s = cut(9 * TOK + 1280, 6, P)
        fx_sqq, fx_sqk, fx_q, fx_k = [cut(i * TOK, TOK) for i in range(4)]
        fx_kt, fx_v = cut(4 * TOK, 5, P), cut(4 * TOK + 640, 5, P)
        fx_kc = cut(4 * TOK + 1280, P)
        fx_ex = [cut(4 * TOK + 1408 + i * 512, 512) for i in range(2)]
        fx_pt = [cut(4 * TOK + 2432 + i * 512, 512) for i in range(2)]
        fx_os = cut(4 * TOK + 3456, NS_TOK)
        lr_tiles = [[cut((6 * par + i) * CONV, CONV) for i in range(6)] for par in range(2)]

        with ExitStack() as r2:
            def late(name, shape, dt=F32):
                return r2.enter_context(nc.sbuf_tensor(name, shape, dt))

            y32 = late("y32", [P, KT, TOK])
            xT = late("xT", [P, KT, TOK])
            ss2 = late("ss2", [P, TOK])
            sq2 = [late(f"sq2_{i}", [P, TOK]) for i in range(2)]
            rstd2 = late("rstd2", [P, TOK])
        with ExitStack() as r3:
            act_hi = r3.enter_context(nc.sbuf_tensor("act_hi", [P, 4, TOK], F32R))
            act_lo = r3.enter_context(nc.sbuf_tensor("act_lo", [P, 4, TOK], F32R))
            silu = [r3.enter_context(nc.sbuf_tensor(f"silu{i}", [P, TOK], F32)) for i in range(2)]
            glu = [r3.enter_context(nc.sbuf_tensor(f"glu{i}", [P, TOK], F32)) for i in range(2)]
            y_tok = [r3.enter_context(nc.sbuf_tensor(f"y_tok{i}", [P, 512], F32)) for i in range(4)]

        pair = [ctx.enter_context(nc.psum_tensor(f"pair{i}", [P, 1024], F32)) for i in range(4)]

        def banks(t, n=HT):
            return t[:, :].rearrange("p (b n) -> p b n", b=2)[:, :, 0:n]

        def two(ap):
            return ap.rearrange("p (b n) -> p b n", b=2)

        def raw_half(at):
            block, h = raw[(at // 2) % 2], at % 2
            if at >= 2 * (N1 + N2 + 8):
                src = block[:, :].rearrange("p (k c) -> p k c", k=4)[:, :, h * 2 * P:(h + 1) * 2 * P]
            else:
                src = block[:, h * 8 * P:(h + 1) * 8 * P].rearrange("p (k c) -> p k c", k=8)
            k = src.shape[1]
            return src, *[w[at % RING][:, :].rearrange("p (k c) -> p k c", k=k) for w in (w_hi, w_lo)]

        xT_dram = nc.dram_tensor("xT_spill", [KT, P, TOK], F32, kind="Internal").ap()
        mixed_dram = nc.dram_tensor("mixed_spill", [KT, P, TOK], F32, kind="Internal").ap()

        S = {}
        for name in """
        pe_step dve_step act_step pool_step
        ident_made consts_made raw0_loaded raw1_loaded hi_done lo_done half_used evac_done
        x_loaded0 x_loaded1 x_loaded2 x_loaded3 x_loaded4 prow_loaded prow_zeroed pcol_psum pcol_ready
        xt_psum xt_copied xt_spilled x_squared ss_psum rstd_ready norm_t norm_hi norm_lo
        cols_set bias_loaded cache_loaded lru_w_loaded ssm_in_loaded hgrn_in_loaded
        sm_abs sm_exp sm_a sm_arg_ready sm_cum sm_rows_ready sm_past_psum sm_tr sm_col sm_tot sm_tot_psum sm_etot sm_fox sm_fox2 logf_out
        y_done y_stored
        sd_conv sd_silu sd_tr sd_btok sd_vx sd_cb_psum sd_cbm sd_kv sd_state sd_bc_psum sd_bc_copied sd_argd sd_expd sd_attd
        sd_o sd_yv sd_sqd sd_stat sd_rstd sd_out
        hg_f hg_ln hg_cumd hg_ec hg_karg hg_kexp hg_kdd hg_tr hg_tok hg_diag hg_att0 hg_zarg hg_zexp hg_zd hg_lvl hg_lvld hg_kv
        hg_state hg_o hg_sqd hg_stat hg_rstd hg_out
        fx_sqd fx_stat fx_rstd fx_qkd fx_tr fx_tok fx_bias fx_score fx_neg fx_expd fx_pd fx_t fx_ptd fx_pv fx_osd fx_kout fx_vout
        lr_conv lr_gates lr_act lr_m2 lr_sqrt oc_ready oc_psum oc_copied oc_stored
        """.split():
            S[name] = ctx.enter_context(nc.semaphore(name))
        for name in """
        y_loaded xT_loaded0 xT_loaded x2_done x2_squared x2_summed
        gate_done silu_done silu_scaled glu_done act_hi_done act_lo_done down_out x_added
        out_psum out_copied0 out_copied1 out_stored0 out_stored1 out_stored2 out_stored3
        """.split():
            S[name] = ctx.enter_context(nc.semaphore(name))

        block = ctx.enter_context(nc.Block())

        class Own:

            def __init__(self, eng, step_name):
                self.eng, self.step_name, self.count = eng, step_name, {}

            def tell(self, ins, name):
                self.count[name] = self.count.get(name, 0) + 1
                ins.then_inc(S[name], 1)

            def mark(self, ins, name):
                self.tell(ins, name)
                self.eng.wait_ge(S[name], self.count[name])

            def step(self, ins):
                self.mark(ins, self.step_name)

        @block.sync
        def _(sp):
            def load_vectors():
                def prow(r, n):
                    return prow0[r:r + n, :] if r < P else prow1[r - P:r - P + n, :]

                sp.wait_ge(S["prow_zeroed"], 1)
                for name, r, n in (("ln1", R_LN1, 16), ("ln2", R_LN2, 16), ("ssm_conv_b", R_SCB, 8),
                                   ("ssm_norm", R_SNORM, 4), ("hgrn_norm", R_HNORM, 4), ("hgrn_lb_logits", R_LB, 4),
                                   ("lru_conv_b", R_LCB, 4), ("lru_b_r", R_BR, 4), ("lru_b_i", R_BI, 4),
                                   ("lru_lambda", R_LAM, 4)):
                    sp.dma_start(prow(r, n), a[name][0].rearrange("(n p) -> n p", p=P)).then_inc(S["prow_loaded"], 16)
                sp.dma_start(prow(R_H0, 4), a["state_lru"][0, 0].rearrange("(n p) -> n p", p=P)
                             ).then_inc(S["prow_loaded"], 16)
                for name, r, j, n in (("ssm_conv_w", R_SCW, 4, 8), ("lru_conv_w", R_LCW, 4, 4)):
                    sp.dma_start(prow(r, j * n), a[name][0].rearrange("j (n p) -> (j n) p", p=P)
                                 ).then_inc(S["prow_loaded"], 16)
                for name, r, j, n in (("state_ssm_conv", R_SCS, 3, 8), ("state_lru_conv", R_LCS, 3, 4)):
                    sp.dma_start(prow(r, j * n), a[name][0, 0].rearrange("j (n p) -> (j n) p", p=P)
                                 ).then_inc(S["prow_loaded"], 16)
                for name, r in (("fox_q_norm", R_QN), ("fox_k_norm", R_KN)):
                    for k in range(2):
                        sp.dma_start(prow(r, 1)[:, 64 * k:64 * k + 64], a[name]).then_inc(S["prow_loaded"], 16)

            for c, (t_0, n) in enumerate(CHUNKS):
                if c == 3:
                    load_vectors()
                src = a["x_prompt"][0, t_0:t_0 + n, :] if c < 4 else a["x_sample"][0]
                sp.dma_start(xtok[0:n, c, :], src).then_inc(S[f"x_loaded{c}"], 16)

            w_in = a["w_in"][0].rearrange("(k p) c -> p k c", p=P)
            for n, (kind, unit, pt, u) in enumerate(BLOCKS):
                if n >= 2:
                    sp.wait_ge(S["lo_done"], 2 * n - 2)
                dst = raw[n % 2][:, :].rearrange("p (k c) -> p k c", c=P)
                if kind == "small":
                    sp.dma_start(dst[:, :, 0:64], w_in[:, :, W_CF:W_CF + 64]).then_inc(S["raw0_loaded"], 16)
                    sp.dma_start(dst[:, :, 64:P], w_in[:, :, W_DT:W_DT + 64]).then_inc(S["raw0_loaded"], 16)
                else:
                    c0 = column_of(kind, unit, pt)
                    sp.dma_start(dst, w_in[:, :, c0:c0 + P]).then_inc(S[f"raw{n % 2}_loaded"], 16)
                if n == N1 - 3:
                    sp.wait_ge(S["y_done"], 12)
                    sp.wait_ge(S["y_stored"], 16 * 12)
                    for q in range(4):
                        sp.dma_start(y32[:, 3 * q:3 * q + 3, :], mixed_dram[3 * q:3 * q + 3].rearrange("k p t -> p k t")
                                     ).then_inc(S["y_loaded"], 16)
                if n == 1:
                    sp.wait_ge(S["xt_copied"], 20)
                    for q in range(4):
                        sp.dma_start(xT_dram[4 * q:4 * q + 4].rearrange("k p t -> p k t"), xT0[:, 4 * q:4 * q + 4, :]
                                     ).then_inc(S["xt_spilled"], 16)

            w_out = a["w_out"][0].rearrange("(k p) c -> p k c", p=P)
            for n in range(N1, N1 + 2):
                sp.wait_ge(S["lo_done"], 2 * n - 2)
                c0 = (n - N1) * P
                sp.dma_start(raw[n % 2][:, :].rearrange("p (k c) -> p k c", c=P), w_out[:, :, c0:c0 + P]
                             ).then_inc(S[f"raw{n % 2}_loaded"], 16)
            sp.wait_ge(S["y_done"], 16)
            sp.wait_ge(S["oc_stored"], 96)
            for q in range(4):
                sp.dma_start(xT[:, 4 * q:4 * q + 4, :], xT_dram[4 * q:4 * q + 4].rearrange("k p t -> p k t")
                             ).then_inc(S["xT_loaded" if q else "xT_loaded0"], 16)
            with sp.Fori(0, (N2 - 2) // 2) as i:
                for j in range(2):
                    n = N1 + 2 + j
                    sp.wait_ge(S["lo_done"], i * 4 + (2 * n - 2))
                    sp.dma_start(raw[n % 2][:, :].rearrange("p (k c) -> p k c", c=P),
                                 w_out[:, :, bass.ds(i * (2 * P) + (2 + j) * P, P)]
                                 ).then_inc(S[f"raw{n % 2}_loaded"], 16)
            w_gate = a["w_gate"][0].rearrange("(k p) c -> p k c", p=P)
            w_up = a["w_up"][0].rearrange("(k p) c -> p k c", p=P)
            with sp.Fori(0, GROUPS) as g:
                for j in range(12):
                    n = N1 + N2 + j
                    sp.wait_ge(S["lo_done"], g * 24 + (2 * n - 2))
                    if j < 8:
                        w = w_gate if j % 2 == 0 else w_up
                        sp.dma_start(raw[n % 2][:, :].rearrange("p (k c) -> p k c", c=P),
                                     w[:, :, bass.ds(g * (4 * P) + (j // 2) * P, P)]
                                     ).then_inc(S[f"raw{n % 2}_loaded"], 16)
                    else:
                        c0 = (j - 8) * 4 * P
                        src = a["w_down"][0][bass.ds(g * (4 * P), 4 * P), :].rearrange("(k p) c -> p k c", p=P)
                        sp.dma_start(raw[n % 2][:, :].rearrange("p (k c) -> p k c", k=4), src[:, :, c0:c0 + 4 * P]
                                     ).then_inc(S[f"raw{n % 2}_loaded"], 16)

        @block.gpsimd
        def _(pool):
            own = Own(pool, "pool_step")
            own.step(pool.memset(ones[:, :], 1.0))
            own.step(pool.memset(const[:, :], 0.0))
            own.step(pool.memset(const[:, 0:1], EPS))
            own.mark(pool.affine_select(out=ident[:, :], in_=ones[:, :], compare_op=ALU.is_equal, fill=0.0, base=0,
                                        pattern=[[-1, P]], channel_multiplier=1), "ident_made")

            def lo_half(u):
                value, at = u if isinstance(u, tuple) else (u, u)
                pool.wait_ge(S["hi_done"], value + 1)
                src, hi, lo = raw_half(at)
                pool.tensor_tensor(lo, src, hi.bitcast(F32), ALU.subtract).then_inc(S["lo_done"], 1)

            for u in range(4):
                lo_half(u)
            pool.wait_ge(S["norm_lo"], KT)
            pool.wait_ge(S["xt_spilled"], 64)
            lo_half(4)
            own.step(pool.affine_select(out=tri[:, :], in_=ones[:, :], compare_op=ALU.is_ge, fill=0.0, base=0,
                                        pattern=[[1, P]], channel_multiplier=-1))
            own.step(pool.affine_select(out=ident_r[:, :], in_=ones[:, :], compare_op=ALU.is_equal, fill=0.0, base=0,
                                        pattern=[[-1, P]], channel_multiplier=1))
            own.step(pool.memset(block_ones[:, :], 0.0))
            own.step(pool.affine_select(out=maskneg[:, :], in_=block_ones[:, :], compare_op=ALU.is_ge, fill=NEG, base=0,
                                        pattern=[[-1, P]], channel_multiplier=1))
            own.step(pool.memset(block_ones[0:64, 0:64], 1.0))
            own.step(pool.memset(block_ones[64:P, 64:P], 1.0))
            lo_half(5)
            own.step(pool.memset(level_mask[:, :, :], 1))
            for lv in range(LEVELS):
                lo_half(6 + lv)
                h = 1 << lv
                m = level_mask[:, lv, :].rearrange("p (c b j) -> p c b j", c=4, j=h)
                own.step(pool.affine_select(out=m, in_=m, compare_op=ALU.is_ge, fill=0.0, base=0,
                                            pattern=[[0, 4], [-2 * h, 64 // h], [0, h]], channel_multiplier=1))
                last = pool.affine_select(out=m, in_=m, compare_op=ALU.is_ge, fill=0.0, base=h - 1,
                                          pattern=[[0, 4], [2 * h, 64 // h], [0, h]], channel_multiplier=-1)
                if lv < LEVELS - 1:
                    own.step(last)
            own.mark(last, "consts_made")
            before = 2 * (N1 + N2)
            done = 6 + LEVELS
            whole = (before - done) // 4
            with pool.Fori(0, whole) as i:
                for j in range(4):
                    lo_half((i * 4 + (done + j), done + j))
            for u in range(done + whole * 4, before):
                lo_half(u)
            with pool.Fori(0, GROUPS) as g:
                for j in range(24):
                    lo_half((g * 24 + (before + j), before + j))

        @block.tensor
        def _(pe):
            def mm(out, lhsT, rhs, start=True, stop=True):
                return nc.tensor.matmul(out, lhsT, rhs, start=start, stop=stop)

            def gemm_half(value, at, h, dst, inputs_of=None):
                pe.wait_ge(S["lo_done"], value + 1)
                wh, wl = w_hi[at % RING], w_lo[at % RING]
                for k in range(8):
                    kt = 8 * h + k
                    if inputs_of is not None:
                        pe.wait_ge(S["norm_lo"], inputs_of + kt + 1)
                    first, last = (h == 0 and k == 0), (h == 1 and k == 7)
                    for q, (w, x) in enumerate(((wh, h_hi), (wh, h_lo), (wl, h_hi))):
                        for b in range(2):
                            m = mm(dst[:, b * 512:b * 512 + HT], w[:, k * P:(k + 1) * P],
                                   x[:, kt, b * HT:(b + 1) * HT], start=first and q == 0, stop=last and q == 2)
                return m

            def sum_over_partitions(dst, src, mat, start=True, stop=True):
                for b in range(2):
                    m = mm(dst[:, b * 512:b * 512 + HT], mat[:, :], src[:, b * HT:(b + 1) * HT], start, stop)
                return m

            def chunk_transposes(dst, src):
                for c, (t_0, n) in enumerate(CHUNKS):
                    m = pe.transpose(dst[0:n, c * P:(c + 1) * P], src[:, t_0:t_0 + n], ident[:, :])
                return m

            pe.wait_ge(S["ident_made"], 1)
            for c, (t_0, n) in enumerate(CHUNKS):
                pe.wait_ge(S[f"x_loaded{c}"], 16)
                for q in range(4):
                    i = 4 * c + q
                    if i >= 8:
                        pe.wait_ge(S["xt_copied"], i - 7)
                    bank = pair[(i % 8) // 2][:, 512 * (i % 2):512 * (i % 2) + 512]
                    for r in range(4):
                        k = 4 * q + r
                        m = pe.transpose(bank[:, r * n:(r + 1) * n], xtok[0:n, c, k * P:(k + 1) * P], ident[0:n, 0:n])
                    m.then_inc(S["xt_psum"], 1)
            pe.wait_ge(S["xt_copied"], 16)
            for c, (t_0, n) in enumerate(CHUNKS):
                pe.wait_ge(S["x_squared"], c + 1)
                m = mm(pair[3][:, t_0:t_0 + n], ss_tok[0:n, c:c + 1].to_broadcast([n, P]), ident[0:n, 0:n])
            m.then_inc(S["ss_psum"], 1)
            pe.wait_ge(S["prow_loaded"], 16 * 19)
            pe.transpose(pair[2][:, 0:P], prow0[:, :], ident[:, :])
            pe.transpose(pair[2][:, P:P + 64], prow1[:, :], ident[0:64, 0:64]).then_inc(S["pcol_psum"], 1)

            def small(n, s, u):
                if s == 0:
                    pe.wait_ge(S["cache_loaded"], 48)
                    pe.transpose(pair[3][0:8, 0:P], past_logf[:, :], ident[:, :]).then_inc(S["sm_past_psum"], 1)
                else:
                    pe.wait_ge(S["sm_rows_ready"], 1)
                    chunk_transposes(pair[2], sm_rows[:, 0:TOK]).then_inc(S["sm_tr"], 1)
                    pe.wait_ge(S["sm_tot"], 1)
                    mm(pair[3][:, 512:552], ones[64:72, :], tot8[64:72, :, :].rearrange("p h c -> p (h c)")
                       ).then_inc(S["sm_tot_psum"], 1)

            def ssd(g, s, u):
                if s == 1:
                    pe.wait_ge(S["sd_silu"], 4 * g + 4)
                    if u > 0:
                        pe.wait_ge(S["y_done"], Y_AFTER[u - 1])
                    else:
                        pe.wait_ge(S["sm_col"], 1)
                        pe.wait_ge(S["sm_etot"], 1)
                    chunk_transposes(pair[2], part[u % 2, 0]).then_inc(S["sd_tr"], 1)
                    chunk_transposes(pair[3], part[u % 2, 2]).then_inc(S["sd_tr"], 1)
                elif s == 2:
                    pe.wait_ge(S["sd_btok"], g + 1)
                    chunk_transposes(pair[2], part[u % 2, 3]).then_inc(S["sd_tr"], 1)
                    pe.wait_ge(S["sd_vx"], 2 * g + 1)
                    for c, (t_0, n) in enumerate(CHUNKS):
                        m = mm(pair[3][0:n, t_0:t_0 + n], part[u % 2, 0][:, t_0:t_0 + n], part[u % 2, 1][:, t_0:t_0 + n])
                    m.then_inc(S["sd_cb_psum"], 1)
                elif s == 3:
                    pe.wait_ge(S["sd_cbm"], g + 1)
                    for c, (t_0, n) in enumerate(CHUNKS):
                        dst = pair[3][:, c * 2 * P:(c + 1) * 2 * P] if c < 4 else pair[2][:, 0:2 * P]
                        m = mm(dst, sd_b[0:n, c, :], sd_vd[0:n, c, :])
                    m.then_inc(S["sd_kv"], 1)
                if 4 <= s <= 8:
                    hh = s - 5
                    if hh >= 0:
                        pe.wait_ge(S["sd_attd"], 4 * g + hh + 1)
                        if hh == 2:
                            pe.wait_ge(S["sd_yv"], 2 * g + 1)
                        pb, vc = 64 * (hh % 2), slice(64 * hh, 64 * hh + 64)
                        for c, (t_0, n) in enumerate(CHUNKS):
                            out = pair[3][pb:pb + 64, t_0:t_0 + n]
                            m = mm(out, sd_v[0:n, c, vc], sd_att[0:n, t_0:t_0 + n], True, c == 0)
                            if c > 0:
                                m = mm(out, sd_s[:, c - 1 if c < 4 else 4, vc], sd_cd[:, t_0:t_0 + n], False, True)
                        m.then_inc(S["sd_o"], 1)
                    if hh < 3:
                        if s == 4:
                            pe.wait_ge(S["sd_state"], g + 1)
                        else:
                            pe.wait_ge(S["sd_bc_copied"], 4 * g + hh + 1)
                        h = 4 * g + hh + 1
                        row = ident[64:72, 64 + h:65 + h].to_broadcast([8, P])
                        mm(pair[2][:, 0:512], row, small_cum[64:72, 0:512])
                        mm(pair[2][:, 512:TOK], row, small_cum[64:72, 512:TOK]).then_inc(S["sd_bc_psum"], 1)
                elif s == 9:
                    pe.wait_ge(S["sd_sqd"], 2 * g + 2)
                    sum_over_partitions(pair[2], sd_sq[0], ones, True, False)
                    sum_over_partitions(pair[2], sd_sq[1], ones, False, True).then_inc(S["sd_stat"], 1)

            def hgrn(n, s, u):
                if s == 1:
                    pe.wait_ge(S["y_done"], Y_AFTER[u - 1])
                    pe.wait_ge(S["evac_done"], 1 + 12 + 4 * n + 3)
                    chunk_transposes(pair[2], part[u % 2, 2]).then_inc(S["hg_tr"], 1)
                    pe.wait_ge(S["hg_kdd"], n + 1)
                    chunk_transposes(pair[3], hg_kd).then_inc(S["hg_tr"], 1)
                elif s == 2:
                    pe.wait_ge(S["hg_tok"], 2 * n + 1)
                    for c, (t_0, m_) in enumerate(CHUNKS):
                        m = mm(pair[2][0:m_, t_0:t_0 + m_], hg_k[:, t_0:t_0 + m_], part[u % 2, 0][:, t_0:t_0 + m_])
                    m.then_inc(S["hg_diag"], 1)
                    pe.wait_ge(S["hg_tok"], 2 * n + 2)
                    level(n, 0, u)
                    level(n, 1, u)
                elif s in (3, 4):
                    level(n, 2 * s - 4, u)
                    level(n, 2 * s - 3, u)
                    if s == 4:
                        pe.wait_ge(S["hg_att0"], n + 1)
                        for c, (t_0, m_) in enumerate(CHUNKS):
                            m = mm(pair[2][:, c * P:(c + 1) * P], hg_kt[0:m_, c, :], hg_v[0:m_, c, :])
                        m.then_inc(S["hg_kv"], 1)
                elif s == 5:
                    level(n, 6, u)
                elif s == 6:
                    pe.wait_ge(S["hg_state"], n + 1)
                    pe.wait_ge(S["hg_lvld"], LEVELS * (n + 1))
                    for c, (t_0, m_) in enumerate(CHUNKS):
                        out = pair[3][:, t_0:t_0 + m_]
                        m = mm(out, hg_v[0:m_, c, :], hg_att[0:m_, t_0:t_0 + m_], True, c == 0)
                        if c > 0:
                            m = mm(out, hg_s[:, c - 1 if c < 4 else 4, :], hg_qc[:, t_0:t_0 + m_], False, True)
                    m.then_inc(S["hg_o"], 1)
                elif s == 7:
                    pe.wait_ge(S["hg_sqd"], n + 1)
                    sum_over_partitions(pair[2], hg_lf, ones).then_inc(S["hg_stat"], 1)

            def level(n, lv, u):
                h = 1 << lv
                pe.wait_ge(S["hg_zd"], LEVELS * n + lv + 1)
                if lv >= 2:
                    pe.wait_ge(S["hg_lvld"], LEVELS * n + lv - 1)
                bank = pair[3][:, 512 * (lv % 2):512 * (lv % 2) + 512]
                z = hg_z[lv % 2]
                for c, (t_0, n_) in enumerate(CHUNKS if lv < 6 else CHUNKS[:4]):
                    right = z[:, t_0:t_0 + n_].rearrange("p (b s j) -> p b s j", s=2, j=h)[:, :, 1, :]
                    w = n_ // 2
                    m = mm(bank[0:n_, c * 64:c * 64 + w].rearrange("p (b j) -> p b j", j=h), z[:, t_0:t_0 + n_], right)
                m.then_inc(S["hg_lvl"], 1)

            def fox_step(n, k):
                base = 10 * n
                if k + 2 < 10:
                    i = k + 2
                    hh, tb = FOX_ITEMS[i]
                    pb = 64 * hh
                    if i >= 2:
                        pe.wait_ge(S["fx_expd"], base + i - 1)
                    bank = pair[2][:, 512 * (i % 2):512 * (i % 2) + 512]
                    if tb < 4:
                        t_0, m_, keys, k0, q0 = tb * P, P, (tb + 1) * P, 0, tb * P
                    else:
                        t_0, m_, keys, k0, q0 = NP_TOK, NS_TOK, PAST + NS_TOK, NP_TOK, NP_TOK + PAST
                    q = fx_q[pb:pb + 64, t_0:t_0 + m_]
                    mm(bank[0:m_, 0:keys], cum_t[0:104, q0:q0 + m_], fx_ch[hh][0:104, k0:k0 + keys], True, False)
                    if tb < 4:
                        mm(bank[0:m_, 0:keys], q, fx_k[pb:pb + 64, 0:keys], False, False)
                    else:
                        mm(bank[0:m_, 0:PAST], q, fx_kc[pb:pb + 64, :], False, False)
                        mm(bank[0:m_, PAST:keys], q, fx_k[pb:pb + 64, t_0:t_0 + m_], False, False)
                    r = slice(0, P) if m_ == P else slice(pb, pb + NS_TOK)
                    mm(bank[0:m_, keys - m_:keys], ident_r[r, r], maskneg[r, r], False, True
                       ).then_inc(S["fx_score"], 1)
                if 0 <= k + 1 < 10:
                    i = k + 1
                    hh, tb = FOX_ITEMS[i]
                    pe.wait_ge(S["fx_pd"], base + i + 1)
                    if i >= 1:
                        pe.wait_ge(S["fx_ptd"], base + i)
                    p = fx_ex[i % 2]
                    blocks = [(b * P, P) for b in range(tb + 1)] if tb < 4 else [(0, P), (P, NS_TOK)]
                    m_ = P if tb < 4 else NS_TOK
                    for b, (s_0, w) in enumerate(blocks):
                        m = pe.transpose(pair[3][0:w, 512 + b * m_:512 + (b + 1) * m_], p[0:m_, s_0:s_0 + w],
                                         ident[0:m_, 0:m_])
                    m.then_inc(S["fx_t"], 1)
                if 0 <= k:
                    hh, tb = FOX_ITEMS[k]
                    pb = 64 * hh
                    pe.wait_ge(S["fx_ptd"], base + k + 1)
                    pt = fx_pt[k % 2]
                    if tb < 4:
                        if k == 2:
                            pe.wait_ge(S["fx_osd"], n + 1)
                        out = pair[3][pb:pb + 64, tb * P:(tb + 1) * P]
                        for b in range(tb + 1):
                            m = mm(out, fx_v[:, b, pb:pb + 64], pt[:, b * P:(b + 1) * P], b == 0, b == tb)
                    else:
                        out = pair[3][pb:pb + 64, 0:NS_TOK]
                        mm(out, cache_v[:, P * n + pb:P * n + pb + 64], pt[:, 0:NS_TOK], True, False)
                        m = mm(out, fx_v[0:NS_TOK, 4, pb:pb + 64], pt[0:NS_TOK, NS_TOK:2 * NS_TOK], False, True)
                    m.then_inc(S["fx_pv"], 1)

            def fox(n, s, u):
                if s == 1:
                    pe.wait_ge(S["y_done"], Y_AFTER[u - 1])
                    pe.wait_ge(S["fx_sqd"], 2 * n + 2)
                    sum_over_partitions(pair[2], fx_sqq, block_ones).then_inc(S["fx_stat"], 1)
                    sum_over_partitions(pair[3], fx_sqk, block_ones).then_inc(S["fx_stat"], 1)
                elif s == 2:
                    pe.wait_ge(S["fx_qkd"], 2 * n + 2)
                    chunk_transposes(pair[2], fx_k)
                    pe.transpose(pair[2][:, 5 * P:6 * P], cache_k[:, n * P:(n + 1) * P], ident[:, :]
                                 ).then_inc(S["fx_tr"], 1)
                    chunk_transposes(pair[3], part[u % 2, 2]).then_inc(S["fx_tr"], 1)
                elif s == 3:
                    pe.wait_ge(S["fx_tok"], 3 * n + 3)
                    pe.wait_ge(S["fx_bias"], 2 * n + 2)
                if s in FOX_STEPS:
                    for k in FOX_STEPS[s]:
                        fox_step(n, k)

            def lru(n, s, u):
                if s == 1:
                    pe.wait_ge(S["lr_conv"], n + 1)
                    pe.wait_ge(S["lru_w_loaded"], 32 * (n + 1))
                    if n > 0:
                        pe.wait_ge(S["lr_act"], n)
                    else:
                        pe.wait_ge(S["y_done"], Y_AFTER[u - 1])
                    lr_x = lr_tiles[n % 2][0]
                    for w in range(2):
                        for b in range(2):
                            m = mm(pair[2 + w][:, 512 * b:512 * b + 290], lru_w[:, w, :], lr_x[:, 290 * b:290 * b + 290])
                        m.then_inc(S["lr_gates"], 1)

            mixers = {"small": small, "ssd": ssd, "hgrn": hgrn, "fox": fox, "lru": lru}

            for task in ORDER:
                if task[0] == "half":
                    _, n, h = task
                    if h == 0 and n >= 2:
                        pe.wait_ge(S["evac_done"], n - 1)
                    m = gemm_half(2 * n + h, 2 * n + h, h, pair[n % 2], inputs_of=0 if n == 0 else None)
                    m.then_inc(S["half_used"], 1)
                else:
                    _, kind, n, s, u = task
                    mixers[kind](n, s, u)
            for kind, n, s, u in TAIL:
                mixers[kind](n, s, u)
            pe.wait_ge(S["oc_ready"], 1)
            pe.wait_ge(S["lr_act"], 4)
            pe.transpose(pair[2][0:O_ALL, 0:P], out_col[:, :], ident[:, :]).then_inc(S["oc_psum"], 1)

            def wout_block(value_block, j, wait_inputs):
                n = N1 + j
                dst = pair[j % 4]
                if j < 2 and isinstance(value_block, int):
                    pe.wait_ge(S["evac_done"], N1)
                for h in range(2):
                    m = gemm_half(value_block * 2 + (2 * N1 + h), 2 * n + h, h, dst,
                                  inputs_of=KT if wait_inputs else None)
                    m.then_inc(S["half_used"], 1)

            for j in range(4):
                if j == 2:
                    pe.wait_ge(S["oc_copied"], 1)
                wout_block(j, j, j == 0)
            with pe.Fori(1, N2 // 4) as i:
                for j in range(4):
                    pe.wait_ge(S["x2_done"], i * 4 + (j - 3))
                    wout_block(i * 4 + j, j, False)
            def swiglu(g, first, last=False):
                pairs = 3 if last else 4
                for j in range(8):
                    if first and j == 1:
                        pe.wait_ge(S["x2_summed"], N2)
                        sum_over_partitions(pair[3], ss2, ones).then_inc(S["ss_psum"], 1)
                    elif first and j == 3:
                        pe.wait_ge(S["rstd_ready"], 2)
                    if not first or j >= 4:
                        if j < 4:
                            pe.wait_ge(S["x_added"], g * 16 + (j - 3))
                        elif j % 2 == 0:
                            pe.wait_ge(S["glu_done"], g * 4 + (j // 2 - 1))
                    for h in range(2):
                        at = 2 * (N1 + N2 + j) + h
                        m = gemm_half(g * 24 + at, at, h, pair[j % 4], inputs_of=2 * KT if first and j == 0 else None)
                        m.then_inc(S["half_used"], 1)
                for q in range(8):
                    at = 2 * (N1 + N2 + 8) + q
                    pe.wait_ge(S["lo_done"], g * 24 + (at + 1))
                    wh, wl = w_hi[at % RING], w_lo[at % RING]
                    for jj in range(2):
                        n = 2 * q + jj
                        if n == 0:
                            pe.wait_ge(S["glu_done"], g * 4 + 3)
                        elif n == 2:
                            pe.wait_ge(S["glu_done"], g * 4 + 4)
                        elif n >= pairs:
                            pe.wait_ge(S["x_added"], g * 16 + (n - (pairs - 1)))
                        dst = pair[n % pairs]
                        for k in range(4):
                            if n == 0:
                                pe.wait_ge(S["act_lo_done"], g * 4 + (k + 1))
                            for r, (w, x) in enumerate(((wh, act_hi), (wh, act_lo), (wl, act_hi))):
                                for b in range(2):
                                    c0 = k * 2 * P + jj * P
                                    m = mm(dst[:, b * 512:b * 512 + HT], w[:, c0:c0 + P],
                                           x[:, k, b * HT:(b + 1) * HT], k == 0 and r == 0, k == 3 and r == 2)
                        m.then_inc(S["half_used" if jj else "down_out"], 1)
                        if last:
                            for i, iq, c, after in OUT_STEPS:
                                if after == n:
                                    out_step(i, iq, c)

            def out_step(i, q, c):
                t_0, n = CHUNKS[c]
                pe.wait_ge(S["x_added"], 16 * (GROUPS - 1) + 4 * q + 4)
                if i >= 2:
                    pe.wait_ge(S[f"out_copied{i % 2}"], i // 2)
                bank = pair[3][0:n, 512 * (i % 2):512 * (i % 2) + 512]
                for f in range(4):
                    m = pe.transpose(bank[:, f * P:(f + 1) * P], xT[:, 4 * q + f, t_0:t_0 + n], ident[:, :])
                m.then_inc(S["out_psum"], 1)

            swiglu(0, True)
            with pe.Fori(1, GROUPS - 1) as g:
                swiglu(g, False)
            swiglu(GROUPS - 1, False, True)

        @block.scalar
        def _(act):
            own = Own(act, "act_step")

            def fn(out, in_, f, **kw):
                return nc.scalar.activation(out, in_, f, **kw)

            def hi_half(value, at):
                n = at // 2
                if at % 2 == 0:
                    extra = 16 if n % 2 == 0 else 0
                    act.wait_ge(S[f"raw{n % 2}_loaded"], (value - at) * 4 + (16 * (n // 2 + 1) + extra))
                if at >= RING:
                    act.wait_ge(S["half_used"], value - 3)
                src, hi, _ = raw_half(at)
                fn(hi, src, ACT.Copy).then_inc(S["hi_done"], 1)

            def squares(out, src, name):
                own.tell(fn(out, src, ACT.Square), name)

            def rstd_of(out, psum, width, name, src_name, count):
                act.wait_ge(S[src_name], count)
                own.step(fn(out, psum, ACT.Ln, scale=1.0 / width, bias=eps_col))
                own.mark(fn(out, out, ACT.Exp, scale=-0.5), name)

            for c, (t_0, n) in enumerate(CHUNKS):
                act.wait_ge(S[f"x_loaded{c}"], 16)
                own.mark(fn(sq0[0:n, :], xtok[0:n, c, :], ACT.Square, accum_out=ss_tok[0:n, c:c + 1]), "x_squared")
            for u in range(3):
                hi_half(u, u)
            rstd_of(rstd0, pair[3][:, 0:TOK], D, "rstd_ready", "ss_psum", 1)
            act.wait_ge(S["pcol_psum"], 1)
            own.mark(fn(pcol[:, :], pair[2][:, 0:192], ACT.Copy), "pcol_ready")
            for k in range(KT):
                act.wait_ge(S["norm_t"], k + 1)
                own.tell(fn(h_hi[:, k, :], t0[k], ACT.Copy), "norm_hi")

            def load_small():
                act.wait_ge(S["norm_lo"], KT)
                act.wait_ge(S["xt_spilled"], 64)
                act.wait_ge(S["cols_set"], 1)
                for dst2, src in ((cols[0:8, C_BIAS:C_BIAS + 1], a["fox_f_bias"]),
                                  (cols[64:72, C_BIAS:C_BIAS + 1], a["ssm_dt_bias"]),
                                  (cols[64:72, C_A:C_A + 1], a["ssm_a_log"])):
                    act.dma_start(dst2, src.rearrange("a h -> h a")).then_inc(S["bias_loaded"], 16)
                act.dma_start(ssm_d8[:, :], a["ssm_d"].to_broadcast([P, 8])).then_inc(S["bias_loaded"], 16)
                for dst2, src in ((cache_k[:, :], a["cache_fox_k"][0, 0].rearrange("t h d -> t (h d)")),
                                  (cache_v[:, :], a["cache_fox_v"][0, 0].rearrange("t h d -> t (h d)")),
                                  (past_logf[:, :], a["cache_fox_logf"][0, 0])):
                    act.dma_start(dst2, src).then_inc(S["cache_loaded"], 16)

            def evacuate(n):
                kind, unit, pt, u = BLOCKS[n]
                if kind == "small":
                    return
                act.wait_ge(S["half_used"], 2 * n + 2)
                if u >= 2:
                    act.wait_ge(S["y_done"], Y_AFTER[u - 2])
                if n == 1:
                    act.wait_ge(S["evac_done"], 1)
                    act.wait_ge(S["norm_lo"], KT)
                    act.wait_ge(S["xt_spilled"], 64)
                src = pair[n % 2]
                slot = {"B": 0, "C": 1, "x0": 2, "x1": 3, "z0": 4, "z1": 5, "q": 0, "f": 1, "i": 2, "g": 3,
                        "cq": 0, "ck": 1, "cv": 2, "cg": 3, "dx": 0, "dg": 1}[pt]
                dst = part[u % 2, slot]
                if pt in ("B", "C", "x0", "x1", "dx"):
                    if pt == "dx":
                        state = pcol[:, R_LCS:R_LCS + 12].rearrange("p (j t) -> p j t", j=3)[:, :, unit]
                    else:
                        tile = {"x0": 2 * unit, "x1": 2 * unit + 1, "B": 4 + unit, "C": 6 + unit}[pt]
                        state = pcol[:, R_SCS:R_SCS + 24].rearrange("p (j t) -> p j t", j=3)[:, :, tile]
                    fn(dst[:, 0:3], zeros3, ACT.Copy)
                    fn(dst[:, PAD - 1:PAD], zeros3[:, 0:1], ACT.Copy)
                    fn(dst[:, SAMPLE_AT:SAMPLE_AT + 3], state, ACT.Copy)
                    fn(dst[:, 3:3 + HT], src[:, 0:HT], ACT.Copy)
                    fn(dst[:, 3 + HT:SAMPLE_AT], src[:, 512:512 + NP_TOK - HT], ACT.Copy)
                    ins = fn(dst[:, SAMPLE_AT + 3:SAMPLE_AT + 3 + NS_TOK], src[:, 512 + NP_TOK - HT:512 + HT], ACT.Copy)
                elif pt == "f":
                    fn(two(part[u % 2, 4][:, 0:TOK]), banks(src), ACT.Sigmoid, scale=-1.0)
                    ins = fn(two(dst[:, 0:TOK]), banks(src), ACT.Sigmoid)
                else:
                    f = {"z0": ACT.Silu, "z1": ACT.Silu, "q": ACT.Silu, "g": ACT.Silu, "cg": ACT.Sigmoid,
                         "dg": ACT.Gelu_apprx_tanh}.get(pt, ACT.Copy)
                    ins = fn(two(dst[:, 0:TOK]), banks(src), f)
                ins.then_inc(S["evac_done"], 1)

            def unit_starts(u):
                if u > 0:
                    act.wait_ge(S["y_done"], Y_AFTER[u - 1])

            def store_y(u):
                for j in range(Y_AFTER[u - 1] if u else 0, Y_AFTER[u]):
                    act.wait_ge(S["y_done"], j + 1)
                    act.dma_start(mixed_dram[Y_TILES[j]], y_out[j % 2][:, :]).then_inc(S["y_stored"], 16)

            def small(n, s, u):
                if s == 0:
                    act.wait_ge(S["sm_abs"], 1)
                    own.mark(fn(sm_e[:, 0:CONV], sm_e[:, 0:CONV], ACT.Exp, scale=-1.0), "sm_exp")
                    act.wait_ge(S["bias_loaded"], 64)
                    fn(cols[64:96, C_A:C_A + 1], cols[64:96, C_A:C_A + 1], ACT.Exp)
                    own.mark(fn(cols[:, C_LB:C_LB + 4], cols[:, C_LB:C_LB + 4], ACT.Exp), "sm_a")
                else:
                    act.wait_ge(S["sm_arg_ready"], 1)
                    fn(sm_rows[32:64, 0:TOK], small_cum[64:96, :], ACT.Copy)
                    own.mark(fn(sm_rows[96:P, 0:TOK], sm_arg[64:96, 0:TOK], ACT.Exp), "sm_rows_ready")
                    act.wait_ge(S["sm_tr"], 1)
                    fn(small_col[:, 0:4, :], pair[2][:, 0:512].rearrange("p (c n) -> p c n", c=4), ACT.Copy)
                    own.mark(fn(small_col[0:64, 4, :], pair[2][0:64, 512:640], ACT.Copy), "sm_col")
                    act.wait_ge(S["sm_tot_psum"], 1)
                    own.mark(fn(ssm_etot[:, :, :].rearrange("p h c -> p (h c)"), pair[3][:, 512:552], ACT.Exp), "sm_etot")
                    act.wait_ge(S["sm_fox"], 1)
                    fn(cum_t[0:32, :], sm_cf[0:32, :], ACT.Copy)
                    own.mark(fn(cum_s[64:96, :], sm_cf[0:32, :], ACT.Copy), "sm_fox2")
                    act.dma_start(o_pfl[0, 0].rearrange("(c t) h -> t c h", t=P), small_col[:, 0:4, 0:8]
                                  ).then_inc(S["logf_out"], 16)
                    act.dma_start(o_sfl[0, 0], small_col[0:64, 4, 0:8]).then_inc(S["logf_out"], 16)

            def ssd(g, s, u):
                if s == 0:
                    unit_starts(u)
                    act.dma_start(sd_s[:, 4, :].rearrange("n (h v) -> n h v", h=4),
                                  a["state_ssm"][0, 0, 4 * g:4 * g + 4].rearrange("h n v -> n h v")
                                  ).then_inc(S["ssm_in_loaded"], 16)
                elif s == 1:
                    for j in range(4):
                        act.wait_ge(S["sd_conv"], 4 * g + j + 1)
                        dst = part[u % 2, j]
                        fn(dst[:, 0:NP_TOK], sd_cw[j][:, 0:NP_TOK], ACT.Silu)
                        own.tell(fn(dst[:, NP_TOK:TOK], sd_cw[j][:, SAMPLE_AT:SAMPLE_AT + NS_TOK], ACT.Silu), "sd_silu")
                    act.wait_ge(S["sd_tr"], 3 * g + 1)
                    act.wait_ge(S["sd_silu"], 4 * g + 4)
                    fn(sd_b[:, 0:4, :], pair[2][:, 0:512].rearrange("p (c n) -> p c n", c=4), ACT.Copy)
                    own.tell(fn(sd_b[0:64, 4, :], pair[2][0:64, 512:640], ACT.Copy), "sd_btok")
                elif 4 <= s <= 7:
                    i = 4 * g + s - 4
                    act.wait_ge(S["sd_bc_psum"], i + 1)
                    if i > 4 * g:
                        act.wait_ge(S["sd_attd"], i)
                    own.mark(fn(sd_bc, pair[2][:, 0:TOK], ACT.Copy), "sd_bc_copied")
                    fn(sd_cd, sd_bc, ACT.Exp)
                    act.wait_ge(S["sd_argd"], i + 1)
                    own.mark(fn(sd_att, sd_att, ACT.Exp), "sd_expd")
                    if s == 4:
                        act.wait_ge(S["sd_state"], g + 1)
                        for slot, dst in ((3, o_pss), (5, o_sss)):
                            act.dma_start(dst[0, 0, 4 * g:4 * g + 4].rearrange("h n v -> n h v"),
                                          sd_s[:, slot, :].rearrange("n (h v) -> n h v", h=4)).then_inc(S["sd_out"], 16)
                elif s == 9:
                    for t in range(2):
                        act.wait_ge(S["sd_yv"], 2 * g + 2)
                        squares(sd_sq[t], sd_y[t], "sd_sqd")
                elif s == 10:
                    act.wait_ge(S["sd_sqd"], 2 * g + 2)
                    rstd_of(two(sd_bc), banks(pair[2]), 2 * P, "sd_rstd", "sd_stat", g + 1)

            def tokens_out(dst, psum):
                fn(dst[:, 0:4, :], psum[:, 0:512].rearrange("p (c n) -> p c n", c=4), ACT.Copy)
                return fn(dst[0:64, 4, :], psum[0:64, 512:640], ACT.Copy)

            def zexp(n, lv):
                act.wait_ge(S["hg_zarg"], LEVELS * n + lv + 1)
                w = TOK if lv < 6 else NP_TOK
                own.tell(fn(hg_z[lv % 2][:, 0:w], hg_z[lv % 2][:, 0:w], ACT.Exp), "hg_zexp")

            def hgrn(n, s, u):
                if s == 0:
                    unit_starts(u)
                    store_y(u - 1)
                    act.dma_start(hg_s[:, 4, :], a["state_hgrn"][0, 0, n]).then_inc(S["hgrn_in_loaded"], 16)
                    act.wait_ge(S["hg_f"], n + 1)
                    fn(hg_lf, hg_lf, ACT.Ln)
                    own.tell(fn(hg_lf2, hg_lf2, ACT.Ln), "hg_ln")
                    act.wait_ge(S["hg_cumd"], n + 1)
                    own.tell(fn(hg_qc, hg_cum, ACT.Exp), "hg_ec")
                    fn(hgrn_etot[:, 0:4], hg_cum[:, 0:NP_TOK].rearrange("p (c t) -> p c t", c=4)[:, :, P - 1], ACT.Exp)
                    fn(hgrn_etot[:, 4:5], hg_cum[:, TOK - 1:TOK], ACT.Exp)
                    act.wait_ge(S["hg_karg"], n + 1)
                    own.tell(fn(hg_kd, hg_kd, ACT.Exp), "hg_kexp")
                elif s == 1:
                    act.wait_ge(S["hg_tr"], 2 * n + 1)
                    own.tell(tokens_out(hg_v, pair[2]), "hg_tok")
                    zexp(n, 0)
                    zexp(n, 1)
                    act.wait_ge(S["hg_tr"], 2 * n + 2)
                    own.tell(tokens_out(hg_kt, pair[3]), "hg_tok")
                elif s == 2:
                    zexp(n, 2)
                    zexp(n, 3)
                elif s == 3:
                    zexp(n, 4)
                    zexp(n, 5)
                elif s == 4:
                    zexp(n, 6)
                elif s == 5:
                    act.wait_ge(S["hg_state"], n + 1)
                    for slot, dst in ((3, o_phg), (5, o_shg)):
                        act.dma_start(dst[0, 0, n], hg_s[:, slot, :]).then_inc(S["hg_out"], 16)
                elif s == 6:
                    act.wait_ge(S["hg_o"], n + 1)
                    squares(hg_lf, pair[3][:, 0:TOK], "hg_sqd")
                elif s == 7:
                    act.wait_ge(S["hg_sqd"], n + 1)
                    rstd_of(two(hg_lf2), banks(pair[2]), P, "hg_rstd", "hg_stat", n + 1)

            def fox_act(n, i):
                hh, tb = FOX_ITEMS[i]
                m_, keys = (P, (tb + 1) * P) if tb < 4 else (NS_TOK, PAST + NS_TOK)
                act.wait_ge(S["fx_neg"], 10 * n + i + 1)
                bank = pair[2][:, 512 * (i % 2):512 * (i % 2) + 512]
                own.tell(fn(fx_ex[i % 2][0:m_, 0:keys], bank[0:m_, 0:keys], ACT.Exp,
                            bias=cols[0:m_, C_NM + i % 2:C_NM + i % 2 + 1],
                            accum_out=cols[0:m_, C_RS + i % 2:C_RS + i % 2 + 1]), "fx_expd")

            def fox_act_pt(n, i):
                hh, tb = FOX_ITEMS[i]
                act.wait_ge(S["fx_t"], 10 * n + i + 1)
                if tb < 4:
                    ins = fn(fx_pt[i % 2][:, 0:(tb + 1) * P], pair[3][:, 512:512 + (tb + 1) * P], ACT.Copy)
                else:
                    fn(fx_pt[i % 2][:, 0:NS_TOK], pair[3][:, 512:512 + NS_TOK], ACT.Copy)
                    ins = fn(fx_pt[i % 2][0:NS_TOK, NS_TOK:2 * NS_TOK],
                             pair[3][0:NS_TOK, 512 + NS_TOK:512 + 2 * NS_TOK], ACT.Copy)
                own.tell(ins, "fx_ptd")

            def fox(n, s, u):
                if s == 0:
                    unit_starts(u)
                    store_y(u - 1)
                    if n > 0:
                        act.wait_ge(S["fx_kout"], 32 * n)
                        act.wait_ge(S["fx_vout"], 32 * n)
                    act.wait_ge(S["evac_done"], 1 + 12 + 16 + 4 * n + 4)
                    squares(fx_sqq, part[u % 2, 0][:, 0:TOK], "fx_sqd")
                    squares(fx_sqk, part[u % 2, 1][:, 0:TOK], "fx_sqd")
                elif s == 1:
                    for w, (out, psum) in enumerate(((fx_sqq, pair[2]), (fx_sqk, pair[3]))):
                        act.wait_ge(S["fx_stat"], 2 * n + w + 1)
                        ins = fn(two(out), banks(psum), ACT.Ln, scale=1.0 / 64, bias=eps_col)
                    own.step(ins)
                    for out in (fx_sqq, fx_sqk):
                        own.tell(fn(out, out, ACT.Exp, scale=-0.5), "fx_rstd")
                elif s == 2:
                    act.wait_ge(S["fx_tr"], 2 * n + 1)
                    own.mark(tokens_out(fx_kt, pair[2]), "fx_tok")
                    own.tell(fn(fx_kc, pair[2][:, 640:768], ACT.Copy), "fx_tok")
                    act.wait_ge(S["fx_tr"], 2 * n + 2)
                    own.mark(tokens_out(fx_v, pair[3]), "fx_tok")
                    for src, dp, ds, name in ((fx_kt, o_pfk, o_sfk, "fx_kout"), (fx_v, o_pfv, o_sfv, "fx_vout")):
                        act.dma_start(dp[0, 0].rearrange("(c t) h d -> t c (h d)", t=P)[:, :, n * P:(n + 1) * P],
                                      src[:, 0:4, :]).then_inc(S[name], 16)
                        act.dma_start(ds[0, 0].rearrange("t h d -> t (h d)")[:, n * P:(n + 1) * P],
                                      src[0:64, 4, :]).then_inc(S[name], 16)
                if s in FOX_STEPS:
                    for k in FOX_STEPS[s]:
                        if k + 2 < 10:
                            fox_act(n, k + 2)
                        if 0 <= k + 1 < 10:
                            fox_act_pt(n, k + 1)

            def load_lru(n):
                for w, name in enumerate(("lru_w_r", "lru_w_i")):
                    act.dma_start(lru_w[:, w, :], a[name][0, n]).then_inc(S["lru_w_loaded"], 16)

            def lru(n, s, u):
                lr_x, lr_r, lr_i, lr_th, lr_a, lr_m = lr_tiles[n % 2]
                if s == 0:
                    if n == 0:
                        unit_starts(u)
                        store_y(u - 1)
                        load_lru(0)
                elif s == 1:
                    act.wait_ge(S["lr_gates"], 2 * n + 2)
                    if n < 3:
                        load_lru(n + 1)
                    lb = ((lr_r, pair[2], R_BR), (lr_i, pair[3], R_BI))
                    for dst, src, r in lb:
                        ins = fn(dst.rearrange("p (b n) -> p b n", b=2), banks(src, 290), ACT.Sigmoid,
                                 bias=pcol[:, r + n:r + n + 1])
                    own.step(ins)
                    fn(lr_th, lr_r, ACT.Tanh, scale=cols[:, C_NLS8 + n:C_NLS8 + n + 1])
                    own.tell(fn(lr_a, lr_r, ACT.Exp, scale=cols[:, C_LS8 + n:C_LS8 + n + 1]), "lr_act")
                elif s == 2:
                    act.wait_ge(S["lr_m2"], n + 1)
                    own.tell(fn(lr_m, lr_m, ACT.Sqrt), "lr_sqrt")

            def split_y(ks):
                for k in ks:
                    if k < 12:
                        act.wait_ge(S["y_loaded"], 64)
                    else:
                        act.wait_ge(S["y_done"], k + 1)
                    if k % 8 == 0:
                        act.wait_ge(S["half_used"], 2 * N1 - 1 + k // 8)
                    own.tell(fn(h_hi[:, k, :], y32[:, k, :], ACT.Copy), "norm_hi")

            mixers = {"small": small, "ssd": ssd, "hgrn": hgrn, "fox": fox, "lru": lru}
            for task in ORDER:
                if task[0] == "half":
                    _, n, h = task
                    hi_half(2 * n + h + 3, 2 * n + h + 3)
                    if (n, h) == (0, 0):
                        load_small()
                    if (n, h) == (N1 - 1, 1):
                        split_y(range(8))
                    if h == 1:
                        evacuate(n)
                else:
                    _, kind, n, s, u = task
                    if (kind, s) == ("ssd", 0) and u > 0:
                        store_y(u - 1)
                    mixers[kind](n, s, u)

            split_y(range(8, 12))
            act.wait_ge(S["oc_psum"], 1)
            own.mark(fn(oc_rows[:, :], pair[2][0:O_ALL, 0:P], ACT.Copy), "oc_copied")
            for r, dst, j, t in ((O_PSC, o_psc, 3, 8), (O_SSC, o_ssc, 3, 8), (O_PLC, o_plc, 3, 4), (O_SLC, o_slc, 3, 4)):
                act.dma_start(dst[0, 0].rearrange("j (t p) -> (j t) p", p=P), oc_rows[r:r + j * t, :]
                              ).then_inc(S["oc_stored"], 16)
            for r, dst in ((O_PLH, o_plh), (O_SLH, o_slh)):
                act.dma_start(dst[0, 0].rearrange("(t p) -> t p", p=P), oc_rows[r:r + 4, :]).then_inc(S["oc_stored"], 16)

            split_y(range(12, KT))

            def wout_squares(value, j):
                act.wait_ge(S["x2_done"], value + 1)
                if j >= 2:
                    act.wait_ge(S["x2_summed"], value - 1)
                src = xT[:, bass.ds(value, 1), :].rearrange("p a t -> p (a t)")
                own.tell(fn(sq2[j % 2][:, :], src, ACT.Square), "x2_squared")

            for j in range(4):
                for h in range(2):
                    at = 2 * (N1 + j) + h + 3
                    hi_half(at, at)
                if j > 0:
                    wout_squares(j - 1, j - 1)
            with act.Fori(1, N2 // 4 - 1) as i:
                for j in range(4):
                    for h in range(2):
                        at = 2 * (N1 + j) + h + 3
                        hi_half(i * 8 + at, at)
                    wout_squares(i * 4 + (j - 1), j + 3)

            def split_x(ks):
                act.wait_ge(S["half_used"], 2 * (N1 + N2) - 1 + ks[0] // 8)
                for k in ks:
                    own.tell(fn(h_hi[:, k, :], xT[:, k, :], ACT.Copy, scale=pcol[:, R_LN2 + k:R_LN2 + k + 1]), "norm_hi")

            for j in range(N2 - 4, N2):
                for h in range(2):
                    at = 2 * (N1 + j) + h + 3
                    hi_half(at, at)
                wout_squares(j - 1, j - 1)
            split_x(range(8))
            wout_squares(N2 - 1, N2 - 1)
            split_x(range(8, KT))

            def swiglu(g, first, last):
                for j in range(12):
                    for h in range(2):
                        at = 2 * (N1 + N2 + j) + h + 3
                        if at < 2 * (N1 + N2 + 12):
                            hi_half(g * 24 + at, at)
                        elif not last:
                            hi_half(g * 24 + at, at - 24)
                    if first and j == 0:
                        rstd_of(two(rstd2[:, :]), banks(pair[3]), D, "rstd_ready", "ss_psum", 2)
                    if j < 8:
                        t = j // 2
                        if j % 2 == 0:
                            act.wait_ge(S["gate_done"], g * 4 + (t + 1))
                            own.tell(fn(silu[t % 2][:, :], silu[t % 2][:, :], ACT.Silu), "silu_done")
                        else:
                            act.wait_ge(S["glu_done"], g * 4 + (t + 1))
                            own.tell(fn(act_hi[:, t, :], glu[t % 2][:, :], ACT.Copy), "act_hi_done")

            swiglu(0, True, False)
            with act.Fori(1, GROUPS - 1) as g:
                swiglu(g, False, False)
            swiglu(GROUPS - 1, False, True)

            for i, q, c, _ in OUT_STEPS:
                t_0, n = CHUNKS[c]
                if i % 2 == 1:
                    act.wait_ge(S["out_psum"], i + 1)
                    if i >= 4:
                        act.wait_ge(S[f"out_stored{i % 4}"], 16 * (i // 4))
                    own.mark(fn(y_tok[i % 4][0:n, :], pair[3][0:n, 512:1024], ACT.Copy), "out_copied1")
                else:
                    act.wait_ge(S["out_copied0"], i // 2 + 1)
                dst = o_yp[0, t_0:t_0 + n, :] if c < 4 else o_ys[0]
                act.dma_start(dst[:, 512 * q:512 * q + 512], y_tok[i % 4][0:n, :]).then_inc(S[f"out_stored{i % 4}"], 16)
            for i in range(4):
                act.wait_ge(S[f"out_stored{i}"], 80)
            act.wait_ge(S["logf_out"], 32)
            act.wait_ge(S["oc_stored"], 96)
            act.wait_ge(S["sd_out"], 64)
            act.wait_ge(S["hg_out"], 128)
            act.wait_ge(S["fx_kout"], 128)
            act.wait_ge(S["fx_vout"], 128)

        @block.vector
        def _(dve):
            own = Own(dve, "dve_step")
            V = nc.vector

            def tt(out, x, y, op):
                return V.tensor_tensor(out, x, y, op)

            def ts(out, x, s1, s2=None, op0=ALU.mult, op1=None):
                if s2 is None:
                    return V.tensor_scalar(out, x, s1, None, op0)
                return V.tensor_scalar(out, x, s1, s2, op0, op1)

            def stt(out, x, s, y, op0, op1):
                return V.scalar_tensor_tensor(out=out, in0=x, scalar=s, in1=y, op0=op0, op1=op1)

            own.mark(V.memset(prow1[:, :], 0.0), "prow_zeroed")
            for c, (t_0, n) in enumerate(CHUNKS):
                for q in range(4):
                    i = 4 * c + q
                    dve.wait_ge(S["xt_psum"], i + 1)
                    bank = pair[(i % 8) // 2][:, 512 * (i % 2):512 * (i % 2) + 4 * n]
                    own.tell(V.tensor_copy(xT0[:, 4 * q:4 * q + 4, t_0:t_0 + n], bank.rearrange("p (r n) -> p r n", r=4)),
                             "xt_copied")
            dve.wait_ge(S["xt_copied"], 20)

            dve.wait_ge(S["pcol_ready"], 1)
            dve.wait_ge(S["rstd_ready"], 1)

            def h_lo_tile(k):
                dve.wait_ge(S["norm_hi"], k + 1)
                own.tell(tt(h_lo[:, k, :], t0[k], h_hi[:, k, :].bitcast(F32), ALU.subtract), "norm_lo")

            for k in range(KT):
                own.tell(stt(t0[k], xT0[:, k, :], pcol[:, R_LN1 + k:R_LN1 + k + 1], rstd0, ALU.mult, ALU.mult), "norm_t")
                if k >= 2:
                    if k == 2:
                        dve.wait_ge(S["norm_t"], 3)
                    h_lo_tile(k - 2)
            dve.wait_ge(S["norm_t"], KT)
            h_lo_tile(KT - 2)
            h_lo_tile(KT - 1)

            dve.wait_ge(S["norm_lo"], KT)
            dve.wait_ge(S["xt_spilled"], 64)
            own.step(V.memset(cols[:, :], 0.0))
            own.step(V.memset(cols[0:64, C_SGN:C_SGN + 1], -1.0))
            own.step(V.memset(cols[64:P, C_SGN:C_SGN + 1], 1.0))
            own.step(ts(cols[:, C_QN:C_QN + 1], pcol[:, R_QN:R_QN + 1], 64 ** -0.5))
            V.memset(sm_cf[0:32, :], 0.0)
            V.memset(sm_cf[64:P, :], 1.0)
            own.step(V.memset(sm_cf[32:64, :], 1.0))
            own.step(ts(cum_t[64:P, :], sm_cf[64:P, :], -1.0))
            own.step(V.tensor_copy(cum_s[0:64, :], sm_cf[64:P, :]))
            own.step(tt(sel_fox[:, :], ident[:, 0:8], ident[:, 32:40], ALU.add))
            for r in (64, 96):
                own.step(tt(sel_fox[:, :], sel_fox[:, :], ident[:, r:r + 8], ALU.add))
            lg = pcol[:, R_LB:R_LB + 4]
            own.mark(tt(cols[:, C_LB:C_LB + 4], lg, lg, ALU.subtract), "cols_set")

            def conv(dst, x, w_base, stride, b_col):
                own.step(ts(dst, x[:, 3:3 + CONV], pcol[:, w_base + 3 * stride:w_base + 3 * stride + 1], b_col,
                            ALU.mult, ALU.add))
                for j in (2, 1, 0):
                    ins = stt(dst, x[:, j:j + CONV], pcol[:, w_base + j * stride:w_base + j * stride + 1], dst,
                              ALU.mult, ALU.add)
                    if j:
                        own.step(ins)
                return ins

            def keep_rows(x, prompt_at, sample_at, n_tiles, tile):
                for at, src in ((prompt_at, x[:, NP_TOK:NP_TOK + 3]), (sample_at, x[:, PAD - 4:PAD - 1])):
                    dst = out_col[:, at:at + 3 * n_tiles].rearrange("p (j t) -> p j t", j=3)[:, :, tile]
                    V.tensor_copy(dst, src)

            def small(n, s, u):
                if s == 0:
                    dve.wait_ge(S["half_used"], 2)
                    dve.wait_ge(S["bias_loaded"], 64)
                    own.tell(ts(two(sm_z[:, 0:TOK]), banks(pair[0]), cols[:, C_BIAS:C_BIAS + 1],
                                cols[:, C_SGN:C_SGN + 1], ALU.add, ALU.mult), "evac_done")
                    own.step(ts(sm_z[:, TOK:CONV], pcol[:, R_LAM:R_LAM + 4], -1.0))
                    for k in range(2):
                        own.step(V.tensor_copy(cols[64 * k:64 * k + 64, C_SD:C_SD + 4],
                                               ssm_d8[64 * k:64 * k + 64, :].rearrange("p (r k) -> p k r", k=2)[:, k, :]))
                    own.mark(stt(sm_e, sm_z, -1.0, sm_z, ALU.mult, ALU.max), "sm_abs")
                    dve.wait_ge(S["sm_past_psum"], 1)
                    own.step(V.tensor_copy(sm_la[0:8, 0:P], pair[3][0:8, 0:P]))
                    dve.wait_ge(S["sm_exp"], 1)
                    own.step(ts(sm_t, sm_e, 2.0, None, ALU.add))
                    own.step(V.reciprocal(sm_t, sm_t))
                    own.step(tt(sm_s, sm_e, sm_t, ALU.mult))
                    own.step(tt(sm_s2, sm_s, sm_s, ALU.mult))
                    own.step(ts(sm_t, sm_s2, 1.0 / 17))
                    for c in (15, 13, 11, 9, 7, 5, 3):
                        own.step(stt(sm_t, sm_t, 1.0 / c, sm_s2, ALU.add, ALU.mult))
                    own.step(stt(sm_t, sm_t, 1.0, sm_s, ALU.add, ALU.mult))
                    own.step(ts(sm_z, sm_z, 0.0, None, ALU.max))
                    own.step(stt(sm_z, sm_t, 2.0, sm_z, ALU.mult, ALU.add))
                    own.step(ts(cols[:, C_LS8:C_LS8 + 4], sm_z[:, TOK:CONV], -8.0))
                    own.step(ts(cols[:, C_NLS8:C_NLS8 + 4], sm_z[:, TOK:CONV], 8.0))
                    own.step(ts(sm_rows[0:32, 0:TOK], sm_z[0:32, 0:TOK], -1.0))
                    own.step(V.tensor_copy(sm_rows[64:96, 0:TOK], sm_z[64:96, 0:TOK]))
                    dve.wait_ge(S["sm_a"], 1)
                    own.step(V.reciprocal(cols[:, C_T:C_T + 4], cols[:, C_LB:C_LB + 4]))
                    own.step(tt(cols[:, C_T:C_T + 4], cols[:, C_T:C_T + 4], cols[:, C_LB:C_LB + 4], ALU.mult))
                    own.step(tt(cols[:, C_LB:C_LB + 4], cols[:, C_T:C_T + 4], cols[:, C_T:C_T + 4], ALU.subtract))
                    own.step(ts(cols[:, C_1MLB:C_1MLB + 4], cols[:, C_LB:C_LB + 4], -1.0, 1.0, ALU.mult, ALU.add))
                    own.step(ts(sm_arg[64:96, 0:TOK], sm_z[64:96, 0:TOK], cols[64:96, C_A:C_A + 1], -1.0,
                                ALU.mult, ALU.mult))
                    for t_0, m in CHUNKS:
                        own.step(V.tensor_tensor_scan(small_cum[64:96, t_0:t_0 + m], ones[64:96, 0:m],
                                                      sm_arg[64:96, t_0:t_0 + m], 0.0, ALU.mult, ALU.add))
                    for (t_0, m), c in zip(CHUNKS, range(5)):
                        own.step(tt(sm_arg[64:96, t_0:t_0 + m],
                                    small_cum[64:96, t_0 + m - 1:t_0 + m].to_broadcast([32, m]),
                                    small_cum[64:96, t_0:t_0 + m], ALU.subtract))
                        last = tt(tot8[64:72, :, c], ident[64:72, 64:72],
                                  small_cum[64:72, t_0 + m - 1:t_0 + m].to_broadcast([8, 8]), ALU.mult)
                        if c < 4:
                            own.step(last)
                    own.mark(last, "sm_tot")
                    own.mark(V.memset(cols[:, C_T:C_T + 1], 0.0), "sm_arg_ready")
                    one = ones[0:8, 0:1]
                    own.step(V.tensor_tensor_scan(sm_cf[0:8, 0:NP_TOK], one.to_broadcast([8, NP_TOK]), sm_rows[0:8, 0:NP_TOK],
                                                  0.0, ALU.mult, ALU.add))
                    own.step(V.tensor_tensor_scan(sm_cf[0:8, 512:640], one.to_broadcast([8, P]), sm_la[0:8, 0:P],
                                                  0.0, ALU.mult, ALU.add))
                    own.mark(V.tensor_tensor_scan(sm_cf[0:8, 640:704], one.to_broadcast([8, NS_TOK]), sm_rows[0:8, NP_TOK:TOK],
                                                  sm_cf[0:8, 639:640], ALU.mult, ALU.add), "sm_fox")
                else:
                    dve.wait_ge(S["sm_fox2"], 1)
                    hi = cum_t[0:32, :].bitcast(F32)
                    tt(cum_t[32:64, :], sm_cf[0:32, :], hi, ALU.subtract)
                    own.step(tt(cum_s[96:P, :], sm_cf[0:32, :], hi, ALU.subtract))

            def ssd(g, s, u):
                if s == 0:
                    if u == 0:
                        dve.wait_ge(S["sm_fox2"], 1)
                        dve.wait_ge(S["sm_col"], 1)
                    else:
                        dve.wait_ge(S["sd_out"], 32 * g)
                    dve.wait_ge(S["evac_done"], 1 + 6 * g + 4)
                    for j, tile in enumerate((4 + g, 6 + g, 2 * g, 2 * g + 1)):
                        x = part[u % 2, j]
                        keep_rows(x, O_PSC, O_SSC, 8, tile)
                        own.tell(conv(sd_cw[j], x, R_SCW + tile, 8, pcol[:, R_SCB + tile:R_SCB + tile + 1]), "sd_conv")
                elif s in (1, 2):
                    t = s - 1
                    dve.wait_ge(S["sd_tr"], 3 * g + 2 + t)
                    src = pair[3 - t]
                    c0 = 64 + 4 * g + 2 * t
                    V.tensor_tensor(sd_v[:, 0:4, t * P:(t + 1) * P].rearrange("p c (h d) -> p c h d", h=2),
                                    src[:, 0:512].rearrange("p (c h d) -> p c h d", c=4, h=2),
                                    small_col[:, 0:4, c0:c0 + 2].unsqueeze(3).to_broadcast([P, 4, 2, 64]), ALU.mult)
                    own.mark(tt(sd_v[0:64, 4, t * P:(t + 1) * P].rearrange("p (h d) -> p h d", h=2),
                                src[0:64, 512:640].rearrange("p (h d) -> p h d", h=2),
                                small_col[0:64, 4, c0:c0 + 2].unsqueeze(2).to_broadcast([64, 2, 64]), ALU.mult), "sd_vx")
                    if s == 2:
                        c1 = 96 + 4 * g
                        tt(sd_vd[:, 0:4, :].rearrange("p c (h d) -> p c h d", h=4),
                           sd_v[:, 0:4, :].rearrange("p c (h d) -> p c h d", h=4),
                           small_col[:, 0:4, c1:c1 + 4].unsqueeze(3).to_broadcast([P, 4, 4, 64]), ALU.mult)
                        tt(sd_vd[0:64, 4, :].rearrange("p (h d) -> p h d", h=4),
                           sd_v[0:64, 4, :].rearrange("p (h d) -> p h d", h=4),
                           small_col[0:64, 4, c1:c1 + 4].unsqueeze(2).to_broadcast([64, 4, 64]), ALU.mult)
                        dve.wait_ge(S["sd_cb_psum"], g + 1)
                        dve.wait_ge(S["consts_made"], 1)
                        tt(sd_cb[:, 0:512].rearrange("p (c t) -> p c t", c=4),
                           pair[3][:, 0:512].rearrange("p (c t) -> p c t", c=4),
                           tri[:, :].unsqueeze(1).to_broadcast([P, 4, P]), ALU.mult)
                        own.mark(tt(sd_cb[0:64, 512:TOK], pair[3][0:64, 512:TOK], tri[0:64, 0:64], ALU.mult), "sd_cbm")
                elif s == 3:
                    dve.wait_ge(S["sd_kv"], g + 1)
                    dve.wait_ge(S["ssm_in_loaded"], 16 * (g + 1))
                    own.step(V.tensor_copy(sd_s[:, 0, :], pair[3][:, 0:2 * P]))
                    for c in range(1, 5):
                        before, after = (c - 1, c) if c < 4 else (4, 5)
                        kv = pair[3][:, c * 2 * P:(c + 1) * 2 * P] if c < 4 else pair[2][:, 0:2 * P]
                        own.step(tt(sd_tmp.rearrange("p (h v) -> p h v", h=4),
                                    sd_s[:, before, :].rearrange("p (h v) -> p h v", h=4),
                                    ssm_etot[:, 4 * g:4 * g + 4, c].unsqueeze(2).to_broadcast([P, 4, 64]), ALU.mult))
                        last = tt(sd_s[:, after, :], sd_tmp, kv, ALU.add)
                        if c < 4:
                            own.step(last)
                    own.mark(last, "sd_state")
                if 4 <= s <= 7:
                    i = 4 * g + s - 4
                    h = i
                    dve.wait_ge(S["sd_bc_copied"], i + 1)
                    for c, (t_0, m) in enumerate(CHUNKS):
                        last = ts(sd_att[0:m, t_0:t_0 + m], sd_bc[0:m, t_0:t_0 + m],
                                  small_col[0:m, c, 32 + h:33 + h], 0.0, ALU.subtract, ALU.min)
                        if c == 3:
                            V.memset(sd_att[64:P, 512:TOK], 0.0)
                    own.mark(last, "sd_argd")
                    dve.wait_ge(S["sd_expd"], i + 1)
                    tt(sd_att[:, 0:512], sd_att[:, 0:512], sd_cb[:, 0:512], ALU.mult)
                    tt(sd_att[0:64, 512:TOK], sd_att[0:64, 512:TOK], sd_cb[0:64, 512:TOK], ALU.mult)
                    own.mark(tt(sd_cd, sd_cd, part[u % 2, 1][:, 0:TOK], ALU.mult), "sd_attd")
                if s in (6, 8):
                    t = (s - 6) // 2
                    dve.wait_ge(S["sd_o"], 4 * g + 2 * t + 2)
                    own.step(stt(sd_y[t], part[u % 2, 2 + t][:, 0:TOK], cols[:, C_SD + 2 * g + t:C_SD + 2 * g + t + 1],
                                 pair[3][:, 0:TOK], ALU.mult, ALU.add))
                    own.mark(tt(sd_y[t], sd_y[t], part[u % 2, 4 + t][:, 0:TOK], ALU.mult), "sd_yv")
                elif s == 10:
                    dve.wait_ge(S["sd_rstd"], g + 1)
                    for t in range(2):
                        j = 2 * g + t
                        if j >= 2:
                            dve.wait_ge(S["y_stored"], 16 * (j - 1))
                        own.mark(stt(y_out[j % 2][:, :], sd_y[t], pcol[:, R_SNORM + j:R_SNORM + j + 1], sd_bc,
                                     ALU.mult, ALU.mult), "y_done")

            def z_make(n, lv, u):
                h = 1 << lv
                w = TOK if lv < 6 else NP_TOK
                view = lambda x: x[:, 0:w].rearrange("p (b s j) -> p b s j", s=2, j=h)
                cum, z = view(hg_cum), view(hg_z[lv % 2])
                ref = cum[:, :, 0, h - 1:h].to_broadcast([P, w // (2 * h), h])
                tt(z[:, :, 0, :], ref, cum[:, :, 0, :], ALU.subtract)
                own.tell(tt(z[:, :, 1, :], cum[:, :, 1, :], ref, ALU.subtract), "hg_zarg")

            def z_scale(n, lv, u):
                h = 1 << lv
                w = TOK if lv < 6 else NP_TOK
                view = lambda x: x[:, 0:w].rearrange("p (b s j) -> p b s j", s=2, j=h)
                z = view(hg_z[lv % 2])
                dve.wait_ge(S["hg_zexp"], LEVELS * n + lv + 1)
                tt(z[:, :, 0, :], z[:, :, 0, :], view(hg_k)[:, :, 0, :], ALU.mult)
                own.tell(tt(z[:, :, 1, :], z[:, :, 1, :], view(part[u % 2, 0])[:, :, 1, :], ALU.mult), "hg_zd")

            def z_take(n, lv):
                h = 1 << lv
                dve.wait_ge(S["hg_lvl"], LEVELS * n + lv + 1)
                bank = pair[3][:, 512 * (lv % 2):512 * (lv % 2) + 512]
                for rows, t_0, t_1, c0, c1 in ((P, 0, 512, 0, 256), (64, 512, TOK, 256, 288)):
                    if rows == 64 and lv == 6:
                        continue
                    dst = hg_att[0:rows, t_0:t_1].rearrange("p (b s j) -> p b s j", s=2, j=h)[:, :, 1, :]
                    mask = level_mask[0:rows, lv, 0:c1 - c0].rearrange("p (b j) -> p b j", j=h)
                    last = V.copy_predicated(dst, mask, bank[0:rows, c0:c1].rearrange("p (b j) -> p b j", j=h))
                own.mark(last, "hg_lvld")

            def hgrn(n, s, u):
                if s == 0:
                    dve.wait_ge(S["evac_done"], 1 + 12 + 4 * n + 4)
                    if n > 0:
                        dve.wait_ge(S["hg_out"], 32 * n)
                    else:
                        dve.wait_ge(S["sd_out"], 64)
                    sig, neg = part[u % 2, 1][:, 0:TOK], part[u % 2, 4][:, 0:TOK]
                    lb, om = cols[:, C_LB + n:C_LB + n + 1], cols[:, C_1MLB + n:C_1MLB + n + 1]
                    own.step(ts(hg_lf, sig, om, lb, ALU.mult, ALU.add))
                    own.step(ts(hg_lf2, hg_lf, F_FLOOR, TWO60, ALU.max, ALU.mult))
                    own.step(ts(hg_lf2, hg_lf2, 1.0, None, ALU.min))
                    own.step(ts(hg_k, neg, om))
                    own.mark(ts(hg_lf, hg_lf, 1.0 / TWO60, None, ALU.max), "hg_f")
                    dve.wait_ge(S["hg_ln"], n + 1)
                    own.step(tt(hg_lf, hg_lf, hg_lf2, ALU.add))
                    for t_0, m in CHUNKS:
                        last = V.tensor_tensor_scan(hg_cum[:, t_0:t_0 + m], ones[:, 0:m], hg_lf[:, t_0:t_0 + m],
                                                    0.0, ALU.mult, ALU.add)
                    own.mark(last, "hg_cumd")
                    tt(hg_kd[:, 0:512].rearrange("p (c t) -> p c t", c=4),
                       hg_cum[:, 0:512].rearrange("p (c t) -> p c t", c=4)[:, :, P - 1:P].to_broadcast([P, 4, P]),
                       hg_cum[:, 0:512].rearrange("p (c t) -> p c t", c=4), ALU.subtract)
                    own.mark(tt(hg_kd[:, 512:TOK], hg_cum[:, TOK - 1:TOK].to_broadcast([P, NS_TOK]),
                                hg_cum[:, 512:TOK], ALU.subtract), "hg_karg")
                    dve.wait_ge(S["hg_ec"], n + 1)
                    tt(hg_qc, hg_qc, part[u % 2, 0][:, 0:TOK], ALU.mult)
                    dve.wait_ge(S["hg_kexp"], n + 1)
                    own.mark(tt(hg_kd, hg_kd, hg_k, ALU.mult), "hg_kdd")
                    z_make(n, 0, u)
                    z_make(n, 1, u)
                elif s == 1:
                    z_scale(n, 0, u)
                    z_scale(n, 1, u)
                elif s == 2:
                    dve.wait_ge(S["hg_diag"], n + 1)
                    tt(hg_att[:, 0:512].rearrange("p (c t) -> p c t", c=4),
                       pair[2][:, 0:512].rearrange("p (c t) -> p c t", c=4),
                       ident[:, :].unsqueeze(1).to_broadcast([P, 4, P]), ALU.mult)
                    own.mark(tt(hg_att[0:64, 512:TOK], pair[2][0:64, 512:TOK], ident[0:64, 0:64], ALU.mult), "hg_att0")
                if s in (2, 3, 4):
                    lv = 2 * s - 4
                    z_take(n, lv)
                    z_take(n, lv + 1)
                    z_make(n, lv + 2, u)
                    if s < 4:
                        z_make(n, lv + 3, u)
                    z_scale(n, lv + 2, u)
                    if s < 4:
                        z_scale(n, lv + 3, u)
                if s == 4:
                    dve.wait_ge(S["hg_kv"], n + 1)
                    dve.wait_ge(S["hgrn_in_loaded"], 16 * (n + 1))
                    own.step(V.tensor_copy(hg_s[:, 0, :], pair[2][:, 0:P]))
                    for c in range(1, 5):
                        before, after = (c - 1, c) if c < 4 else (4, 5)
                        last = stt(hg_s[:, after, :], hg_s[:, before, :], hgrn_etot[:, c:c + 1],
                                   pair[2][:, c * P:(c + 1) * P], ALU.mult, ALU.add)
                        if c < 4:
                            own.step(last)
                    own.mark(last, "hg_state")
                elif s == 5:
                    z_take(n, 6)
                elif s == 7:
                    dve.wait_ge(S["hg_rstd"], n + 1)
                    own.step(tt(hg_lf, pair[3][:, 0:TOK], hg_lf2, ALU.mult))
                    j = 4 + n
                    dve.wait_ge(S["y_stored"], 16 * (j - 1))
                    own.mark(stt(y_out[j % 2][:, :], hg_lf, pcol[:, R_HNORM + n:R_HNORM + n + 1],
                                 part[u % 2, 3][:, 0:TOK], ALU.mult, ALU.mult), "y_done")

            def fox_dve(n, i):
                hh, tb = FOX_ITEMS[i]
                m_, keys = (P, (tb + 1) * P) if tb < 4 else (NS_TOK, PAST + NS_TOK)
                dve.wait_ge(S["fx_score"], 10 * n + i + 1)
                bank = pair[2][:, 512 * (i % 2):512 * (i % 2) + 512]
                own.tell(V.tensor_reduce(cols[0:m_, C_NM + i % 2:C_NM + i % 2 + 1], bank[0:m_, 0:keys], AX.X, ALU.max,
                                         negate=True), "fx_neg")

            def fox_norm(n, i):
                hh, tb = FOX_ITEMS[i]
                m_, keys = (P, (tb + 1) * P) if tb < 4 else (NS_TOK, PAST + NS_TOK)
                dve.wait_ge(S["fx_expd"], 10 * n + i + 1)
                own.step(V.reciprocal(cols[0:m_, C_RI + i % 2:C_RI + i % 2 + 1], cols[0:m_, C_RS + i % 2:C_RS + i % 2 + 1]))
                own.tell(ts(fx_ex[i % 2][0:m_, 0:keys], fx_ex[i % 2][0:m_, 0:keys],
                            cols[0:m_, C_RI + i % 2:C_RI + i % 2 + 1]), "fx_pd")

            def fox(n, s, u):
                if s == 1:
                    if n == 0:
                        dve.wait_ge(S["hg_out"], 128)
                    for w, (dst, gain, r) in enumerate(((fx_q, cols[:, C_QN:C_QN + 1], fx_sqq),
                                                        (fx_k, pcol[:, R_KN:R_KN + 1], fx_sqk))):
                        dve.wait_ge(S["fx_rstd"], 2 * n + w + 1)
                        own.tell(stt(dst, part[u % 2, w][:, 0:TOK], gain, r, ALU.mult, ALU.mult), "fx_qkd")
                elif s == 2:
                    for hh in range(2):
                        dve.wait_ge(S["sm_fox2"], 1)
                        h = 2 * n + hh
                        own.tell(ts(fx_ch[hh][0:104, :], cum_s[0:104, :].bitcast(F32), sel_fox[0:104, h:h + 1]), "fx_bias")
                if s in FOX_STEPS:
                    for k in FOX_STEPS[s]:
                        if k + 2 < 10:
                            fox_dve(n, k + 2)
                            fox_norm(n, k + 2)
                        if k == 1:
                            dve.wait_ge(S["fx_pv"], 10 * n + 2)
                            own.tell(V.tensor_copy(fx_os, pair[3][:, 0:NS_TOK]), "fx_osd")
                if s == 7:
                    dve.wait_ge(S["fx_pv"], 10 * n + 10)
                    j = 8 + n
                    dve.wait_ge(S["y_stored"], 16 * (j - 1))
                    dve.wait_ge(S["fx_osd"], n + 1)
                    tt(y_out[j % 2][:, 0:512], pair[3][:, 0:512], part[u % 2, 3][:, 0:512], ALU.mult)
                    own.mark(tt(y_out[j % 2][:, 512:TOK], fx_os, part[u % 2, 3][:, 512:TOK], ALU.mult), "y_done")

            def lru(n, s, u):
                lr_x, lr_r, lr_i, lr_th, lr_a, lr_m = lr_tiles[n % 2]
                if s == 0:
                    if n == 0:
                        dve.wait_ge(S["fx_kout"], 128)
                        dve.wait_ge(S["fx_vout"], 128)
                    dve.wait_ge(S["evac_done"], EVACUATED["lru", n, "dx"])
                    x = part[u % 2, 0]
                    keep_rows(x, O_PLC, O_SLC, 4, n)
                    own.mark(conv(lr_x, x, R_LCW + n, 4, pcol[:, R_LCB + n:R_LCB + n + 1]), "lr_conv")
                elif s == 1:
                    dve.wait_ge(S["lr_act"], n + 1)
                    own.step(tt(lr_m, lr_a, lr_a, ALU.mult))
                    own.mark(stt(lr_m, lr_m, 1.0, lr_th, ALU.add, ALU.mult), "lr_m2")
                elif s == 2:
                    own.step(tt(lr_i, lr_i, lr_x, ALU.mult))
                    dve.wait_ge(S["lr_sqrt"], n + 1)
                    own.step(V.memset(lr_m[:, 0:1], 1.0))
                    own.step(tt(lr_m, lr_m, lr_i, ALU.mult))
                    V.tensor_tensor_scan(lr_r[:, 0:NP_TOK], lr_a[:, 0:NP_TOK], lr_m[:, 0:NP_TOK], 0.0, ALU.mult, ALU.add)
                    own.step(V.tensor_tensor_scan(lr_r[:, SAMPLE_AT:SAMPLE_AT + NS_TOK],
                                                  lr_a[:, SAMPLE_AT:SAMPLE_AT + NS_TOK],
                                                  lr_m[:, SAMPLE_AT:SAMPLE_AT + NS_TOK],
                                                  pcol[:, R_H0 + n:R_H0 + n + 1], ALU.mult, ALU.add))
                    V.tensor_copy(out_col[:, O_PLH + n:O_PLH + n + 1], lr_r[:, NP_TOK - 1:NP_TOK])
                    last = V.tensor_copy(out_col[:, O_SLH + n:O_SLH + n + 1],
                                         lr_r[:, SAMPLE_AT + NS_TOK - 1:SAMPLE_AT + NS_TOK])
                    if n == 3:
                        own.mark(last, "oc_ready")
                else:
                    dve.wait_ge(S["evac_done"], EVACUATED["lru", n, "dg"])
                    if n == 0:
                        dve.wait_ge(S["y_stored"], 16 * 12)
                    g = part[u % 2, 1]
                    tt(y32[:, 12 + n, 0:NP_TOK], lr_r[:, 0:NP_TOK], g[:, 0:NP_TOK], ALU.mult)
                    own.mark(tt(y32[:, 12 + n, NP_TOK:TOK], lr_r[:, SAMPLE_AT:SAMPLE_AT + NS_TOK], g[:, NP_TOK:TOK],
                                ALU.mult), "y_done")

            mixers = {"small": small, "ssd": ssd, "hgrn": hgrn, "fox": fox, "lru": lru}
            for task in ORDER:
                if task[0] == "stage":
                    _, kind, n, s, u = task
                    mixers[kind](n, s, u)

            def split_y(ks):
                for k in ks:
                    dve.wait_ge(S["norm_hi"], KT + k + 1)
                    own.tell(tt(h_lo[:, k, :], y32[:, k, :], h_hi[:, k, :].bitcast(F32), ALU.subtract), "norm_lo")

            split_y(range(8))
            for kind, n, s, u in TAIL:
                mixers[kind](n, s, u)
            split_y(range(8, KT))
            dve.wait_ge(S["xT_loaded0"], 16)
            own.step(V.memset(ss2[:, :], 0.0))

            def add_residual(value, j):
                x = xT[:, bass.ds(value, 1), :].rearrange("p a (b n) -> p (a b) n", b=2)
                dve.wait_ge(S["half_used"], value * 2 + (2 * N1 + 2))
                tt(x, x, banks(pair[j % 4]), ALU.add).then_inc(S["x2_done"], 1)
                dve.wait_ge(S["x2_squared"], value + 1)
                if j > 0 or not isinstance(value, int):
                    dve.wait_ge(S["x2_summed"], value + 0)
                tt(ss2[:, :], ss2[:, :], sq2[j % 2][:, :], ALU.add).then_inc(S["x2_summed"], 1)

            for j in range(4):
                add_residual(j, j)
            dve.wait_ge(S["xT_loaded"], 48)
            with dve.Fori(1, N2 // 4 - 1) as i:
                for j in range(4):
                    add_residual(i * 4 + j, j)

            def split_x(ks):
                for k in ks:
                    dve.wait_ge(S["norm_hi"], 2 * KT + k + 1)
                    own.tell(stt(h_lo[:, k, :], xT[:, k, :], pcol[:, R_LN2 + k:R_LN2 + k + 1],
                                 h_hi[:, k, :].bitcast(F32), ALU.mult, ALU.subtract), "norm_lo")

            for j in range(N2 - 4, N2):
                if j == N2 - 1:
                    split_x(range(8))
                add_residual(j, j)
            split_x(range(8, KT))
            dve.wait_ge(S["rstd_ready"], 2)

            def swiglu(g, first, last=False):
                for t in range(4):
                    v = g * 4 + t
                    dve.wait_ge(S["half_used"], g * 24 + 2 * (N1 + N2 + 2 * t + 1))
                    if not first or t >= 2:
                        dve.wait_ge(S["glu_done"], v - 1)
                    tt(two(silu[t % 2][:, :]), banks(pair[(2 * t) % 4]), two(rstd2[:, :]), ALU.mult
                       ).then_inc(S["gate_done"], 1)
                    dve.wait_ge(S["silu_done"], v + 1)
                    tt(silu[t % 2][:, :], silu[t % 2][:, :], rstd2[:, :], ALU.mult).then_inc(S["silu_scaled"], 1)
                    dve.wait_ge(S["silu_scaled"], v + 1)
                    dve.wait_ge(S["half_used"], g * 24 + 2 * (N1 + N2 + 2 * t + 2))
                    if not first or t >= 2:
                        dve.wait_ge(S["act_lo_done"], v - 1)
                    tt(two(glu[t % 2][:, :]), two(silu[t % 2][:, :]), banks(pair[(2 * t + 1) % 4]), ALU.mult
                       ).then_inc(S["glu_done"], 1)
                    dve.wait_ge(S["act_hi_done"], v + 1)
                    tt(act_lo[:, t, :], glu[t % 2][:, :], act_hi[:, t, :].bitcast(F32), ALU.subtract
                       ).then_inc(S["act_lo_done"], 1)
                for n in range(KT):
                    if n % 2 == 0:
                        dve.wait_ge(S["down_out"], g * 8 + (n // 2 + 1))
                    else:
                        dve.wait_ge(S["half_used"], g * 24 + (2 * (N1 + N2 + 8) + n // 2 + 1))
                    if not first:
                        dve.wait_ge(S["x_added"], g * 16 + (n - 15))
                    tt(two(xT[:, n, :]), two(xT[:, n, :]), banks(pair[n % (3 if last else 4)]), ALU.add
                       ).then_inc(S["x_added"], 1)
                    if last:
                        for i, q, c, after in OUT_STEPS:
                            if after == n and i % 2 == 0:
                                m = CHUNKS[c][1]
                                dve.wait_ge(S["out_psum"], i + 1)
                                if i >= 4:
                                    dve.wait_ge(S[f"out_stored{i % 4}"], 16 * (i // 4))
                                own.tell(V.tensor_copy(y_tok[i % 4][0:m, :], pair[3][0:m, 0:512]), "out_copied0")

            swiglu(0, True)
            with dve.Fori(1, GROUPS - 1) as g:
                swiglu(g, False)
            swiglu(GROUPS - 1, False, True)


_PROMPT = [(1, 1, 3, 1024), (1, 1, 8, 128, 64), (1, 1, 4, 128, 128), (1, 1, 512, 8, 64), (1, 1, 512, 8, 64),
           (1, 1, 512, 8), (1, 1, 3, 512), (1, 1, 512)]
_SAMPLE = [(1, 1, 3, 1024), (1, 1, 8, 128, 64), (1, 1, 4, 128, 128), (1, 1, 64, 8, 64), (1, 1, 64, 8, 64),
           (1, 1, 64, 8), (1, 1, 3, 512), (1, 1, 512)]
OUTPUTS = [(1, 512, 2048), (1, 64, 2048)] + _PROMPT + _SAMPLE


def kernel(**inputs):
    import concourse.bacc as bacc
    import numpy as np
    from concourse.bass_utils import run_bass_kernel_spmd

    nc = bacc.Bacc("TRN2", target_bir_lowering=False, num_devices=1)
    arrays, a = {}, {}
    for name, value in inputs.items():
        value = np.ascontiguousarray(value)
        arrays[f"in_{name}_dram"] = value
        a[name] = nc.dram_tensor(f"in_{name}_dram", value.shape, mybir.dt.from_np(value.dtype), kind="ExternalInput").ap()
    o = [nc.dram_tensor(f"out_{i}_dram", shape, F32, kind="ExternalOutput").ap() for i, shape in enumerate(OUTPUTS)]
    hybrid_layer(nc, a, o)
    r = run_bass_kernel_spmd(nc, [arrays], core_ids=[0])
    return tuple(r.results[0][f"out_{i}_dram"] for i in range(len(OUTPUTS)))
```
